# Optimizing a Trainium2 kernel written in Bass

```python
import math
import jax
import jax.numpy as jnp
from jax import lax
import numpy as np

D_MODEL = 1024
BATCH = 1
SEQ = 512
DEPTH = 1
DEC_BATCH = 8
DEC_SEQ = 4
PAST_LEN = 4096
PAGE_SIZE = 128

N_META = 16
MIX_WIDTH = D_MODEL
GDN_WIDTH = MIX_WIDTH // 2
CONF_WIDTH = MIX_WIDTH - GDN_WIDTH
GDN_HEAD_DIM = 128
GDN_HEADS = GDN_WIDTH // GDN_HEAD_DIM
GDN_CONV = 4
GDN_CHUNK = 64
QKV_WIDTH = 3 * GDN_WIDTH
CONF_CONV = 31
IN_WIDTH = QKV_WIDTH + GDN_WIDTH + 2 * GDN_HEADS + 2 * CONF_WIDTH
N_KEYS = 128
N_EXPERTS = N_KEYS * N_KEYS
PEER_HEADS = 8
PEER_KEY_DIM = 128
PEER_TOPK = 16
PEER_BLOCK = 128
DT_MIN = 0.001
DT_MAX = 0.1
EPS = 1e-6

kernel_name = 'gdn_conformer_peer_hybrid_step'

def rmsnorm(x, w):
    xf = x.astype(jnp.float32)
    y = xf * lax.rsqrt(jnp.mean(xf * xf, axis=-1, keepdims=True) + EPS)
    return (y * w.astype(jnp.float32)).astype(x.dtype)

def layernorm(x, w, b):
    xf = x.astype(jnp.float32)
    mu = jnp.mean(xf, axis=-1, keepdims=True)
    xc = xf - mu
    var = jnp.mean(xc * xc, axis=-1, keepdims=True)
    return xc * lax.rsqrt(var + EPS) * w.astype(jnp.float32) + b.astype(jnp.float32)

def l2norm(x):
    return x * lax.rsqrt(jnp.sum(x * x, axis=-1, keepdims=True) + EPS)

def causal_dwconv(x_ext, w):
    channels = x_ext.shape[-1]
    return lax.conv_general_dilated(
        x_ext, w[:, None, :], window_strides=(1,), padding='VALID',
        dimension_numbers=('NWC', 'WIO', 'NWC'), feature_group_count=channels)

def gdn_chunk(S, q, k, v, g, beta):
    C = q.shape[2]
    dv = v.shape[-1]
    G = jnp.cumsum(g, axis=-1)
    incl = jnp.tril(jnp.ones((C, C), dtype=bool))
    strict = jnp.tril(jnp.ones((C, C), dtype=bool), -1)
    decay = jnp.exp(jnp.where(incl, G[..., :, None] - G[..., None, :], -jnp.inf))
    kb = k * beta[..., None]
    L = jnp.where(strict, jnp.einsum('bhik,bhjk->bhij', kb, k) * decay, 0.0)
    rhs = jnp.concatenate([v * beta[..., None], kb * jnp.exp(G)[..., None]], axis=-1)
    sol = lax.linalg.triangular_solve(L, rhs, left_side=True, lower=True, unit_diagonal=True)
    u_v, w_k = sol[..., :dv], sol[..., dv:]
    v_new = u_v - jnp.einsum('bhck,bhkv->bhcv', w_k, S)
    attn = jnp.einsum('bhik,bhjk->bhij', q, k) * decay
    o = (jnp.einsum('bhck,bhkv->bhcv', q * jnp.exp(G)[..., None], S)
         + jnp.einsum('bhij,bhjv->bhiv', attn, v_new))
    G_last = G[..., -1:]
    S_new = (S * jnp.exp(G_last)[..., None]
             + jnp.einsum('bhck,bhcv->bhkv', k * jnp.exp(G_last - G)[..., None], v_new))
    return S_new, o

def gdn_prompt(S0, q, k, v, g, beta):
    B, H, T, dk = q.shape
    dv = v.shape[-1]
    S1, o_meta = gdn_chunk(S0, q[:, :, :N_META], k[:, :, :N_META], v[:, :, :N_META],
                           g[:, :, :N_META], beta[:, :, :N_META])
    n_chunks = (T - N_META) // GDN_CHUNK

    def to_chunks(a):
        a = a[:, :, N_META:]
        a = a.reshape((B, H, n_chunks, GDN_CHUNK) + a.shape[3:])
        return jnp.moveaxis(a, 2, 0)

    def body(S, inp):
        return gdn_chunk(S, *inp)

    S_fin, o_real = lax.scan(body, S1, (to_chunks(q), to_chunks(k), to_chunks(v),
                                          to_chunks(g), to_chunks(beta)))
    o_real = jnp.moveaxis(o_real, 0, 2).reshape(B, H, n_chunks * GDN_CHUNK, dv)
    return S_fin, jnp.concatenate([o_meta, o_real], axis=2)

def gdn_recurrent(S0, q, k, v, g, beta):
    def step(S, inp):
        q_t, k_t, v_t, g_t, b_t = inp
        S = S * jnp.exp(g_t)[..., None, None]
        u = b_t[..., None] * (v_t - jnp.einsum('bhkv,bhk->bhv', S, k_t))
        S = S + jnp.einsum('bhk,bhv->bhkv', k_t, u)
        return S, jnp.einsum('bhkv,bhk->bhv', S, q_t)

    xs = (jnp.moveaxis(q, 2, 0), jnp.moveaxis(k, 2, 0), jnp.moveaxis(v, 2, 0),
          jnp.moveaxis(g, 2, 0), jnp.moveaxis(beta, 2, 0))
    S_fin, o = lax.scan(step, S0, xs)
    return S_fin, jnp.moveaxis(o, 0, 2)

def token_mixer(xn, S0, qkv_buf, conf_buf, w_in, conv_qkv_w, a_log, dt_bias, gdn_norm_w,
                conf_dw_w, conf_dw_b, conf_ln_w, conf_ln_b, w_out, prompt):
    B, T, _ = xn.shape
    proj = xn @ w_in
    s0 = QKV_WIDTH
    s1 = s0 + GDN_WIDTH
    s2 = s1 + GDN_HEADS
    s3 = s2 + GDN_HEADS
    qkv, z, a, b, glu_in = proj[..., :s0], proj[..., s0:s1], proj[..., s1:s2], proj[..., s2:s3], proj[..., s3:]

    qkv_ext = jnp.concatenate([qkv_buf.astype(qkv.dtype), qkv], axis=1)
    qkv_c = jax.nn.silu(causal_dwconv(qkv_ext, conv_qkv_w.astype(qkv.dtype)))
    new_qkv_buf = qkv_ext[:, -(GDN_CONV - 1):]

    def heads(t):
        return t.reshape(B, T, GDN_HEADS, GDN_HEAD_DIM).transpose(0, 2, 1, 3).astype(jnp.float32)

    q = l2norm(heads(qkv_c[..., :GDN_WIDTH])) * (GDN_HEAD_DIM ** -0.5)
    k = l2norm(heads(qkv_c[..., GDN_WIDTH:2 * GDN_WIDTH]))
    v = heads(qkv_c[..., 2 * GDN_WIDTH:])
    g = (-jnp.exp(a_log.astype(jnp.float32))
         * jax.nn.softplus(a.astype(jnp.float32) + dt_bias.astype(jnp.float32))).transpose(0, 2, 1)
    beta = jax.nn.sigmoid(b.astype(jnp.float32)).transpose(0, 2, 1)
    S0f = S0.astype(jnp.float32)
    if prompt:
        S_new, o = gdn_prompt(S0f, q, k, v, g, beta)
    else:
        S_new, o = gdn_recurrent(S0f, q, k, v, g, beta)
    o = rmsnorm(o.transpose(0, 2, 1, 3), gdn_norm_w) * jax.nn.silu(
        z.reshape(B, T, GDN_HEADS, GDN_HEAD_DIM).astype(jnp.float32))
    o = o.reshape(B, T, GDN_WIDTH).astype(xn.dtype)

    glu = glu_in[..., :CONF_WIDTH] * jax.nn.sigmoid(glu_in[..., CONF_WIDTH:])
    c_ext = jnp.concatenate([conf_buf.astype(glu.dtype), glu], axis=1)
    c = causal_dwconv(c_ext, conf_dw_w.astype(glu.dtype)) + conf_dw_b
    new_conf_buf = c_ext[:, -(CONF_CONV - 1):]
    c = jax.nn.silu(layernorm(c, conf_ln_w, conf_ln_b)).astype(xn.dtype)

    out = jnp.concatenate([o, c], axis=-1) @ w_out
    return out, S_new.astype(xn.dtype), new_qkv_buf, new_conf_buf

def peer_ffn(x, w_query, sub_keys, expert_u, expert_v):
    B, T, D = x.shape
    xt = x.reshape(B * T, D)
    n = xt.shape[0]
    q = (xt @ w_query).reshape(n, PEER_HEADS, 2, PEER_KEY_DIM).astype(jnp.float32)
    s = jnp.einsum('nhpd,hpkd->nhpk', q, sub_keys.astype(jnp.float32))
    s1, i1 = lax.top_k(s[:, :, 0], PEER_TOPK)
    s2, i2 = lax.top_k(s[:, :, 1], PEER_TOPK)
    cand = (s1[..., :, None] + s2[..., None, :]).reshape(n, PEER_HEADS, PEER_TOPK * PEER_TOPK)
    cidx = (i1[..., :, None] * N_KEYS + i2[..., None, :]).reshape(n, PEER_HEADS, PEER_TOPK * PEER_TOPK)
    top, pos = lax.top_k(cand, PEER_TOPK)
    eidx = jnp.take_along_axis(cidx, pos, axis=-1)
    gates = jax.nn.softmax(top, axis=-1).astype(x.dtype)

    pad = (-n) % PEER_BLOCK
    nb = (n + pad) // PEER_BLOCK
    xp = jnp.pad(xt, ((0, pad), (0, 0))).reshape(nb, PEER_BLOCK, D)
    ep = jnp.pad(eidx, ((0, pad), (0, 0), (0, 0))).reshape(nb, PEER_BLOCK, PEER_HEADS, PEER_TOPK)
    gp = jnp.pad(gates, ((0, pad), (0, 0), (0, 0))).reshape(nb, PEER_BLOCK, PEER_HEADS, PEER_TOPK)

    def block(args):
        xb, eb, gb = args
        u = expert_u[eb]
        act = jax.nn.gelu(jnp.einsum('nd,nhed->nhe', xb, u), approximate=False)
        return jnp.einsum('nhe,nhed->nd', gb * act, expert_v[eb])

    y = lax.map(block, (xp, ep, gp))
    return y.reshape(nb * PEER_BLOCK, D)[:n].reshape(B, T, D)

def setup_inputs(seed: int = 0) -> dict:
    key = jax.random.key(seed)
    ks = jax.random.split(key, 24)
    f32 = jnp.float32

    def nrm(k, shape, scale):
        return scale * jax.random.normal(k, shape, f32)

    dt = jnp.exp(jax.random.uniform(ks[7], (DEPTH, GDN_HEADS), f32, math.log(DT_MIN), math.log(DT_MAX)))
    return {
        'x_prompt': nrm(ks[0], (BATCH, SEQ, D_MODEL), 1.0),
        'x_sample': nrm(ks[1], (DEC_BATCH, DEC_SEQ, D_MODEL), 1.0),
        'state_gdn': nrm(ks[2], (DEPTH, DEC_BATCH, GDN_HEADS, GDN_HEAD_DIM, GDN_HEAD_DIM), 0.05),
        'state_qkv_conv': nrm(ks[3], (DEPTH, DEC_BATCH, GDN_CONV - 1, QKV_WIDTH), 1.0),
        'state_conf_conv': nrm(ks[4], (DEPTH, DEC_BATCH, CONF_CONV - 1, CONF_WIDTH), 1.0),
        'meta_tokens': nrm(ks[5], (N_META, D_MODEL), 1.0),
        'norm_mix_w': 1.0 + nrm(ks[6], (DEPTH, D_MODEL), 0.02),
        'w_in': nrm(ks[8], (DEPTH, D_MODEL, IN_WIDTH), D_MODEL ** -0.5),
        'conv_qkv_w': nrm(ks[9], (DEPTH, GDN_CONV, QKV_WIDTH), GDN_CONV ** -0.5),
        'a_log': jnp.log(jax.random.uniform(ks[10], (DEPTH, GDN_HEADS), f32, 1.0, 16.0)),
        'dt_bias': dt + jnp.log(-jnp.expm1(-dt)),
        'gdn_norm_w': 1.0 + nrm(ks[11], (DEPTH, GDN_HEAD_DIM), 0.02),
        'conf_dw_w': nrm(ks[12], (DEPTH, CONF_CONV, CONF_WIDTH), CONF_CONV ** -0.5),
        'conf_dw_b': nrm(ks[13], (DEPTH, CONF_WIDTH), 0.02),
        'conf_ln_w': 1.0 + nrm(ks[14], (DEPTH, CONF_WIDTH), 0.02),
        'conf_ln_b': nrm(ks[15], (DEPTH, CONF_WIDTH), 0.02),
        'w_out': nrm(ks[16], (DEPTH, MIX_WIDTH, D_MODEL), MIX_WIDTH ** -0.5),
        'norm_ffn_w': 1.0 + nrm(ks[17], (DEPTH, D_MODEL), 0.02),
        'w_query': nrm(ks[18], (DEPTH, D_MODEL, PEER_HEADS * 2 * PEER_KEY_DIM), D_MODEL ** -0.5),
        'sub_keys': nrm(ks[19], (DEPTH, PEER_HEADS, 2, N_KEYS, PEER_KEY_DIM), PEER_KEY_DIM ** -0.5),
        'expert_u': nrm(ks[20], (DEPTH, N_EXPERTS, D_MODEL), D_MODEL ** -0.5),
        'expert_v': nrm(ks[21], (DEPTH, N_EXPERTS, D_MODEL), PEER_HEADS ** -0.5),
        'final_norm_w': 1.0 + nrm(ks[22], (D_MODEL,), 0.02),
    }

def reference(x_prompt, x_sample, state_gdn, state_qkv_conv, state_conf_conv, meta_tokens,
              norm_mix_w, w_in, conv_qkv_w, a_log, dt_bias, gdn_norm_w, conf_dw_w, conf_dw_b,
              conf_ln_w, conf_ln_b, w_out, norm_ffn_w, w_query, sub_keys, expert_u, expert_v,
              final_norm_w):
    def run_trunk(h, S_in, qkv_in, conf_in, prompt):
        S_out, qkv_out, conf_out = [], [], []
        for layer in range(DEPTH):
            mix, S_l, qb_l, cb_l = token_mixer(
                rmsnorm(h, norm_mix_w[layer]), S_in[layer], qkv_in[layer], conf_in[layer],
                w_in[layer], conv_qkv_w[layer], a_log[layer], dt_bias[layer], gdn_norm_w[layer],
                conf_dw_w[layer], conf_dw_b[layer], conf_ln_w[layer], conf_ln_b[layer],
                w_out[layer], prompt)
            h = h + mix
            h = h + peer_ffn(rmsnorm(h, norm_ffn_w[layer]), w_query[layer], sub_keys[layer],
                             expert_u[layer], expert_v[layer])
            S_out.append(S_l)
            qkv_out.append(qb_l)
            conf_out.append(cb_l)
        return (rmsnorm(h, final_norm_w), jnp.stack(S_out), jnp.stack(qkv_out), jnp.stack(conf_out))

    dt_p = x_prompt.dtype
    meta = jnp.broadcast_to(meta_tokens.astype(dt_p)[None], (BATCH, N_META, D_MODEL))
    h_p = jnp.concatenate([meta, x_prompt], axis=1)
    zS = jnp.zeros((DEPTH, BATCH, GDN_HEADS, GDN_HEAD_DIM, GDN_HEAD_DIM), jnp.float32)
    zq = jnp.zeros((DEPTH, BATCH, GDN_CONV - 1, QKV_WIDTH), dt_p)
    zc = jnp.zeros((DEPTH, BATCH, CONF_CONV - 1, CONF_WIDTH), dt_p)
    out_p, new_gdn_prompt, new_qkv_conv_prompt, new_conf_conv_prompt = run_trunk(h_p, zS, zq, zc, True)
    y_prompt = out_p[:, N_META:]

    y_sample, new_gdn_sample, new_qkv_conv_sample, new_conf_conv_sample = run_trunk(
        x_sample, state_gdn, state_qkv_conv, state_conf_conv, False)

    return (y_prompt, y_sample, new_gdn_prompt, new_qkv_conv_prompt, new_conf_conv_prompt,
            new_gdn_sample, new_qkv_conv_sample, new_conf_conv_sample)


_drawn_inputs = setup_inputs


def setup_inputs(seed=0):
    import zlib

    import numpy as np

    out = dict(_drawn_inputs(seed))
    spreads = {}
    factors = {'gdn_norm_w': 36.311,
     'conf_ln_w': 29.482,
     'conf_ln_b': 30.477,
     'final_norm_w': 22.467,
     'norm_ffn_w': 16.386}
    for name, (base, spread) in spreads.items():
        noise = np.random.default_rng([zlib.crc32(name.encode()), seed]).standard_normal(out[name].shape)
        drawn = base * np.exp(spread * noise) if base else spread * noise
        out[name] = jnp.asarray(drawn.astype(out[name].dtype))
    for name, factor in factors.items():
        out[name] = (out[name] * factor).astype(out[name].dtype)
    return out
```

```python
from contextlib import ExitStack

import numpy as np

import concourse.bass as bass
from concourse import mybir

F32 = mybir.dt.float32
F32R = mybir.dt.float32r
U32 = mybir.dt.uint32
ALU = mybir.AluOpType
ACT = mybir.ActivationFunctionType
AX = mybir.AxisListType

P = 128
D = 1024
KT = D // P
META, SEQ, NSEQ, STEPS = 16, 512, 8, 4
TP = META + SEQ
TS = NSEQ * STEPS
NT = TP + TS
TB = 112
NTB = NT // TB
HALF = NT // 2
HEADS, DH = 4, 128
QC, CC = 4, 31
QKV, GW, CW = 1536, 512, 512
NQ, NG = QKV // P, CW // P
INW = QKV + GW + 2 * HEADS + 2 * CW
QEXT = (QC - 1) + TP
QSEG = (QC - 1) + STEPS
CEXT = (CC - 1) + TP
CSEG = (CC - 1) + STEPS
PH, KD, NK, TOPK = 8, 128, 128, 16
NE = NK * NK
PAIRS = PH * TOPK
EPS = 1e-6
BIG = 1e30
LOWEST = -3.0e38
CHUNKS = [(0, 128), (128, 128), (256, 128), (384, 128), (512, 16), (TP, TS)]
SAMPLE = len(CHUNKS) - 1
WB = 256
GE = 2
NGRP = NK // GE
GB = 56
NGB = NT // GB
assert NT == NTB * TB and NT == NGB * GB and NGRP % 2 == 0


class Steps:

    def __init__(self, sem, counts):
        self.sem, self.counts, self.n = sem, counts, 0

    def op(self, ins, *name):
        ins.then_inc(self.sem, 1)
        self.n += 1
        if name:
            self.counts[name] = self.n
        return ins

    def now(self, eng):
        if self.n:
            eng.wait_ge(self.sem, self.n)

    def wait(self, eng, *name):
        eng.wait_ge(self.sem, self.counts.get(name, 1))


def linear_blocks():
    z0, ab0 = QKV, QKV + GW
    v0 = ab0 + 2 * HEADS
    blocks = [("ab", 0, [("in", ab0, P)])]
    blocks += [("qkv", i, [("in", WB * i, WB)]) for i in range(QKV // WB)]
    glu = [("glu", c, [("in", v0 + P * c, P), ("in", v0 + CW + P * c, P)]) for c in range(NG)]
    z = [("z", i, [("in", z0 + WB * i, WB)]) for i in range(GW // WB)]
    blocks += [glu[0], z[0], glu[1], z[1], glu[2], glu[3]]
    blocks += [("out", i, [("out", WB * i, WB)]) for i in range(D // WB)]
    blocks += [("query", i, [("query", WB * i, WB)]) for i in range(2 * PH * KD // WB)]
    return blocks


BLOCKS = linear_blocks()
UNIT0 = [0]
for _kind, _, _parts in BLOCKS:
    UNIT0.append(UNIT0[-1] + (NTB if _kind == "out" else 2 * sum(n for _, _, n in _parts) // P))


def build(nc, ins, outs, counts):
    (x_prompt, x_sample, state_gdn, state_qkv, state_conf, meta, norm_mix_w, w_in, conv_qkv_w, a_log,
     dt_bias, gdn_norm_w, conf_dw_w, conf_dw_b, conf_ln_w, conf_ln_b, w_out, norm_ffn_w, w_query,
     sub_keys, expert_u, expert_v, final_norm_w) = ins
    (y_prompt, y_sample, gdn_prompt, qkv_prompt, conf_prompt, gdn_sample, qkv_sample, conf_sample) = outs
    WEIGHTS = {"in": w_in[0].rearrange("(k p) n -> p k n", p=P),
               "out": w_out[0].rearrange("(k p) n -> p k n", p=P),
               "query": w_query[0].rearrange("(k p) n -> p k n", p=P)}

    h2_dram = nc.dram_tensor("h2_dram", (NT, D), F32, kind="Internal").ap()
    gate_dram = nc.dram_tensor("gate_dram", (NGB, NK, NK, GB), F32, kind="Internal").ap()

    ctx = ExitStack()
    with ctx:
        def at(name, shape, dt, word):
            return nc.alloc_sbuf_tensor_at(name, shape, dt, offset=base + 4 * word)

        base = -(-nc.sbuf_base // 64) * 64
        room = (nc.sbuf_top - base) // 4
        used = {"all": 0}

        def place(name, shape, dt=F32, region="all"):
            words = int(np.prod(shape[1:]))
            words = -(-words // 8) * 8
            t = at(name, shape, dt, used[region])
            used[region] += words
            assert used[region] <= room
            return t

        ident = place("ident", [P, P])
        tri = place("tri", [P, P])
        neg = place("neg", [P, P])
        pos = place("pos", [P, P])
        diag16 = place("diag16", [P, P])
        tri_s = place("tri_s", [TS, TS])
        neg_s = place("neg_s", [TS, TS])
        pos_s = place("pos_s", [TS, TS])
        same_s = place("same_s", [TS, TS])
        seq_of = place("seq_of", [TS, NSEQ])
        ones = place("ones", [P, P])
        iota = place("iota", [P, P])
        cols = place("cols", [P, 61])
        dwcols = place("dwcols", [P, CC * NG])
        wrow = place("wrow", [TB, D])
        xT = place("xT", [P, 2, KT, NT], F32R)
        WR = place("WR", [P, 2, 2, KT, WB], F32R)
        RAW = place("RAW", [P, 4, KT, WB])
        late = used["all"]
        used["x"] = used["m"] = used["t"] = used["g"] = used["e"] = used["n"] = late

        h = place("h", [TB, NTB, D], region="n")
        xn = place("xn", [TB, 2, D], region="n")
        sq = place("sq", [TB, D], region="n")
        ss = place("ss", [TB, 3 * 8], region="n")
        qext = place("qext", [P, 2, QEXT + NSEQ * QSEG], region="m")
        gext = place("gext", [P, CEXT + NSEQ * CSEG], region="m")
        gate = place("gate", [P, NT], region="m")
        qkvT = place("qkvT", [P, NQ, NT], region="m")
        cT = place("cT", [P, NG, NT], region="m")
        zT = place("zT", [P, HEADS, NT], region="m")
        sqT = place("sqT", [P, NQ, NSEQ * (QC - 1)], region="m")
        qtail = place("qtail", [P, NQ, (QC - 1) + TS], region="m")
        ctail = place("ctail", [P, NG, (CC - 1) + TS], region="m")
        abT = place("abT", [2 * HEADS, NT], region="m")
        tok = place("tok", [P, 14, len(CHUNKS), HEADS], region="m")
        state = place("state", [P, HEADS, DH], region="m")
        dtb = place("dtb", [P, 2 * HEADS], region="m")
        spare = place("spare", [1, 8], region="m")
        gdn0 = used["m"]
        used["c"] = gdn0
        crow = place("crow", [61, P], region="c")
        dwrow = place("dwrow", [CC * NG, P], region="c")
        sconf = place("sconf", [120, 2, CW], region="c")
        sqkv = place("sqkv", [NSEQ * (QC - 1), QKV], region="c")
        scT = place("scT", [P, NG, NSEQ * (CC - 1)], region="c")
        used["d"] = gdn0
        KH = place("KH", [P, HEADS, DH], region="d")
        KHT = place("KHT", [P, HEADS, P], region="d")
        KE = place("KE", [P, HEADS, DH], region="d")
        RA = place("RA", [P, HEADS, 2, DH], region="d")
        RB = place("RB", [P, HEADS, 2, DH], region="d")
        m0 = used["d"]
        M = [place(f"M{i}", [P, HEADS, P], region="d") for i in range(8)]
        AT = place("AT", [P, HEADS, P], region="d")
        VN = place("VN", [P, HEADS, DH], region="d")
        OS = at("OS", [P, 2, HEADS, DH], F32, late)
        pairT = place("pairT", [P, 4, NT], region="t")
        used["g"] = used["t"]
        ghi = place("ghi", [P, NT], F32R, region="t")
        used["g"] = used["t"]
        qT = place("qT", [P, 2, NT], region="t")
        keysT = place("keysT", [P, 2 * PH, NK], region="t")
        scores = place("scores", [TB, NTB, 2 * PH, NK], region="t")
        best = place("best", [TB, 2 * PH, TOPK], region="t")
        besti = place("besti", [TB, 2 * PH, TOPK], U32, region="t")
        bestf = place("bestf", [TB, 2 * PH, TOPK], region="t")
        cand = place("cand", [TB, PH, TOPK, TOPK], region="t")
        eqa = place("eqa", [TB, PAIRS, TOPK], region="t")
        sel = place("sel", [TB, PAIRS, TOPK], region="t")
        top16 = place("top16", [TB, PAIRS], region="t")
        topi = place("topi", [TB, PAIRS], U32, region="t")
        topa = place("topa", [TB, 2, PAIRS], U32, region="t")
        topf = place("topf", [TB, 2, PAIRS], region="t")
        pick = place("pick", [TB, 3, PAIRS], region="t")
        gsum = place("gsum", [TB, 2 * PH], region="t")
        is1 = place("is1", [P, 8, NK], F32R, region="g")
        is2 = place("is2", [P, 8, 2, NK], F32R, region="g")
        gblk = place("gblk", [P, 2, NK, GB], region="g")
        keys = at("keys", [P, 2 * PH, KD], F32, used["t"] if used["t"] + 2048 <= room else late)
        SS = [at(f"SS{i}", [P, NSEQ, DH], F32, m0 + 512 * (0, 5)[i]) for i in range(2)]
        WQ = at("WQ", [P, HEADS, NSEQ, 2 * STEPS], F32, m0 + 512 * 3)
        CN = at("CN", [TB, NTB, CW], F32, m0)
        gls = at("gls", [P, NSEQ, HEADS], F32, late + 1024)
        gm = at("gm", [TS, NSEQ, HEADS], F32, late + 1056)
        lnst = at("lnst", [TB, NTB, 6 + 2 + 2], F32, late + 1088)
        sqb = [at(f"sqb{i}", [P, NT], F32, m0 - 1024 * (2 - i)) for i in range(2)]
        RA2 = at("RA2", [P, 3 * CW], F32, m0 - 1024)
        KTM = at("KTM", [TS, NSEQ * DH], F32, m0 - 2048)
        RA3 = at("RA3", [CC - 1 + TS, CW], F32, late + 1176 + 832)
        ONB = [at(f"ONB{i}", [P, HEADS, DH], F32, m0 - 2048 + 512 * i) for i in range(2)]
        mixf = [at(f"mixf{i}", [P, HEADS, P], F32, m0 - 1024 + 512 * i) for i in range(2)]
        keysrow = at("keysrow", [P, 2 * PH, KD], F32, used["n"])
        raws = used["all"] - 4 * KT * WB
        Uraw = at("Uraw", [P, 2, GE, D], F32, raws)
        Vraw = at("Vraw", [P, 2, GE, D], F32, raws + 2 * GE * D)
        wrs = raws - 4 * KT * WB
        UT = at("UT", [P, 2, 2, KT, P], F32R, wrs)
        VR = at("VR", [P, 2, GE, D], F32R, wrs + 4 * KT * P)
        AR = place("AR", [P, 2, 2, GE, NT], F32R, region="e")
        Gt = place("Gt", [P, 2, NGB, GE * GB], region="e")
        actv = place("actv", [P, 2, NT], region="e")
        prod = place("prod", [P, 2, NT], region="e")
        yT = place("yT", [P, KT, NT], region="e")
        hf = place("hf", [TB, NTB, D], region="e")
        yo = place("yo", [TB, 2, D], region="e")
        fs = place("fs", [TB, 24], region="e")

        bank = [ctx.enter_context(nc.psum_tensor(f"bank{i}", [P, 512], F32)) for i in range(8)]

        def sem(name):
            return ctx.enter_context(nc.semaphore(name))

        V = Steps(sem("vector_done"), counts.setdefault("V", {}))
        A = Steps(sem("scalar_done"), counts.setdefault("A", {}))
        T = Steps(sem("tensor_done"), counts.setdefault("T", {}))
        G = Steps(sem("gpsimd_done"), counts.setdefault("G", {}))
        h_in = [sem(f"h_in{i}") for i in range(2)]
        row_in = [sem(f"row_in{i}") for i in range(3)]
        small_in = sem("small_in")
        raw_in = [sem(f"raw_in{i}") for i in range(4)]
        gate_mm = sem("gate_mm")
        gate_bank = sem("gate_bank")
        is_ready = sem("is_ready")
        gblk_out = [sem(f"gblk_out{i}") for i in range(2)]
        u_in = [sem(f"u_in{i}") for i in range(2)]
        v_in = [sem(f"v_in{i}") for i in range(2)]
        g_in = [sem(f"g_in{i}") for i in range(2)]
        ut_mm, ut_high, ut_low = sem("ut_mm"), sem("ut_high"), sem("ut_low")
        s_mm, gelu_done, a_mul = sem("s_mm"), sem("gelu_done"), sem("a_mul")
        a_high, a_low = sem("a_high"), sem("a_low")
        v_high, v_low = sem("v_high"), sem("v_low")
        y_mm, y_add = sem("y_mm"), sem("y_add")
        hf_in = sem("hf_in")
        y_out = [sem(f"y_out{i}") for i in range(2)]
        out_done = sem("out_done")
        h2_done = sem("h2_done")
        ss_in = [sem(f"ss_in{i}") for i in range(2)]
        ss_out = [sem(f"ss_out{i}") for i in range(2)]

        nb = len(BLOCKS)
        first = {k: next(b for b in range(nb) if BLOCKS[b][0] == k) for k in ("ab", "out", "query")}
        raw_count = []
        for b in range(nb):
            raw_count.append(len(BLOCKS[b][2]) + (raw_count[b - 4] if b >= 4 else 0))

        def groups(ci):
            c = CHUNKS[ci][1]
            g = [("k", V), ("v", V), ("gb", V), ("khT", A), ("kk", V), ("kq", V), ("ldT", A),
                 ("p2", A), ("pt2", V), ("t1", V)]
            if ci != SAMPLE:
                g += [("p4", A), ("pt4", V), ("t2", V), ("p8", A), ("t3", V)]
            if c == P:
                g += [("n", A), ("nt", V), ("n2", A), ("nt2", V), ("nt4", A)]
            g += [("r0a", A), ("r0b", V)]
            if c == P:
                g += [("r1a", V), ("r1b", V), ("r2a", V), ("r2b", V), ("r3a", V), ("r3b", V)]
            g += [("wT", A)]
            if ci == SAMPLE:
                g += [("sw", V)]
            g += [("ws", V), ("qs", V), ("o1", V)]
            if ci == SAMPLE:
                g += [(f"su{h}{i}", V) for h in range(HEADS) for i in range(2)]
            else:
                g += [("su", V)]
            return g

        GROUPS = [(n, ci, e) for ci in range(len(CHUNKS)) for n, e in groups(ci)]
        WHERE = {(n, ci): i for i, (n, ci, _) in enumerate(GROUPS)}

        def gbank(n, ci):
            return bank[4 + WHERE[n, ci] % 4]

        def grant(eng, s_, n):
            eng.sem_inc(s_, n)

        class Grp:

            def __init__(self, k, turn=None):
                self.k, self.turn = k, turn

            def __add__(self, n):
                return Grp(self.k + n, self.turn)

            def __rmul__(self, m):
                return m * self.k if self.turn is None else self.turn * (2 * m) + m * self.k

        def par(g):
            return g.k % 2

        def half_of(g):
            return g.k // 2 if g.turn is None else g.turn + g.k // 2

        def unit_read(eng, u):
            b = max(b for b in range(nb) if UNIT0[b] <= u)
            (V if BLOCKS[b][0] == "out" else A).wait(eng, "unit", u)

        def rows(i, c, ci, width):
            return tok[0:c, i, ci, :].unsqueeze(2).to_broadcast([c, HEADS, width])

        def ostore(ci):
            if ci < 4:
                return qkvT[:, 2 * HEADS:3 * HEADS, CHUNKS[ci][0]:CHUNKS[ci][0] + P]
            return OS[0:CHUNKS[ci][1], ci - 4]

        GD, BETA, X2, X3, GC, EG, GL, EL, RQ, RK, BEG, EGL, OSS, EQ = range(14)

        block = ctx.enter_context(nc.Block())

        @block.sync
        def _(sp):
            def load_rows(dst, s):
                sp.dma_start(dst[0:META, 0, :], meta).then_inc(s, 16)
                sp.dma_start(dst[META:TB, 0, :], x_prompt[0, 0:TB - META, :]).then_inc(s, 16)
                sp.dma_start(dst[:, 1:NTB - 1, :],
                             x_prompt[0, TB - META:(NTB - 1) * TB - META, :].rearrange("(t p) d -> p t d", p=TB)
                             ).then_inc(s, 16)
                sp.dma_start(dst[0:TB - TS, NTB - 1, :],
                             x_prompt[0, (NTB - 1) * TB - META:SEQ, :]).then_inc(s, 16)
                sp.dma_start(dst[TB - TS:TB, NTB - 1, :],
                             x_sample.rearrange("b s d -> (b s) d")).then_inc(s, 16)

            def load_row(w, s):
                sp.dma_start(wrow[:], w.to_broadcast([TB, D])).then_inc(s, 16)

            load_rows(h, h_in[0])
            load_row(norm_mix_w, row_in[0])
            for b in range(nb):
                if b >= 4:
                    V.wait(sp, "low", b - 4)
                at_ = 0
                for name, c0, n in BLOCKS[b][2]:
                    sp.dma_start(RAW[:, b % 4, :, at_:at_ + n], WEIGHTS[name][:, :, c0:c0 + n]
                                 ).then_inc(raw_in[b % 4], 16)
                    at_ += n
                if b == first["out"] + 3:
                    V.wait(sp, "mixlow", "last")
                    T.wait(sp, "mixer", "last")
                    A.wait(sp, "mixer", "last")
                    V.wait(sp, "mixer", "last")
                    G.wait(sp, "mixer", "last")
                    load_rows(h, h_in[1])
                    sp.dma_start(keysrow[:], sub_keys[0].rearrange("h p k d -> k (h p) d")).then_inc(h_in[1], 16)
                    load_row(norm_ffn_w, row_in[1])
                if b == first["query"] + 5:
                    V.wait(sp, "h2", "last")
                    sp.dma_start(h2_dram.rearrange("(t p) d -> p t d", p=TB), h[:]).then_inc(h2_done, 16)
            V.wait(sp, "xn", 2, NTB - 1)
            load_row(final_norm_w.rearrange("(a d) -> a d", a=1), row_in[2])

            with sp.Fori(0, NGB // 2, 1) as i:
                for blk in range(2):
                    sp.wait_ge(gate_bank, i * (GB // 2) + ((blk + 1) * (GB // 4) + 4))
                    sp.dma_start(gate_dram[bass.ds(i * 2 + blk, 1)].rearrange("a p k n -> (a p) k n"),
                                 gblk[:, blk]).then_inc(gblk_out[blk], 16)
            for blk in range(2):
                sp.wait_ge(gblk_out[blk], 16 * (NGB // 2 + 1))

            U = expert_u[0].rearrange("(p k) d -> p k d", p=NK)
            Vw = expert_v[0].rearrange("(p k) d -> p k d", p=NK)

            def load(dst, src, g, s_):
                k0 = GE * g
                sp.dma_start(dst, src(bass.ds(k0, GE))).then_inc(s_, 16)

            def load_u(g):
                load(Uraw[:, par(g)], lambda k: U[:, k, :], g, u_in[par(g)])

            def load_v(g):
                load(Vraw[:, par(g)], lambda k: Vw[:, k, :], g, v_in[par(g)])

            def load_g(g):
                load(Gt[:, par(g)].rearrange("p b (k n) -> p b k n", n=GB),
                     lambda k: gate_dram[:, :, k, :].rearrange("b p k n -> p b k n"), g, g_in[par(g)])

            sp.wait_ge(h2_done, 16)
            for g in range(2):
                load_u(Grp(g))
                load_g(Grp(g))
                load_v(Grp(g))
            sp.dma_start(hf[:], h2_dram.rearrange("(t p) d -> p t d", p=TB)).then_inc(hf_in, 16)
            with sp.Fori(0, NGRP // 2 - 1, 1) as i:
                for k in range(2):
                    g = Grp(k + 2, i)
                    sp.wait_ge(ut_mm, 2 * GE * Grp(k + 1, i))
                    load_u(g)
                    sp.wait_ge(a_mul, GE * Grp(k + 1, i) + 2)
                    load_g(g)
                    sp.wait_ge(v_low, 1 * Grp(k + 1, i))
                    load_v(g)

            for t in range(NTB):
                V.wait(sp, "yo", t)
                r0 = t * TB - META
                if t == 0:
                    sp.dma_start(y_prompt[0, 0:TB - META, :], yo[META:TB, 0, :]).then_inc(y_out[t % 2], 16)
                elif t < NTB - 1:
                    sp.dma_start(y_prompt[0, r0:r0 + TB, :], yo[:, t % 2, :]).then_inc(y_out[t % 2], 16)
                else:
                    sp.dma_start(y_prompt[0, r0:SEQ, :], yo[0:TB - TS, t % 2, :]).then_inc(y_out[t % 2], 16)
                    sp.dma_start(y_sample.rearrange("b s d -> (b s) d"), yo[TB - TS:TB, t % 2, :]
                                 ).then_inc(y_out[t % 2], 16)
            sp.wait_ge(y_out[0], 16 * 4)
            sp.wait_ge(y_out[1], 16 * 2)

        @block.gpsimd
        def _(pool):
            n = 0
            for dst, src in (
                    (crow[0:48, :], conv_qkv_w[0].rearrange("t (c p) -> (t c) p", p=P)),
                    (crow[48:52, :], conf_dw_b[0].rearrange("(c p) -> c p", p=P)),
                    (crow[52:56, :], conf_ln_w[0].rearrange("(c p) -> c p", p=P)),
                    (crow[56:60, :], conf_ln_b[0].rearrange("(c p) -> c p", p=P)),
                    (crow[60:61, :], gdn_norm_w),
                    (dwrow[:], conf_dw_w[0].rearrange("t (c p) -> (t c) p", p=P)),
                    (sconf[:], state_conf[0].rearrange("(r b) t c -> (b t) r c", r=2)),
                    (sqkv[:], state_qkv[0].rearrange("b t c -> (b t) c")),
                    (dtb[:, 0:HEADS], dt_bias.to_broadcast([P, HEADS])),
                    (dtb[:, HEADS:], a_log.to_broadcast([P, HEADS]))):
                pool.dma_start(dst, src).then_inc(small_in, 16)
                n += 1
            assert n == 10

            def op(ins, *name):
                G.op(ins, *name)
                G.now(pool)

            def keep(m, compare, fill, base_, pattern, cm):
                op(pool.affine_select(out=m, in_=m, compare_op=compare, fill=fill, base=base_,
                                      pattern=pattern, channel_multiplier=cm))

            op(pool.memset(ident[:], 0.0))
            keep(ident[:], ALU.not_equal, 1.0, 0, [[-1, P]], 1)
            op(pool.memset(ones[:], 1.0), "ident")
            op(pool.memset(tri[:], 1.0))
            keep(tri[:], ALU.is_ge, 0.0, 0, [[1, P]], -1)
            op(pool.memset(neg[:], 0.0))
            keep(neg[:], ALU.is_ge, -BIG, 0, [[1, P]], -1)
            op(pool.memset(pos[:], 0.0))
            keep(pos[:], ALU.is_gt, BIG, 0, [[-1, P]], 1)

            def within(m, width, fill, inner):
                n_ = m.shape[1] // (width if inner else 1)
                v = m.rearrange("p (b w) -> p b w", w=width) if inner else m
                tail = [[0, width]] if inner else []
                keep(v, ALU.is_ge, fill, 0, [[-width, n_]] + tail, 1)
                keep(v, ALU.is_ge, fill, width - 1, [[width, n_]] + tail, -1)

            op(pool.memset(diag16[:], 1.0))
            within(diag16[:], 16, 0.0, True)
            op(pool.memset(same_s[:], 1.0))
            within(same_s[:], STEPS, 0.0, True)
            op(pool.memset(seq_of[:], 1.0))
            within(seq_of[:], STEPS, 0.0, False)
            op(pool.tensor_copy(tri_s[:], tri[0:TS, 0:TS]))
            within(tri_s[:], STEPS, 0.0, True)
            op(pool.tensor_copy(neg_s[:], neg[0:TS, 0:TS]))
            within(neg_s[:], STEPS, -BIG, True)
            op(pool.tensor_copy(pos_s[:], pos[0:TS, 0:TS]))
            within(pos_s[:], STEPS, BIG, True)
            op(pool.iota(iota[:], pattern=[[1, P]], base=0, channel_multiplier=0,
                         allow_small_or_imprecise_dtypes=True), "masks")

            T.wait(pool, "xT", 1, NTB - 1, 1)
            V.wait(pool, "xn", 1, NTB - 1)
            op(pool.memset(qext[:, :, 0:QC - 1], 0.0))
            op(pool.memset(gext[:, 0:CC - 1], 0.0))
            op(pool.memset(tok[:], 1.0))
            op(pool.memset(state[:], 0.0), "zeros")

            outs_ = 0
            pool.dma_start(conf_sample[0][:, 0:CC - 1 - STEPS, :], state_conf[0][:, STEPS:CC - 1, :]
                           ).then_inc(out_done, 16)
            A.wait(pool, "tails")
            V.wait(pool, "tails")
            pool.dma_start(qkv_prompt[0, 0], RA2[0:QC - 1, 0:QKV]).then_inc(out_done, 16)
            for s in range(1, STEPS):
                pool.dma_start(qkv_sample[0][:, s - 1, :],
                               RA2[QC - 1 + s:QC - 1 + s + STEPS * (NSEQ - 1) + 1:STEPS, 0:QKV]
                               ).then_inc(out_done, 16)
            pool.dma_start(conf_prompt[0, 0], RA3[0:CC - 1, :]).then_inc(out_done, 16)
            pool.dma_start(conf_sample[0][:, CC - 1 - STEPS:, :], RA3[CC - 1:, :]).then_inc(out_done, 16)
            outs_ += 7
            pool.wait_ge(out_done, 16 * outs_)
            op(pool.memset(spare[0:1, 0:1], 0.0), "tails_out")
            def load_state(n):
                pool.dma_start(SS[n % 2][:], state_gdn[0].rearrange("b h k v -> h k b v")[n % HEADS]
                               ).then_inc(ss_in[n % 2], 16)

            def store_state(hh):
                V.wait(pool, "ss", hh)
                pool.dma_start(gdn_sample[0].rearrange("b h k v -> h k b v")[hh], SS[hh % 2][:]
                               ).then_inc(ss_out[hh % 2], 16)

            A.wait(pool, "wT", SAMPLE)
            V.wait(pool, "r0b", SAMPLE)
            T.wait(pool, "wT", SAMPLE)
            load_state(0)
            load_state(1)
            for n in range(2, HEADS + 2):
                T.wait(pool, "swh", n - 2)
                load_state(n)
            for hh in range(HEADS):
                store_state(hh)
                if hh < 2:
                    pool.wait_ge(ss_out[hh], 16)
                    load_state(HEADS + 2 + hh)
            V.wait(pool, "su", SAMPLE - 1)
            pool.dma_start(gdn_prompt[0, 0].rearrange("h k v -> k h v"), state[:]).then_inc(out_done, 16)
            pool.wait_ge(ss_out[0], 32)
            pool.wait_ge(ss_out[1], 32)
            pool.wait_ge(out_done, 16 * (outs_ + 1))
            op(pool.memset(spare[0:1, 0:1], 0.0), "mixer", "last")

        @block.tensor
        def _(pe):
            mm = pe.matmul

            G.wait(pe, "ident")
            pe.wait_ge(small_in, 160)
            pe.transpose(bank[4][:, 0:61], crow[:], ident[0:61, 0:61])
            T.op(pe.transpose(bank[4][:, 128:128 + CC * NG], dwrow[:], ident[0:CC * NG, 0:CC * NG]), "cols")
            for c in range(NQ):
                last = pe.transpose(bank[5][:, 24 * c:24 * c + 24], sqkv[:, P * c:P * c + P], ident[0:24, 0:24])
            T.op(last, "sqT")
            for c in range(NG):
                for r in range(2):
                    last = pe.transpose(bank[6 + c // 2][:, 240 * (c % 2) + 120 * r:240 * (c % 2) + 120 * r + 120],
                                        sconf[:, r, P * c:P * c + P], ident[0:120, 0:120])
            T.op(last, "scT")

            def norm(k):
                for t in range(NTB):
                    V.wait(pe, "xn", k, t)
                    for i in range(2):
                        if t >= 2:
                            V.wait(pe, "xlow", k, t - 2, i)
                        for j in range(4):
                            last = pe.transpose(bank[2 * (t % 2) + i][:, j * TB:(j + 1) * TB],
                                                xn[:, t % 2, (4 * i + j) * P:(4 * i + j + 1) * P],
                                                ident[0:TB, 0:TB])
                        T.op(last, "xT", k, t, i)

            def linear(b):
                kind, _, parts = BLOCKS[b]
                V.wait(pe, "low", b)
                W = WR[:, b % 2]
                for u in range(UNIT0[b], UNIT0[b + 1]):
                    if u >= 4:
                        unit_read(pe, u - 4)
                    n = u - UNIT0[b]
                    for kt in range(KT):
                        for i, (pw, px) in enumerate(((0, 0), (0, 1), (1, 0))):
                            go = dict(start=(kt == 0 and i == 0), stop=(kt == KT - 1 and i == 2))
                            if kind == "out":
                                last = mm(bank[u % 4][0:TB, 0:WB], xT[:, px, kt, n * TB:(n + 1) * TB],
                                          W[:, pw, kt, :], **go)
                            else:
                                m, half = n // 2, n % 2
                                last = mm(bank[u % 4][:, 0:HALF], W[:, pw, kt, m * P:(m + 1) * P],
                                          xT[:, px, kt, half * HALF:(half + 1) * HALF], **go)
                    T.op(last, "unit", u)

            norm(1)
            V.wait(pe, "xlow", 1, NTB - 1, 1)
            for b in range(first["out"]):
                linear(b)

            unit_read(pe, UNIT0[first["ab"] + 1] - 1)
            V.wait(pe, "scT")
            for ci, (c0, c) in enumerate(CHUNKS):
                last = pe.transpose(bank[4][0:c, 8 * ci:8 * ci + 8], abT[:, c0:c0 + c], ident[0:8, 0:8])
            T.op(last, "ab")
            V.wait(pe, "g")
            V.wait(pe, "gm")
            for ci, (c0, c) in enumerate(CHUNKS):
                s_ = ci == SAMPLE
                mm(bank[5][0:c, 8 * ci:8 * ci + 4], (tri_s if s_ else tri)[0:c, 0:c], tok[0:c, GD, ci, :])
                rows_ = c if s_ else P
                mm(bank[5][0:rows_, 8 * ci + 4:8 * ci + 8], (same_s if s_ else ones)[0:c, 0:rows_],
                   tok[0:c, GD, ci, :])
            T.op(mm(bank[6][:, 0:TS], ones[0:TS, :], gm[:].rearrange("p b h -> p (b h)")), "cum")
            for c_ in range(2 * HEADS):
                A.wait(pe, "qk2", c_)
                for ci, (c0, c) in enumerate(CHUNKS):
                    last = mm(bank[7][0:c, 8 * ci + c_:8 * ci + c_ + 1], sqb[c_ % 2][:, c0:c0 + c], ones[:, 0:1])
                T.op(last, "qk2", c_)
            A.wait(pe, "qtail")
            V.wait(pe, "ctail")
            V.wait(pe, "cum")
            V.wait(pe, "ab")
            V.wait(pe, "qk2")
            for c in range(NQ):
                last = pe.transpose(bank[4 + c // 4][0:QC - 1 + TS, P * (c % 4):P * (c % 4) + P], qtail[:, c, :],
                                    ident[:])
            for c in range(NG):
                last = pe.transpose(bank[7][0:CC - 1 + TS, P * c:P * c + P], ctail[:, c, :], ident[:])
            T.op(last, "tails")

            for ci, (c0, c) in enumerate(CHUNKS):
                s_ = ci == SAMPLE

                def group(n, *needs):
                    i = WHERE[n, ci]
                    if i >= 4:
                        m, cj, e = GROUPS[i - 4]
                        e.wait(pe, m, cj)
                    elif i == 0:
                        A.wait(pe, "tails")
                        V.wait(pe, "tails")
                    for e, m in needs:
                        e.wait(pe, m, ci)
                    return gbank(n, ci)

                def each(n, f, width, *needs, only=range(HEADS)):
                    b_ = group(n, *needs)
                    for i, hh in enumerate(only):
                        last = f(b_, i, hh)
                    T.op(last, n, ci)

                def prod4(n, L, R, *needs):
                    each(n, lambda b_, i, hh: mm(b_[0:c, i * c:(i + 1) * c], L[0:c, hh, 0:c], R[0:c, hh, 0:c]),
                         c, *needs)

                each("k", lambda b_, i, hh: pe.transpose(b_[0:c, i * P:(i + 1) * P],
                                                         qkvT[:, HEADS + hh, c0:c0 + c], ident[:]), P)
                each("v", lambda b_, i, hh: pe.transpose(b_[0:c, i * P:(i + 1) * P],
                                                         qkvT[:, 2 * HEADS + hh, c0:c0 + c], ident[:]), P)
                each("gb", lambda b_, i, hh: mm(b_[0:c, i * c:(i + 1) * c],
                                                tok[0:c, GD, ci, hh:hh + 1].to_broadcast([c, c]),
                                                (tri_s if s_ else tri)[0:c, 0:c]), c)
                each("khT", lambda b_, i, hh: pe.transpose(b_[:, i * c:(i + 1) * c], KH[0:c, hh, :],
                                                           ident[0:c, 0:c]), c, (V, "k"))
                each("kk", lambda b_, i, hh: mm(b_[0:c, i * c:(i + 1) * c], KHT[:, hh, 0:c], KHT[:, hh, 0:c]),
                     c, (A, "khT"))
                each("kq", lambda b_, i, hh: mm(b_[0:c, i * c:(i + 1) * c], KHT[:, hh, 0:c],
                                                qkvT[:, hh, c0:c0 + c]), c)
                each("ldT", lambda b_, i, hh: pe.transpose(b_[0:c, i * c:(i + 1) * c], M[0][0:c, hh, 0:c],
                                                           ident[0:c, 0:c]), c, (V, "Ld"))
                prod4("p2", M[1], M[0], (A, "ldT"))
                prod4("pt2", M[0], M[1])
                prod4("t1", M[2], M[4], (A, "p2"), (V, "t0"))
                if not s_:
                    prod4("p4", M[3], M[2], (V, "pt2"))
                    prod4("pt4", M[2], M[3])
                    prod4("t2", M[5], M[4], (A, "p4"), (V, "t1"))
                    prod4("p8", M[6], M[5], (V, "pt4"))
                    prod4("t3", M[2], M[4], (A, "p8"), (V, "t2"))
                solved = "t1" if s_ else "t3"
                if c == P:
                    prod4("n", M[4], M[7], (V, "t3"), (V, "Lo"))
                    prod4("nt", M[7], M[4])
                    prod4("n2", M[1], M[0], (V, "nt"), (A, "n"))
                    prod4("nt2", M[0], M[1])
                    prod4("nt4", M[3], M[5], (A, "n2"), (V, "nt2"))

                def solve(n, L, R, *needs):
                    for x, only in (("a", (0, 1)), ("b", (2, 3))):
                        each(n + x, lambda b_, i, hh: mm(b_[0:c, i * 256:(i + 1) * 256], L[0:c, hh, 0:c],
                                                         R[0:c, hh].rearrange("p x d -> p (x d)")),
                             0, *needs, only=only)

                solve("r0", M[4], RA, (V, solved), (V, "RA"))
                R = RB
                if c == P:
                    solve("r1", M[6], RB, (A, "nt4"), (A, "r0a"), (V, "r0b"))
                    solve("r2", M[5], RA, (V, "r1b"))
                    solve("r3", M[1], RB, (V, "r2b"))
                    R = RA
                each("wT", lambda b_, i, hh: pe.transpose(b_[:, i * c:(i + 1) * c], R[0:c, hh, 1, :],
                                                          ident[0:c, 0:c]), c,
                     *([(V, "r3b")] if c == P else [(A, "r0a"), (V, "r0b")]))
                if s_:
                    b_ = group("sw", (A, "wT"))
                    for hh in range(HEADS):
                        pe.wait_ge(ss_in[hh % 2], 16 * (hh // 2 + 1))
                        for q in range(NSEQ):
                            last = mm(b_[:, 64 * hh + 8 * q:64 * hh + 8 * q + 8], SS[hh % 2][:, q, :],
                                      WQ[:, hh, q, :])
                        T.op(last, "swh", hh)
                    each("ws", lambda b2, i, hh: pe.transpose(b2[0:c, i * P:(i + 1) * P],
                                                              M[2][:, 0, hh * TS:(hh + 1) * TS], ident[:]),
                         P, (V, "sw"))
                    each("qs", lambda b2, i, hh: pe.transpose(b2[0:c, i * P:(i + 1) * P],
                                                              M[2][:, 1, hh * TS:(hh + 1) * TS], ident[:]), P)
                else:
                    if ci:
                        V.wait(pe, "su", ci - 1)
                    each("ws", lambda b2, i, hh: mm(b2[0:c, i * P:(i + 1) * P], M[2][:, hh, 0:c], state[:, hh, :]),
                         P, (A, "wT"))
                    each("qs", lambda b2, i, hh: mm(b2[0:c, i * P:(i + 1) * P], qkvT[:, hh, c0:c0 + c],
                                                    state[:, hh, :]), P)
                each("o1", lambda b2, i, hh: mm(b2[0:c, i * P:(i + 1) * P], AT[0:c, hh, 0:c], VN[0:c, hh, :]),
                     P, (V, "ws"), (V, "kq"))
                if s_:
                    for hh in range(HEADS):
                        for i in range(2):
                            b_ = group(f"su{hh}{i}", (V, f"ktm{hh}"))
                            for q in range(4):
                                last = mm(b_[:, P * q:P * q + P], KTM[0:c, P * (4 * i + q):P * (4 * i + q) + P],
                                          VN[0:c, hh, :])
                            T.op(last, f"su{hh}{i}", ci)
                else:
                    each("su", lambda b2, i, hh: mm(b2[:, i * P:(i + 1) * P], KE[0:c, hh, :], VN[0:c, hh, :]),
                         P, (V, "KE"))

            for ci, (c0, c) in enumerate(CHUNKS):
                V.wait(pe, "on", ci)
                if ci >= 2:
                    V.wait(pe, "mix", ci - 2)
                for hh in range(HEADS):
                    last = pe.transpose(bank[4 + ci % 2][:, hh * c:(hh + 1) * c], ONB[ci % 2][0:c, hh, :],
                                        ident[0:c, 0:c])
                T.op(last, "on", ci)
            for t in range(NTB):
                V.wait(pe, "cconv", NG - 1)
                if t >= 2:
                    A.wait(pe, "cn", t - 2)
                for c in range(NG):
                    last = pe.transpose(bank[6 + t % 2][0:TB, c * P:(c + 1) * P], cT[:, c, t * TB:(t + 1) * TB],
                                        ident[:])
                T.op(last, "cn", t)
            for t in range(NTB):
                V.wait(pe, "ln", t)
                if t == 0:
                    V.wait(pe, "mix", len(CHUNKS) - 1)
                if t >= 2:
                    A.wait(pe, "csilu", t - 2)
                for c in range(NG):
                    last = pe.transpose(bank[4 + t % 2][:, c * TB:(c + 1) * TB], CN[:, t, c * P:(c + 1) * P],
                                        ident[0:TB, 0:TB])
                T.op(last, "ln", t)
            T.counts["mixer", "last"] = T.n

            V.wait(pe, "mixlow", "last")
            for b in range(first["out"], first["query"]):
                linear(b)
            unit_read(pe, UNIT0[first["query"]] - 1)
            pe.wait_ge(h_in[1], 96)
            for i in range(4):
                for j in range(4):
                    last = pe.transpose(bank[4 + i][:, j * P:(j + 1) * P], keysrow[:, 4 * i + j, :], ident[:])
            T.op(last, "keys")
            norm(2)
            V.wait(pe, "xlow", 2, NTB - 1, 1)

            def score(ct):
                unit_read(pe, UNIT0[first["query"]] + 2 * ct + 1)
                if ct >= 2:
                    A.wait(pe, "score", ct - 2)
                else:
                    A.wait(pe, "keys")
                for t in range(NTB):
                    last = mm(bank[4 + 2 * (ct % 2) + t // 4][0:TB, (t % 4) * P:(t % 4) * P + P],
                              qT[:, ct % 2, t * TB:(t + 1) * TB], keysT[:, ct, :])
                T.op(last, "score", ct)

            for b in range(first["query"], nb):
                linear(b)
                i = b - first["query"]
                score(2 * i)
                score(2 * i + 1)

            for t in range(NTB):
                V.wait(pe, "gates", t)
                if t >= 2:
                    V.wait(pe, "pairT", t - 2)
                for i in range(3):
                    last = pe.transpose(bank[t % 2][:, i * TB:(i + 1) * TB], pick[:, i, :], ident[0:TB, 0:TB])
                T.op(last, "pairT", t)

            with pe.Fori(0, NGB // 2, 1) as i:
                for n in range(GB // 2):
                    group_ = i * (GB // 2) + (n + 1)
                    pe.wait_ge(is_ready, group_)
                    pe.wait_ge(gate_bank, group_)
                    for k in range(4):
                        s_ = (n % 2) * 4 + k
                        o_ = bank[n % 4][:, k * NK:(k + 1) * NK]
                        mm(o_, is1[:, s_, :], is2[:, s_, 0, :], start=True, stop=False)
                        last = mm(o_, is1[:, s_, :], is2[:, s_, 1, :], start=False, stop=True)
                    last.then_inc(gate_mm, 1)

            def load_wait(e, k):
                pe.wait_ge(ut_low, 2 * e + (k + 1))

            def turn_u(g, j):
                e = GE * g + j
                for k in range(2):
                    load_wait(e, k)
                    for i in range(4):
                        last = pe.transpose(bank[k][:, i * P:(i + 1) * P],
                                            Uraw[:, par(g), j, (4 * k + i) * P:(4 * k + i + 1) * P], ident[:])
                    last.then_inc(ut_mm, 1)

            def scores_of(g, j):
                e = GE * g + j
                pe.wait_ge(ut_low, 2 * e + 4)
                for half in range(2):
                    pe.wait_ge(gelu_done, 2 * e + (half + 1))
                    for kt in range(KT):
                        for i, (pw, px) in enumerate(((0, 0), (0, 1), (1, 0))):
                            last = mm(bank[2 + half][:, 0:HALF], UT[:, j % 2, pw, kt, :],
                                      xT[:, px, kt, half * HALF:(half + 1) * HALF],
                                      start=(kt == 0 and i == 0), stop=(kt == KT - 1 and i == 2))
                    last.then_inc(s_mm, 1)

            def first_part(g, final=False):
                for j in range(GE):
                    nxt = (g, j + 1) if j + 1 < GE else (g + 1, 0)
                    if not (final and j + 1 == GE):
                        if nxt[1] == 0:
                            pe.wait_ge(u_in[par(nxt[0])], 16 * (half_of(nxt[0]) + 1))
                        turn_u(*nxt)
                    scores_of(g, j)

            def second_part(g):
                pe.wait_ge(a_low, GE * g + GE)
                pe.wait_ge(v_low, 1 * g + 1)
                for u in range(2 * KT):
                    dt, half = u // 2, u % 2
                    pe.wait_ge(y_add, 2 * KT * g + (u + 1))
                    for j in range(GE):
                        for i, (pw, pa) in enumerate(((0, 0), (0, 1), (1, 0))):
                            last = mm(bank[4 + u % 4][:, 0:HALF], VR[:, pw, j, dt * P:(dt + 1) * P],
                                      AR[:, par(g), pa, j, half * HALF:(half + 1) * HALF],
                                      start=(j == 0 and i == 0), stop=(j == GE - 1 and i == 2))
                    last.then_inc(y_mm, 1)

            grant(pe, s_mm, 2)
            grant(pe, y_mm, 2 * KT)
            pe.wait_ge(u_in[0], 16)
            turn_u(Grp(0), 0)
            first_part(Grp(0))
            with pe.Fori(0, NGRP // 2 - 1, 1) as i:
                for k in range(2):
                    first_part(Grp(k + 1, i))
                    second_part(Grp(k, i))
            first_part(Grp(NGRP - 1), True)
            second_part(Grp(NGRP - 2))
            second_part(Grp(NGRP - 1))

            V.wait(pe, "y_all")
            for t in range(NTB):
                for i in range(2):
                    if t >= 2:
                        V.wait(pe, "hf", t - 2, i)
                    for j in range(4):
                        last = pe.transpose(bank[2 * (t % 2) + i][0:TB, j * P:(j + 1) * P],
                                            yT[:, 4 * i + j, t * TB:(t + 1) * TB], ident[:])
                    T.op(last, "y", t, i)

        @block.scalar
        def _(act):
            def fn(out, in_, f, *name, **kw):
                return A.op(act.activation(out, in_, f, **kw), *name)

            def high(b):
                n = sum(x[2] for x in BLOCKS[b][2])
                act.wait_ge(raw_in[b % 4], 16 * raw_count[b])
                if b >= 2:
                    T.wait(act, "unit", UNIT0[b - 1] - 1)
                fn(WR[:, b % 2, 0, :, 0:n], RAW[:, b % 4, :, 0:n], ACT.Copy, "high", b)

            def norm(k):
                act.wait_ge(h_in[k - 1], 80 if k == 1 else 96)
                for t in range(NTB):
                    if k == 2:
                        V.wait(act, "h2", t)
                    fn(sq[:], h[:, t, :], ACT.Square, "ss", k, t, accum_out=ss[:, t:t + 1])
                    A.now(act)
                V.wait(act, "ms", k)
                fn(ss[:, 16:16 + NTB], ss[:, 8:8 + NTB], ACT.Sqrt, "rt", k)
                for t in range(NTB):
                    for i in range(2):
                        T.wait(act, "xT", k, t, i)
                        fn(xT[:, 0, 4 * i:4 * i + 4, t * TB:(t + 1) * TB],
                           bank[2 * (t % 2) + i][:, 0:4 * TB].rearrange("p (k n) -> p k n", k=4), ACT.Copy,
                           "xhigh", k, t, i)

            def seqs(ap):
                return ap.rearrange("p (q s) -> p q s", q=NSEQ)

            def evacuate(b):
                kind, i, _ = BLOCKS[b]
                for u in range(UNIT0[b], UNIT0[b + 1]):
                    n = u - UNIT0[b]
                    m, half = n // 2, n % 2
                    bk = bank[u % 4]
                    src = bk[:, 0:HALF]
                    cols_ = slice(half * HALF, (half + 1) * HALF)
                    T.wait(act, "unit", u)
                    if kind == "ab":
                        fn(abT[:, cols_], bk[0:2 * HEADS, 0:HALF], ACT.Copy, "unit", u)
                    elif kind == "z":
                        fn(zT[:, 2 * i + m, cols_], src, ACT.Silu, "unit", u)
                    elif kind == "query":
                        ct = 2 * i + m
                        if ct >= 2:
                            T.wait(act, "score", ct - 2)
                        fn(qT[:, ct % 2, cols_], src, ACT.Copy, "unit", u)
                    elif kind == "qkv":
                        c = 2 * i + m
                        e = c % 2
                        if half == 0:
                            if c >= 2:
                                V.wait(act, "qconv", c - 2)
                            fn(qext[:, e, QC - 1:QC - 1 + HALF], src, ACT.Copy, "unit", u)
                        else:
                            k = TP - HALF
                            x = seqs(qext[:, e, QEXT:])
                            fn(qext[:, e, QC - 1 + HALF:QEXT], bk[:, 0:k], ACT.Copy)
                            fn(x[:, :, QC - 1:], seqs(bk[:, k:HALF]), ACT.Copy)
                            if c == 0:
                                V.wait(act, "sqT")
                            fn(x[:, :, 0:QC - 1], seqs(sqT[:, c, :]), ACT.Copy)
                            fn(qtail[:, c, :], bk[:, k - (QC - 1):HALF], ACT.Copy, "unit", u)
                    elif kind == "glu":
                        if n == 0 and i:
                            V.wait(act, "cconv", i - 1)
                        k = TP - HALF
                        if n == 0:
                            fn(gext[:, CC - 1:CC - 1 + HALF], src, ACT.Copy, "unit", u)
                        elif n == 1:
                            x = seqs(gext[:, CEXT:])
                            fn(gext[:, CC - 1 + HALF:CEXT], bk[:, 0:k], ACT.Copy)
                            fn(x[:, :, CC - 1:], seqs(bk[:, k:HALF]), ACT.Copy, "unit", u)
                            if i == 0:
                                V.wait(act, "scT")
                            fn(x[:, :, 0:CC - 1], seqs(scT[:, i, :]), ACT.Copy)
                        else:
                            fn(gate[:, cols_], src, ACT.Sigmoid, "unit", u)

            def silu(c):
                V.wait(act, "qconv", c)
                fn(qkvT[:, c, :], qkvT[:, c, :], ACT.Silu, "silu", c)

            high(0)
            high(1)
            norm(1)
            G.wait(act, "zeros")
            done = 0
            for b in range(first["out"]):
                evacuate(b)
                while done < 2 * BLOCKS[b][1] and BLOCKS[b][0] == "qkv":
                    silu(done)
                    done += 1
                if b + 2 < nb:
                    high(b + 2)
            A.counts["qtail",] = A.n
            while done < NQ:
                silu(done)
                done += 1

            V.wait(act, "ab")
            fn(tok[:, X2], tok[:, BETA], ACT.Exp, scale=-1.0)
            fn(tok[:, X3], tok[:, GD], ACT.Abs)
            A.now(act)
            fn(tok[:, X3], tok[:, X3], ACT.Exp, scale=-1.0)
            fn(dtb[:, HEADS:], dtb[:, HEADS:], ACT.Exp, "exps")
            V.wait(act, "exps")
            fn(tok[:, X3], tok[:, X3], ACT.Ln, "ln")
            V.wait(act, "cum")
            fn(tok[:, EG], tok[:, GC], ACT.Exp)
            fn(tok[:, EL], tok[:, EL], ACT.Exp)
            fn(tok[:, EGL], tok[:, GL], ACT.Exp)
            fn(gls[:], gls[:], ACT.Exp, "cum")
            for c in range(2 * HEADS):
                if c >= 2:
                    T.wait(act, "qk2", c - 2)
                A.now(act)
                fn(sqb[c % 2][:], qkvT[:, c, :], ACT.Square, "qk2", c)
            V.wait(act, "qk2")
            fn(tok[:, RQ], tok[:, RQ], ACT.Sqrt)
            fn(tok[:, RK], tok[:, RK], ACT.Sqrt, "rqk")
            T.wait(act, "tails")
            for i in range(3):
                fn(RA2[0:QC - 1 + TS, 512 * i:512 * i + 512], bank[4 + i][0:QC - 1 + TS, :], ACT.Copy, "tails")

            for ci, (c0, c) in enumerate(CHUNKS):
                s_ = ci == SAMPLE

                def take(n, dst, rows_=c, width=c, only=HEADS):
                    T.wait(act, n, ci)
                    fn(dst, gbank(n, ci)[0:rows_, 0:only * width].rearrange("p (h n) -> p h n", h=only), ACT.Copy,
                       n, ci)

                V.wait(act, "arg", ci)
                fn(M[6][0:c, :, 0:c], M[6][0:c, :, 0:c], ACT.Exp, scale=-1.0)
                fn(M[5][0:c, :, 0:c], M[5][0:c, :, 0:c], ACT.Exp, "exp", ci)
                take("khT", KHT[:, :, 0:c], P)
                take("ldT", M[1][0:c, :, 0:c])
                take("p2", M[2][0:c, :, 0:c])
                if not s_:
                    take("p4", M[5][0:c, :, 0:c])
                    take("p8", M[2][0:c, :, 0:c])
                if c == P:
                    take("n", M[0][:])
                    take("n2", M[3][:])
                    take("nt4", M[6][:])
                T.wait(act, "r0a", ci)
                if ci == 0:
                    G.wait(act, "tails_out")
                fn(RB[0:c, 0:2].rearrange("p h x d -> p h (x d)"),
                   gbank("r0a", ci)[0:c, :].rearrange("p (h n) -> p h n", h=2), ACT.Copy, "r0a", ci)
                if s_:
                    T.wait(act, "wT", ci)
                    for hh in range(HEADS):
                        fn(WQ[:, hh, :, 0:STEPS], seqs(gbank("wT", ci)[:, hh * TS:(hh + 1) * TS]), ACT.Copy)
                        fn(WQ[:, hh, :, STEPS:], seqs(qkvT[:, hh, TP:]), ACT.Copy, "wT", ci)
                else:
                    take("wT", M[2][:, :, 0:c], P)
            V.wait(act, "oss")
            fn(tok[:, OSS], tok[:, OSS], ACT.Sqrt, "oss")

            def mixed(n, src, dst, *wait):
                V.wait(act, *wait) if wait else A.now(act)
                fn(dst, src, ACT.Copy, *n)

            for ci, (c0, c) in enumerate(CHUNKS):
                mixed(("mixhigh", ci), mixf[ci % 2][:, :, 0:c], xT[:, 0, 0:HEADS, c0:c0 + c], "mix", ci)
            G.wait(act, "mixer", "last")
            for t in range(NTB):
                T.wait(act, "cn", t)
                fn(CN[:, t, :], bank[6 + t % 2][0:TB, :], ACT.Copy, "cn", t)
            V.wait(act, "cvar")
            fn(lnst[:, :, 8:9], lnst[:, :, 8:9], ACT.Sqrt, "cvar")
            for t in range(NTB):
                T.wait(act, "ln", t)
                V.wait(act, "mixlow", len(CHUNKS) - 1) if t < 2 else V.wait(act, "clow", t - 2)
                for c in range(NG):
                    fn(mixf[t % 2][:, c, 0:TB], bank[4 + t % 2][:, c * TB:(c + 1) * TB], ACT.Silu, "csilu", t,
                       bias=cols[:, 56 + c:57 + c], scale=cols[:, 52 + c:53 + c])
                mixed(("chigh", t), mixf[t % 2][:, :, 0:TB], xT[:, 0, HEADS:KT, t * TB:(t + 1) * TB])
            A.counts["mixer", "last"] = A.n

            for b in range(first["out"], first["query"]):
                high(b + 2)
            norm(2)
            act.wait_ge(h2_done, 16)
            for i in range(4):
                T.wait(act, "keys") if i == 0 else None
                fn(keysT[:, 4 * i:4 * i + 4, :], bank[4 + i][:, :].rearrange("p (k n) -> p k n", k=4), ACT.Copy,
                   "keys")
            for b in range(first["query"], nb):
                evacuate(b)
                if b + 2 < nb:
                    high(b + 2)
                for ct in (2 * (b - first["query"]), 2 * (b - first["query"]) + 1):
                    T.wait(act, "score", ct)
                    fn(scores[:, 0:4, ct, :], bank[4 + 2 * (ct % 2)][0:TB, :].rearrange("p (t n) -> p t n", t=4),
                       ACT.Copy)
                    fn(scores[:, 4, ct, :], bank[5 + 2 * (ct % 2)][0:TB, 0:P], ACT.Copy, "score", ct)
            for t in range(NTB):
                V.wait(act, "top", t)
                fn(top16[:], top16[:], ACT.Exp, "gexp", t)

            grant(act, gate_bank, 4)
            grant(act, gblk_out[0], 16)
            grant(act, gblk_out[1], 16)
            with act.Fori(0, NGB // 2, 1) as i:
                for n in range(GB // 2):
                    blk, q = n // (GB // 4), n % (GB // 4)
                    act.wait_ge(gate_mm, i * (GB // 2) + (n + 3))
                    if q == 0:
                        act.wait_ge(gblk_out[blk], i * 16 + 16)
                    act.activation(gblk[:, blk, :, 4 * q:4 * q + 4],
                                   bank[n % 4][:, :].rearrange("p (k n) -> p n k", k=4), ACT.Copy
                                   ).then_inc(gate_bank, 1)

            def split_u(g, j):
                e = GE * g + j
                for k in range(2):
                    act.wait_ge(ut_mm, 2 * e + (k + 1))
                    if k == 0:
                        act.wait_ge(s_mm, 2 * e)
                    act.activation(UT[:, j % 2, 0, 4 * k:4 * k + 4, :],
                                   bank[k][:, :].rearrange("p (k n) -> p k n", k=4), ACT.Copy
                                   ).then_inc(ut_high, 1)

            def first_part(g, final=False):
                for j in range(GE):
                    e = GE * g + j
                    nxt = (g, j + 1) if j + 1 < GE else (g + 1, 0)
                    if not (final and j + 1 == GE):
                        split_u(*nxt)
                    act.wait_ge(a_mul, e + 1)
                    for half in range(2):
                        act.wait_ge(s_mm, 2 * e + (half + 3))
                        act.activation(actv[:, j % 2, half * HALF:(half + 1) * HALF], bank[2 + half][:, 0:HALF],
                                       ACT.Gelu).then_inc(gelu_done, 1)
                    act.wait_ge(a_mul, e + 3)
                    if j == 0:
                        act.wait_ge(y_mm, 2 * KT * g)
                    act.activation(AR[:, par(g), 0, j, :], prod[:, j % 2, :], ACT.Copy).then_inc(a_high, 1)

            def split_v(g):
                act.wait_ge(v_in[par(g)], 16 * (half_of(g) + 1))
                act.wait_ge(y_mm, 2 * KT * g + 2 * KT)
                act.activation(VR[:, 0], Vraw[:, par(g)], ACT.Copy).then_inc(v_high, 1)

            grant(act, gelu_done, 2)
            act.wait_ge(gblk_out[0], 16 * (NGB // 2 + 1))
            act.wait_ge(gblk_out[1], 16 * (NGB // 2 + 1))
            split_u(Grp(0), 0)
            first_part(Grp(0))
            with act.Fori(0, NGRP // 2 - 1, 1) as i:
                for k in range(2):
                    split_v(Grp(k, i))
                    first_part(Grp(k + 1, i))
            split_v(Grp(NGRP - 2))
            first_part(Grp(NGRP - 1), True)
            split_v(Grp(NGRP - 1))

            for t in range(NTB):
                V.wait(act, "hf", t, 1)
                A.now(act)
                fn(yo[:, 0, :], hf[:, t, :], ACT.Square, "ss", 3, t, accum_out=fs[:, t:t + 1])
            V.wait(act, "ms", 3)
            fn(fs[:, 16:16 + NTB], fs[:, 8:8 + NTB], ACT.Sqrt, "rt", 3)

        @block.vector
        def _(dve):
            def op(ins, *name):
                return V.op(ins, *name)

            def chain(ins, *name):
                V.op(ins, *name)
                V.now(dve)

            tt = dve.tensor_tensor

            def low(b):
                n = sum(x[2] for x in BLOCKS[b][2])
                A.wait(dve, "high", b)
                op(tt(WR[:, b % 2, 1, :, 0:n], RAW[:, b % 4, :, 0:n], WR[:, b % 2, 0, :, 0:n].bitcast(F32),
                      ALU.subtract), "low", b)

            def rsqrt_in(src, dst, scale):
                chain(dve.tensor_scalar(dst, src, scale, EPS, ALU.mult, ALU.add))

            def norm(k):
                A.wait(dve, "ss", k, NTB - 1)
                op(dve.tensor_scalar(ss[:, 8:8 + NTB], ss[:, 0:NTB], 1.0 / D, EPS, ALU.mult, ALU.add), "ms", k)
                A.wait(dve, "rt", k)
                chain(dve.reciprocal(ss[:, 8:8 + NTB], ss[:, 16:16 + NTB]))
                dve.wait_ge(row_in[k - 1], 16)

                def lows(t):
                    for i in range(2):
                        A.wait(dve, "xhigh", k, t, i)
                        o_ = (slice(None), slice(4 * i, 4 * i + 4), slice(t * TB, (t + 1) * TB))
                        op(tt(xT[:, 1][o_], bank[2 * (t % 2) + i][:, 0:4 * TB].rearrange("p (k n) -> p k n", k=4),
                              xT[:, 0][o_].bitcast(F32), ALU.subtract), "xlow", k, t, i)

                for t in range(NTB):
                    if t >= 2:
                        T.wait(dve, "xT", k, t - 2, 1)
                    op(dve.scalar_tensor_tensor(xn[:, t % 2, :], h[:, t, :], ss[:, 8 + t:9 + t], wrow[:],
                                                ALU.mult, ALU.mult), "xn", k, t)
                    if t:
                        lows(t - 1)
                lows(NTB - 1)

            def conv(dst, dstq, src, srcq, w, taps, width, bias=None):
                d3 = dstq.rearrange("p (q s) -> p q s", q=NSEQ)
                s3 = srcq.rearrange("p (q s) -> p q s", q=NSEQ)
                for j in range(taps):
                    a, b = src[:, j:j + TP], s3[:, :, j:j + STEPS]
                    if j == 0:
                        if bias is None:
                            op(dve.tensor_scalar(dst, a, w(j), None, ALU.mult))
                            op(dve.tensor_scalar(d3, b, w(j), None, ALU.mult))
                        else:
                            op(dve.tensor_scalar(dst, a, w(j), bias, ALU.mult, ALU.add))
                            op(dve.tensor_scalar(d3, b, w(j), bias, ALU.mult, ALU.add))
                    else:
                        V.now(dve)
                        op(dve.scalar_tensor_tensor(dst, a, w(j), dst, ALU.mult, ALU.add))
                        op(dve.scalar_tensor_tensor(d3, b, w(j), d3, ALU.mult, ALU.add))

            T.wait(dve, "cols")
            op(dve.tensor_copy(cols[:], bank[4][:, 0:61]))
            op(dve.tensor_copy(dwcols[:], bank[4][:, 128:128 + CC * NG]))
            T.wait(dve, "sqT")
            op(dve.tensor_copy(sqT[:].rearrange("p c n -> p (c n)"), bank[5][:, 0:24 * NQ]), "sqT")
            T.wait(dve, "scT")
            for i in range(2):
                chain(dve.tensor_copy(scT[:, 2 * i:2 * i + 2, :].rearrange("p c n -> p (c n)"),
                                      bank[6 + i][:, 0:480]), "scT")
            low(0)
            low(1)
            norm(1)
            for b in range(first["out"]):
                kind, i, _ = BLOCKS[b]
                if kind == "qkv":
                    for c in (2 * i, 2 * i + 1):
                        e = c % 2
                        A.wait(dve, "unit", UNIT0[b] + 2 * (c % 2) + 1)
                        G.wait(dve, "zeros")
                        conv(qkvT[:, c, 0:TP], qkvT[:, c, TP:], qext[:, e, 0:QEXT], qext[:, e, QEXT:],
                             lambda j: cols[:, NQ * j + c:NQ * j + c + 1], QC, QEXT)
                        V.counts["qconv", c] = V.n
                elif kind == "glu":
                    c = i
                    x = gext[:, CC - 1:CEXT]
                    xs = gext[:, CEXT:].rearrange("p (q s) -> p q s", q=NSEQ)
                    A.wait(dve, "unit", UNIT0[b] + 3)
                    op(tt(x, x, gate[:, 0:TP], ALU.mult))
                    chain(tt(xs[:, :, CC - 1:], xs[:, :, CC - 1:],
                             gate[:, TP:].rearrange("p (q s) -> p q s", q=NSEQ), ALU.mult))
                    op(dve.tensor_copy(ctail[:, c, 0:CC - 1], x[:, TP - (CC - 1):]))
                    op(dve.tensor_copy(ctail[:, c, CC - 1:].rearrange("p (q s) -> p q s", q=NSEQ),
                                       xs[:, :, CC - 1:]), "ctail")
                    conv(cT[:, c, 0:TP], cT[:, c, TP:], gext[:, 0:CEXT], gext[:, CEXT:],
                         lambda j: dwcols[:, NG * j + c:NG * j + c + 1], CC, CEXT, cols[:, 48 + c:49 + c])
                    V.counts["cconv", c] = V.n
                if b + 2 < nb:
                    low(b + 2)

            G.wait(dve, "masks")
            T.wait(dve, "ab")
            for ci, (c0, c) in enumerate(CHUNKS):
                op(tt(tok[0:c, GD, ci, :], bank[4][0:c, 8 * ci:8 * ci + 4], dtb[0:c, 0:HEADS], ALU.add))
                op(dve.tensor_copy(tok[0:c, BETA, ci, :], bank[4][0:c, 8 * ci + 4:8 * ci + 8]), "ab")
            A.wait(dve, "exps")
            op(dve.tensor_scalar(tok[:, X2], tok[:, X2], 1.0, None, ALU.add))
            chain(dve.tensor_scalar(tok[:, X3], tok[:, X3], 1.0, None, ALU.add), "exps")
            op(dve.reciprocal(tok[:, BETA], tok[:, X2]))
            A.wait(dve, "ln")
            chain(dve.scalar_tensor_tensor(tok[:, GD], tok[:, GD], 0.0, tok[:, X3], ALU.max, ALU.add))
            chain(dve.scalar_tensor_tensor(tok[:, GD], tok[:, GD], -1.0,
                                           dtb[:, HEADS:].unsqueeze(1).to_broadcast([P, len(CHUNKS), HEADS]),
                                           ALU.mult, ALU.mult), "g")
            op(tt(gm[:], tok[0:TS, GD, SAMPLE, :].unsqueeze(1).to_broadcast([TS, NSEQ, HEADS]),
                  seq_of[:].unsqueeze(2).to_broadcast([TS, NSEQ, HEADS]), ALU.mult), "gm")
            T.wait(dve, "cum")
            op(dve.tensor_copy(gls[:].rearrange("p b h -> p (b h)"), bank[6][:, 0:TS]))
            for ci, (c0, c) in enumerate(CHUNKS):
                n = c if ci == SAMPLE else P
                op(dve.tensor_copy(tok[0:c, GC, ci, :], bank[5][0:c, 8 * ci:8 * ci + 4]))
                op(dve.tensor_copy(tok[0:n, GL, ci, :], bank[5][0:n, 8 * ci + 4:8 * ci + 8]))
            V.now(dve)
            op(tt(tok[:, EL], tok[:, GL], tok[:, GC], ALU.subtract), "cum")
            T.wait(dve, "qk2", 2 * HEADS - 1)
            for ci, (c0, c) in enumerate(CHUNKS):
                op(dve.tensor_scalar(tok[0:c, RQ, ci, :], bank[7][0:c, 8 * ci:8 * ci + 4], EPS, None, ALU.add))
                op(dve.tensor_scalar(tok[0:c, RK, ci, :], bank[7][0:c, 8 * ci + 4:8 * ci + 8], EPS, None, ALU.add),
                   "qk2")
            A.wait(dve, "rqk")
            op(dve.reciprocal(tok[:, RQ], tok[:, RQ]))
            chain(dve.reciprocal(tok[:, RK], tok[:, RK]))
            chain(dve.tensor_scalar(tok[:, RQ], tok[:, RQ], float(DH) ** -0.5, None, ALU.mult))
            A.wait(dve, "cum")
            op(tt(tok[:, EQ], tok[:, EG], tok[:, RQ], ALU.mult))
            chain(tt(tok[:, BEG], tok[:, EG], tok[:, BETA], ALU.mult))
            T.wait(dve, "tails")
            chain(dve.tensor_copy(RA3[:], bank[7][0:CC - 1 + TS, :]), "tails")

            for ci, (c0, c) in enumerate(CHUNKS):
                s_ = ci == SAMPLE

                def src(n, width=c, heads=HEADS, rows_=c):
                    T.wait(dve, n, ci)
                    return gbank(n, ci)[0:rows_, 0:heads * width].rearrange("p (h n) -> p h n", h=heads)

                def mask(m):
                    return m[0:c, 0:c].unsqueeze(1).to_broadcast([c, HEADS, c])

                def sq_(m):
                    return m[0:c, :, 0:c]

                chain(tt(KH[0:c], src("k", P), rows(RK, c, ci, P), ALU.mult), "k", ci)
                op(tt(KE[0:c], KH[0:c], rows(EL, c, ci, P), ALU.mult), "KE", ci)
                op(tt(RA[0:c, :, 1, :], KH[0:c], rows(BEG, c, ci, P), ALU.mult))
                op(tt(RA[0:c, :, 0, :], src("v", P), rows(BETA, c, ci, P), ALU.mult), "v", ci)
                V.counts["RA", ci] = V.n
                chain(tt(sq_(M[7]), src("gb"), rows(GC, c, ci, c), ALU.subtract), "gb", ci)
                op(tt(sq_(M[6]), sq_(M[7]), mask(pos_s if s_ else pos), ALU.add))
                op(tt(sq_(M[5]), sq_(M[7]), mask(neg_s if s_ else neg), ALU.add), "arg", ci)
                A.wait(dve, "exp", ci)
                if ci == 0:
                    G.wait(dve, "tails_out")
                L = M[3] if c == P else M[0]
                chain(tt(sq_(L), src("kk"), sq_(M[6]), ALU.mult), "kk", ci)
                chain(tt(sq_(L), sq_(L), rows(BETA, c, ci, c), ALU.mult), "Ld", ci)
                if c == P:
                    chain(tt(sq_(M[0]), sq_(L), mask(diag16), ALU.mult), "Ld", ci)
                    op(tt(sq_(M[7]), sq_(L), sq_(M[0]), ALU.subtract), "Lo", ci)
                op(tt(AT[0:c, :, 0:c], src("kq"), sq_(M[5]), ALU.mult), "kq", ci)
                A.wait(dve, "ldT", ci)
                chain(tt(sq_(M[4]), mask(ident), sq_(M[1]), ALU.subtract), "t0", ci)
                op(dve.tensor_copy(sq_(M[3]), src("pt2")), "pt2", ci)

                def add(n, dst, a, *sl):
                    chain(tt(dst, a, sl[0], ALU.add), n, ci)

                chain(tt(sq_(M[4]), sq_(M[4]), src("t1"), ALU.add), "t1", ci)
                if not s_:
                    op(dve.tensor_copy(sq_(M[6]), src("pt4")), "pt4", ci)
                    chain(tt(sq_(M[4]), sq_(M[4]), src("t2"), ALU.add), "t2", ci)
                    chain(tt(sq_(M[4]), sq_(M[4]), src("t3"), ALU.add), "t3", ci)
                if c == P:
                    op(dve.tensor_copy(sq_(M[1]), src("nt")), "nt", ci)
                    op(dve.tensor_copy(sq_(M[5]), src("nt2")), "nt2", ci)

                def two(t, i):
                    return t[0:c, 2 * i:2 * i + 2].rearrange("p h x d -> p h (x d)")

                op(dve.tensor_copy(two(RB, 1), src("r0b", 256, 2)), "r0b", ci)
                R = RB
                if c == P:
                    A.wait(dve, "r0a", ci)
                    for n, x, y, f in (("r1", RB, RA, ALU.add), ("r2", RA, RB, ALU.add), ("r3", RB, RA, ALU.subtract)):
                        V.now(dve)
                        for i, ab in enumerate("ab"):
                            op(tt(two(y, i), two(x, i), src(n + ab, 256, 2), f), n + ab, ci)
                    R = RA
                if s_:
                    T.wait(dve, "swh", HEADS - 1)
                    sv = gbank("sw", ci)[:, 0:256].rearrange("p (g x) -> p g x", x=2 * STEPS)
                    for i in range(2):
                        op(dve.tensor_copy(M[2][:, i, :].rearrange("p (g x) -> p g x", x=STEPS),
                                           sv[:, :, STEPS * i:STEPS * (i + 1)]), "sw", ci)
                V.now(dve)
                if c != P:
                    A.wait(dve, "r0a", ci)
                chain(tt(VN[0:c], R[0:c, :, 0, :], src("ws", P), ALU.subtract), "ws", ci)
                O = ostore(ci)
                op(tt(O, src("qs", P), rows(EQ, c, ci, P), ALU.mult), "qs", ci)
                chain(tt(M[3][0:c], src("o1", P), rows(RQ, c, ci, P), ALU.mult), "o1", ci)
                chain(tt(O, O, M[3][0:c], ALU.add))
                chain(tt(M[3][0:c], O, O, ALU.mult))
                op(dve.tensor_reduce(tok[0:c, OSS, ci, :], M[3][0:c], AX.X, ALU.add), "oss", ci)
                if not s_:
                    chain(tt(state[:], state[:], rows(EGL, P, ci, P), ALU.mult))
                    chain(tt(state[:], state[:], src("su", P, HEADS, P), ALU.add), "su", ci)
                else:
                    for hh in range(HEADS):
                        if hh:
                            T.wait(dve, f"su{hh - 1}1", ci)
                        op(tt(KTM[:].rearrange("p (b d) -> p b d", b=NSEQ),
                              KE[0:c, hh, :].unsqueeze(1).to_broadcast([c, NSEQ, DH]),
                              seq_of[:].unsqueeze(2).to_broadcast([c, NSEQ, DH]), ALU.mult), f"ktm{hh}", ci)
                        dve.wait_ge(ss_in[hh % 2], 16 * (hh // 2 + 3))
                        S_ = SS[hh % 2]
                        chain(tt(S_[:], S_[:], gls[:, :, hh:hh + 1].to_broadcast([P, NSEQ, DH]), ALU.mult))
                        for i in range(2):
                            op(tt(S_[:, 4 * i:4 * i + 4], S_[:, 4 * i:4 * i + 4], src(f"su{hh}{i}", P, 4, P), ALU.add),
                               f"su{hh}{i}", ci)
                        V.counts["ss", hh] = V.n

            V.now(dve)
            op(dve.tensor_scalar(tok[:, OSS], tok[:, OSS], 1.0 / DH, EPS, ALU.mult, ALU.add), "oss")
            A.wait(dve, "oss")
            chain(dve.reciprocal(tok[:, OSS], tok[:, OSS]))

            def mixlow(ci):
                c0, c = CHUNKS[ci]
                A.wait(dve, "mixhigh", ci)
                op(tt(xT[:, 1, 0:HEADS, c0:c0 + c], mixf[ci % 2][:, :, 0:c],
                      xT[:, 0, 0:HEADS, c0:c0 + c].bitcast(F32), ALU.subtract), "mixlow", ci)

            for ci, (c0, c) in enumerate(CHUNKS):
                if ci >= 2:
                    T.wait(dve, "on", ci - 2)
                op(tt(ONB[ci % 2][0:c], ostore(ci), rows(OSS, c, ci, P), ALU.mult), "on", ci)
                T.wait(dve, "on", ci)
                op(dve.scalar_tensor_tensor(mixf[ci % 2][:, :, 0:c],
                                            bank[4 + ci % 2][:, 0:HEADS * c].rearrange("p (h n) -> p h n", h=HEADS),
                                            cols[:, 60:61], zT[:, :, c0:c0 + c], ALU.mult, ALU.mult), "mix", ci)
                if ci:
                    mixlow(ci - 1)
            mixlow(len(CHUNKS) - 1)
            for t in range(NTB):
                A.wait(dve, "cn", t)
                chain(dve.bn_stats(lnst[:, t, 0:6], CN[:, t, :]))
                chain(dve.bn_aggr(lnst[:, t, 6:8], lnst[:, t, 0:6]))
            op(dve.tensor_scalar(lnst[:, :, 8:9], lnst[:, :, 7:8], EPS, None, ALU.add), "cvar")
            A.wait(dve, "cvar")
            chain(dve.reciprocal(lnst[:, :, 9:10], lnst[:, :, 8:9]))
            for t in range(NTB):
                op(dve.tensor_scalar(CN[:, t, :], CN[:, t, :], lnst[:, t, 6:7], lnst[:, t, 9:10], ALU.subtract,
                                     ALU.mult), "ln", t)
            for t in range(NTB):
                A.wait(dve, "chigh", t)
                o_ = (slice(None), slice(HEADS, KT), slice(t * TB, (t + 1) * TB))
                op(tt(xT[:, 1][o_], mixf[t % 2][:, :, 0:TB], xT[:, 0][o_].bitcast(F32), ALU.subtract), "clow", t)
            V.counts["mixlow", "last"] = V.n
            V.counts["mixer", "last"] = V.n

            for b in range(first["out"], first["query"]):
                i = BLOCKS[b][1]
                if i == 0:
                    dve.wait_ge(h_in[1], 96)
                for t in range(NTB):
                    T.wait(dve, "unit", UNIT0[b] + t)
                    x = h[:, t, i * WB:(i + 1) * WB]
                    op(tt(x, x, bank[(UNIT0[b] + t) % 4][0:TB, 0:WB], ALU.add), "unit", UNIT0[b] + t)
                    V.counts["h2", t] = V.n
                low(b + 2)
            V.counts["h2", "last"] = V.n
            norm(2)
            for b in range(first["query"], nb - 2):
                low(b + 2)

            for t in range(NTB):
                A.wait(dve, "score", 2 * PH - 1)
                S_ = scores[:, t]

                def top(best_, besti_, v, n):
                    for c in range(n):
                        op(dve.max(best_(c)[:, 0:8], v(c)))
                    V.now(dve)
                    for c in range(n):
                        op(dve.max_index(besti_(c)[:, 0:8], best_(c)[:, 0:8], v(c)))
                    V.now(dve)
                    for c in range(n):
                        op(dve.match_replace(v(c), best_(c)[:, 0:8], v(c), LOWEST))
                    V.now(dve)
                    for c in range(n):
                        op(dve.max(best_(c)[:, 8:16], v(c)))
                    V.now(dve)
                    for c in range(n):
                        op(dve.max_index(besti_(c)[:, 8:16], best_(c)[:, 8:16], v(c)))
                    V.now(dve)

                top(lambda c: best[:, c], lambda c: besti[:, c], lambda c: S_[:, c, :], 2 * PH)
                op(dve.tensor_copy(bestf[:], besti[:]))
                bv = best[:].rearrange("p (h x) a -> p h x a", x=2)
                fv = bestf[:].rearrange("p (h x) a -> p h x a", x=2)
                sh = [TB, PH, TOPK, TOPK]
                chain(tt(cand[:], bv[:, :, 0, :].unsqueeze(3).to_broadcast(sh),
                         bv[:, :, 1, :].unsqueeze(2).to_broadcast(sh), ALU.add))
                if t:
                    T.wait(dve, "pairT", t - 1)
                top(lambda c: top16[:, 16 * c:16 * c + 16], lambda c: topi[:, 16 * c:16 * c + 16],
                    lambda c: cand[:, c].rearrange("p a b -> p (a b)"), PH)
                hr = top16[:].rearrange("p (h r) -> p h r", h=PH)
                op(dve.tensor_copy(gsum[:, PH:], hr[:, :, 0]))
                V.now(dve)
                op(tt(hr, hr, gsum[:, PH:].unsqueeze(2).to_broadcast([TB, PH, TOPK]), ALU.subtract), "top", t)
                op(dve.tensor_scalar(topa[:, 0], topi[:], 4, None, ALU.logical_shift_right))
                chain(dve.tensor_scalar(topa[:, 1], topi[:], 15, None, ALU.bitwise_and))
                chain(dve.tensor_copy(topf[:], topa[:]))
                for x in range(2):
                    chain(tt(eqa[:], iota[0:TB, 0:TOPK].unsqueeze(1).to_broadcast([TB, PAIRS, TOPK]),
                             topf[:, x, :].unsqueeze(2).to_broadcast([TB, PAIRS, TOPK]), ALU.is_equal))
                    chain(tt(sel[:].rearrange("p (h r) a -> p h r a", h=PH),
                             eqa[:].rearrange("p (h r) a -> p h r a", h=PH),
                             fv[:, :, x, :].unsqueeze(2).to_broadcast(sh), ALU.mult))
                    chain(dve.tensor_reduce(pick[:, x, :], sel[:], AX.X, ALU.add))
                A.wait(dve, "gexp", t)
                chain(dve.tensor_reduce(gsum[:, 0:PH], hr, AX.X, ALU.add))
                chain(dve.reciprocal(gsum[:, 0:PH], gsum[:, 0:PH]))
                op(tt(pick[:, 2, :].rearrange("p (h r) -> p h r", h=PH), hr,
                      gsum[:, 0:PH].unsqueeze(2).to_broadcast([TB, PH, TOPK]), ALU.mult), "gates", t)
                T.wait(dve, "pairT", t)
                chain(dve.tensor_copy(pairT[:, 0:3, t * TB:(t + 1) * TB],
                                      bank[t % 2][:, 0:3 * TB].rearrange("p (x n) -> p x n", x=3)), "pairT", t)
            chain(dve.tensor_copy(ghi[:], pairT[:, 2, :]))
            chain(tt(pairT[:, 3, :], pairT[:, 2, :], ghi[:].bitcast(F32), ALU.subtract))

            grant(dve, gate_mm, 2)
            with dve.Fori(0, NGB // 2, 1) as i:
                for n in range(GB // 2):
                    dve.wait_ge(gate_mm, i * (GB // 2) + (n + 1))
                    for k in range(4):
                        s1 = (n % 2) * 4 + k
                        col = i * (2 * GB) + (4 * n + k)
                        dve.tensor_scalar(is1[:, s1, :], iota[:], pairT[:, 0, bass.ds(col, 1)], None, ALU.is_equal)
                        for x, part in enumerate((ghi[:].bitcast(F32), pairT[:, 3, :])):
                            last = dve.tensor_scalar(is2[:, s1, x, :], iota[:], pairT[:, 1, bass.ds(col, 1)],
                                                     part[:, bass.ds(col, 1)], ALU.is_equal, ALU.mult)
                    last.then_inc(is_ready, 1)

            def split_u(g, j):
                e = GE * g + j
                for k in range(2):
                    dve.wait_ge(ut_high, 2 * e + (k + 1))
                    tt(UT[:, j % 2, 1, 4 * k:4 * k + 4, :], bank[k][:, :].rearrange("p (k n) -> p k n", k=4),
                       UT[:, j % 2, 0, 4 * k:4 * k + 4, :].bitcast(F32), ALU.subtract).then_inc(ut_low, 1)

            def first_part(g, final=False):
                for j in range(GE):
                    e = GE * g + j
                    nxt = (g, j + 1) if j + 1 < GE else (g + 1, 0)
                    if not (final and j + 1 == GE):
                        split_u(*nxt)
                    if j == 0:
                        dve.wait_ge(g_in[par(g)], 16 * (half_of(g) + 1))
                    dve.wait_ge(gelu_done, 2 * e + 4)
                    tt(prod[:, j % 2, :].rearrange("p (b n) -> p b n", b=NGB),
                       actv[:, j % 2, :].rearrange("p (b n) -> p b n", b=NGB),
                       Gt[:, par(g), :, j * GB:(j + 1) * GB], ALU.mult).then_inc(a_mul, 1)
                    dve.wait_ge(a_high, e + 1)
                    tt(AR[:, par(g), 1, j, :], prod[:, j % 2, :], AR[:, par(g), 0, j, :].bitcast(F32),
                       ALU.subtract).then_inc(a_low, 1)

            def split_v(g):
                dve.wait_ge(v_high, 1 * g + 1)
                tt(VR[:, 1], Vraw[:, par(g)], VR[:, 0].bitcast(F32), ALU.subtract).then_inc(v_low, 1)

            def sums(g):
                for u in range(2 * KT):
                    dt, half = u // 2, u % 2
                    y = yT[:, dt, half * HALF:(half + 1) * HALF]
                    dve.wait_ge(y_mm, 2 * KT * g + (2 * KT + u + 1))
                    tt(y, y, bank[4 + u % 4][:, 0:HALF], ALU.add).then_inc(y_add, 1)

            grant(dve, ut_low, 2)
            grant(dve, a_mul, 2)
            grant(dve, y_add, 4)
            dve.wait_ge(gblk_out[0], 16 * (NGB // 2 + 1))
            dve.wait_ge(gblk_out[1], 16 * (NGB // 2 + 1))
            chain(dve.memset(yT[:], 0.0))
            split_u(Grp(0), 0)
            first_part(Grp(0))
            with dve.Fori(0, NGRP // 2 - 1, 1) as i:
                for k in range(2):
                    split_v(Grp(k, i))
                    first_part(Grp(k + 1, i))
                    sums(Grp(k, i))
            split_v(Grp(NGRP - 2))
            first_part(Grp(NGRP - 1), True)
            sums(Grp(NGRP - 2))
            split_v(Grp(NGRP - 1))
            sums(Grp(NGRP - 1))
            dve.wait_ge(y_add, 2 * KT * NGRP + 4)
            chain(dve.memset(fs[:, 23:24], 0.0), "y_all")

            dve.wait_ge(hf_in, 16)
            for t in range(NTB):
                for i in range(2):
                    T.wait(dve, "y", t, i)
                    x = hf[:, t, 512 * i:512 * i + 512]
                    op(tt(x, x, bank[2 * (t % 2) + i][0:TB, :], ALU.add), "hf", t, i)
            A.wait(dve, "ss", 3, NTB - 1)
            op(dve.tensor_scalar(fs[:, 8:8 + NTB], fs[:, 0:NTB], 1.0 / D, EPS, ALU.mult, ALU.add), "ms", 3)
            A.wait(dve, "rt", 3)
            chain(dve.reciprocal(fs[:, 8:8 + NTB], fs[:, 16:16 + NTB]))
            dve.wait_ge(row_in[2], 16)
            for t in range(NTB):
                if t >= 2:
                    dve.wait_ge(y_out[t % 2], 16 * (t // 2))
                op(dve.scalar_tensor_tensor(yo[:, t % 2, :], hf[:, t, :], fs[:, 8 + t:9 + t], wrow[:],
                                            ALU.mult, ALU.mult), "yo", t)


INPUTS = ["x_prompt", "x_sample", "state_gdn", "state_qkv_conv", "state_conf_conv", "meta_tokens", "norm_mix_w",
          "w_in", "conv_qkv_w", "a_log", "dt_bias", "gdn_norm_w", "conf_dw_w", "conf_dw_b", "conf_ln_w",
          "conf_ln_b", "w_out", "norm_ffn_w", "w_query", "sub_keys", "expert_u", "expert_v", "final_norm_w"]
OUTPUTS = [(1, SEQ, D), (NSEQ, STEPS, D), (1, 1, HEADS, DH, DH), (1, 1, QC - 1, QKV), (1, 1, CC - 1, CW),
           (1, NSEQ, HEADS, DH, DH), (1, NSEQ, QC - 1, QKV), (1, NSEQ, CC - 1, CW)]


def kernel(**inputs):
    from concourse import bacc
    from concourse.bass_utils import run_bass_kernel_spmd

    counts = {}
    for _ in range(2):
        nc = bacc.Bacc("TRN2", target_bir_lowering=False, num_devices=1)
        arrays, ins = {}, []
        for name in INPUTS:
            a = np.ascontiguousarray(inputs[name])
            arrays[f"in_{name}"] = a
            ins.append(nc.dram_tensor(f"in_{name}", a.shape, F32, kind="ExternalInput").ap())
        outs = [nc.dram_tensor(f"out_{i}", shape, F32, kind="ExternalOutput").ap()
                for i, shape in enumerate(OUTPUTS)]
        build(nc, ins, outs, counts)
    r = run_bass_kernel_spmd(nc, [arrays], core_ids=[0])
    return tuple(r.results[0][f"out_{i}"] for i in range(len(OUTPUTS)))
```

```python
from contextlib import ExitStack

import numpy as np

import concourse.bass as bass
from concourse import mybir

F32 = mybir.dt.float32
F32R = mybir.dt.float32r
U32 = mybir.dt.uint32
ALU = mybir.AluOpType
ACT = mybir.ActivationFunctionType
AX = mybir.AxisListType

P = 128
D = 1024
KT = D // P
META, SEQ, NSEQ, STEPS = 16, 512, 8, 4
TP = META + SEQ
TS = NSEQ * STEPS
NT = TP + TS
TB = 112
NTB = NT // TB
HALF = NT // 2
HEADS, DH = 4, 128
QC, CC = 4, 31
QKV, GW, CW = 1536, 512, 512
NQ, NG = QKV // P, CW // P
INW = QKV + GW + 2 * HEADS + 2 * CW
QEXT = (QC - 1) + TP
QSEG = (QC - 1) + STEPS
CEXT = (CC - 1) + TP
CSEG = (CC - 1) + STEPS
PH, KD, NK, TOPK = 8, 128, 128, 16
NE = NK * NK
PAIRS = PH * TOPK
EPS = 1e-6
BIG = 1e30
LOWEST = -3.0e38
CHUNKS = [(0, 128), (128, 128), (256, 128), (384, 128), (512, 16), (TP, TS)]
SAMPLE = len(CHUNKS) - 1
WB = 256
GE = 2
NGRP = NK // GE
GB = 56
NGB = NT // GB
NG1, TURN2 = 18, 6
NGA = NG1 + TURN2 * (NGB // 2)
ISG = 4
NGF = NGRP - NGA
assert NT == NTB * TB and NT == NGB * GB and NG1 % 2 == 0 and TURN2 % 2 == 0 and NGF % 2 == 0


class Steps:

    def __init__(self, sem, counts):
        self.sem, self.counts, self.n = sem, counts, 0

    def op(self, ins, *name):
        ins.then_inc(self.sem, 1)
        self.n += 1
        if name:
            self.counts[name] = self.n
        return ins

    def now(self, eng):
        if self.n:
            eng.wait_ge(self.sem, self.n)

    def wait(self, eng, *name):
        eng.wait_ge(self.sem, self.counts.get(name, 1))


def linear_blocks():
    z0, ab0 = QKV, QKV + GW
    v0 = ab0 + 2 * HEADS
    blocks = [("ab", 0, [("in", ab0, P)])]
    blocks += [("qkv", i, [("in", WB * i, WB)]) for i in range(QKV // WB)]
    glu = [("glu", c, [("in", v0 + P * c, P), ("in", v0 + CW + P * c, P)]) for c in range(NG)]
    z = [("z", i, [("in", z0 + WB * i, WB)]) for i in range(GW // WB)]
    blocks += [glu[0], z[0], glu[1], z[1], glu[2], glu[3]]
    blocks += [("out", i, [("out", WB * i, WB)]) for i in range(D // WB)]
    blocks += [("query", i, [("query", WB * i, WB)]) for i in range(2 * PH * KD // WB)]
    return blocks


BLOCKS = linear_blocks()
UNIT0 = [0]
for _kind, _, _parts in BLOCKS:
    UNIT0.append(UNIT0[-1] + (NTB if _kind == "out" else 2 * sum(n for _, _, n in _parts) // P))


def build(nc, ins, outs, counts):
    (x_prompt, x_sample, state_gdn, state_qkv, state_conf, meta, norm_mix_w, w_in, conv_qkv_w, a_log,
     dt_bias, gdn_norm_w, conf_dw_w, conf_dw_b, conf_ln_w, conf_ln_b, w_out, norm_ffn_w, w_query,
     sub_keys, expert_u, expert_v, final_norm_w) = ins
    (y_prompt, y_sample, gdn_prompt, qkv_prompt, conf_prompt, gdn_sample, qkv_sample, conf_sample) = outs
    WEIGHTS = {"in": w_in[0].rearrange("(k p) n -> p k n", p=P),
               "out": w_out[0].rearrange("(k p) n -> p k n", p=P),
               "query": w_query[0].rearrange("(k p) n -> p k n", p=P)}

    h2_dram = nc.dram_tensor("h2_dram", (NT, D), F32, kind="Internal").ap()
    gate_dram = nc.dram_tensor("gate_dram", (NGB, NK, NK, GB), F32, kind="Internal").ap()
    act_dram = nc.dram_tensor("act_dram", (GE * NGA, P, NT), F32, kind="Internal").ap()

    ctx = ExitStack()
    with ctx:
        def at(name, shape, dt, word):
            return nc.alloc_sbuf_tensor_at(name, shape, dt, offset=base + 4 * word)

        base = -(-nc.sbuf_base // 64) * 64
        room = (nc.sbuf_top - base) // 4
        used = {"all": 0}

        def place(name, shape, dt=F32, region="all"):
            words = int(np.prod(shape[1:]))
            words = -(-words // 8) * 8
            t = at(name, shape, dt, used[region])
            used[region] += words
            assert used[region] <= room
            return t

        ident = place("ident", [P, P])
        tri = place("tri", [P, P])
        neg = place("neg", [P, P])
        pos = place("pos", [P, P])
        diag16 = place("diag16", [P, P])
        tri_s = place("tri_s", [TS, TS])
        neg_s = place("neg_s", [TS, TS])
        pos_s = place("pos_s", [TS, TS])
        same_s = place("same_s", [TS, TS])
        seq_of = place("seq_of", [TS, NSEQ])
        ones = place("ones", [P, P])
        iota = place("iota", [P, P])
        cols = place("cols", [P, 61])
        dwcols = place("dwcols", [P, CC * NG])
        wrow = place("wrow", [TB, D])
        xT = place("xT", [P, 2, KT, NT], F32R)
        WR = place("WR", [P, 2, 2, KT, WB], F32R)
        RAW = place("RAW", [P, 4, KT, WB])
        late = used["all"]
        used["x"] = used["m"] = used["t"] = used["g"] = used["e"] = used["n"] = late

        h = place("h", [TB, NTB, D], region="n")
        xn = place("xn", [TB, 2, D], region="n")
        sq = place("sq", [TB, D], region="n")
        ss = place("ss", [TB, 3 * 8], region="n")
        qext = place("qext", [P, 2, QEXT + NSEQ * QSEG], region="m")
        gext = place("gext", [P, CEXT + NSEQ * CSEG], region="m")
        gate = place("gate", [P, NT], region="m")
        qkvT = place("qkvT", [P, NQ, NT], region="m")
        cT = place("cT", [P, NG, NT], region="m")
        zT = place("zT", [P, HEADS, NT], region="m")
        sqT = place("sqT", [P, NQ, NSEQ * (QC - 1)], region="m")
        qtail = place("qtail", [P, NQ, (QC - 1) + TS], region="m")
        ctail = place("ctail", [P, NG, (CC - 1) + TS], region="m")
        abT = place("abT", [2 * HEADS, NT], region="m")
        tok = place("tok", [P, 14, len(CHUNKS), HEADS], region="m")
        state = place("state", [P, HEADS, DH], region="m")
        dtb = place("dtb", [P, 2 * HEADS], region="m")
        spare = place("spare", [1, 8], region="m")
        gdn0 = used["m"]
        used["c"] = gdn0
        crow = place("crow", [61, P], region="c")
        dwrow = place("dwrow", [CC * NG, P], region="c")
        sconf = place("sconf", [120, 2, CW], region="c")
        sqkv = place("sqkv", [NSEQ * (QC - 1), QKV], region="c")
        scT = place("scT", [P, NG, NSEQ * (CC - 1)], region="c")
        used["d"] = gdn0
        KH = place("KH", [P, HEADS, DH], region="d")
        KHT = place("KHT", [P, HEADS, P], region="d")
        KE = place("KE", [P, HEADS, DH], region="d")
        RA = place("RA", [P, HEADS, 2, DH], region="d")
        RB = place("RB", [P, HEADS, 2, DH], region="d")
        m0 = used["d"]
        M = [place(f"M{i}", [P, HEADS, P], region="d") for i in range(8)]
        AT = place("AT", [P, HEADS, P], region="d")
        VN = place("VN", [P, HEADS, DH], region="d")
        OS = at("OS", [P, 2, HEADS, DH], F32, late)
        pairT = place("pairT", [P, 4, NT], region="t")
        used["g"] = used["t"]
        ghi = place("ghi", [P, NT], F32R, region="t")
        used["g"] = used["t"]
        used["k"] = used["t"]
        eqa = place("eqa", [TB, PAIRS, TOPK], region="k")
        qT = place("qT", [P, 2, NT], region="t")
        keysT = place("keysT", [P, 2 * PH, NK], region="t")
        scores = place("scores", [TB, NTB, 2 * PH, NK], region="t")
        best = place("best", [TB, 2 * PH, TOPK], region="t")
        besti = place("besti", [TB, 2 * PH, TOPK], U32, region="t")
        bestf = place("bestf", [TB, 2 * PH, TOPK], region="t")
        cand = place("cand", [TB, PH, TOPK, TOPK], region="t")
        sel = place("sel", [TB, PAIRS, TOPK], region="t")
        topi = place("topi", [TB, PAIRS], U32, region="t")
        topa = place("topa", [TB, 2, PAIRS], U32, region="t")
        topf = place("topf", [TB, 2, PAIRS], region="t")
        pick = place("pick", [TB, NTB, 3, PAIRS], region="t")
        gsum = place("gsum", [TB, NTB, PH], region="t")
        gmax = place("gmax", [TB, PH], region="t")
        assert used["t"] <= room - 2 * NT
        is1 = place("is1", [P, 4 * ISG, NK], F32R, region="g")
        is2 = place("is2", [P, 4 * ISG, 2, NK], F32R, region="g")
        assert used["g"] <= room - 2 * NT - 2 * GB * NK
        gblk = place("gblk", [P, 2, NK, GB], region="g")
        SS = [at(f"SS{i}", [P, NSEQ, DH], F32, m0 + 512 * (0, 5)[i]) for i in range(2)]
        WQ = at("WQ", [P, HEADS, NSEQ, 2 * STEPS], F32, m0 + 512 * 3)
        CN = at("CN", [TB, NTB, CW], F32, m0)
        gls = at("gls", [P, NSEQ, HEADS], F32, late + 1024)
        gm = at("gm", [TS, NSEQ, HEADS], F32, late + 1056)
        lnst = at("lnst", [TB, NTB, 6 + 2 + 2], F32, late + 1088)
        sqb = [at(f"sqb{i}", [P, NT], F32, m0 - 1024 * (2 - i)) for i in range(2)]
        RA2 = at("RA2", [P, 3 * CW], F32, m0 - 1024)
        KTM = at("KTM", [TS, NSEQ * DH], F32, m0 - 2048)
        RA3 = at("RA3", [CC - 1 + TS, CW], F32, late + 1176 + 832)
        ONB = [at(f"ONB{i}", [P, HEADS, DH], F32, m0 - 2048 + 512 * i) for i in range(2)]
        mixf = [at(f"mixf{i}", [P, HEADS, P], F32, m0 - 1024 + 512 * i) for i in range(2)]
        keysrow = at("keysrow", [P, 2 * PH, KD], F32, used["n"])
        raws = used["all"] - 4 * KT * WB
        Uraw = at("Uraw", [P, 2, GE, D], F32, raws)
        Vraw = at("Vraw", [P, 2, GE, D], F32, raws + 2 * GE * D)
        wrs = raws - 4 * KT * WB
        Ucopy = at("Ucopy", [P, 2, D], F32, raws + 2 * GE * D)
        actA = at("actA", [P, 2, NT], F32, room - 2 * NT)
        actC = at("actC", [P, 2, GE, NT], F32, raws)
        UT = at("UT", [P, 2, 2, KT, P], F32R, wrs)
        VR1 = at("VR1", [P, 2, GE, D], F32R, wrs + 4 * KT * P)
        VR0 = at("VR0", [P, 2, GE, D], F32R, wrs)
        AR = place("AR", [P, 2, 2, GE, NT], F32R, region="e")
        Gt = place("Gt", [P, 2, NGB, GE * GB], region="e")
        actv = place("actv", [P, 2, NT], region="e")
        prod = place("prod", [P, 2, NT], region="e")
        yT = place("yT", [P, KT, NT], region="e")
        hf = place("hf", [TB, NTB, D], region="e")
        yo = place("yo", [TB, 2, D], region="e")
        fs = place("fs", [TB, 24], region="e")

        bank = [ctx.enter_context(nc.psum_tensor(f"bank{i}", [P, 512], F32)) for i in range(8)]

        def sem(name):
            return ctx.enter_context(nc.semaphore(name))

        V = Steps(sem("vector_done"), counts.setdefault("V", {}))
        A = Steps(sem("scalar_done"), counts.setdefault("A", {}))
        T = Steps(sem("tensor_done"), counts.setdefault("T", {}))
        G = Steps(sem("gpsimd_done"), counts.setdefault("G", {}))
        h_in = [sem(f"h_in{i}") for i in range(2)]
        row_in = [sem(f"row_in{i}") for i in range(3)]
        small_in = sem("small_in")
        raw_in = [sem(f"raw_in{i}") for i in range(4)]
        gate_mm = sem("gate_mm")
        gate_bank = sem("gate_bank")
        is_ready = sem("is_ready")
        gblk_out = [sem(f"gblk_out{i}") for i in range(2)]
        u_in = [sem(f"u_in{i}") for i in range(2)]
        v_in = [sem(f"v_in{i}") for i in range(2)]
        g_in = [sem(f"g_in{i}") for i in range(2)]
        ut_mm, ut_high, ut_low = sem("ut_mm"), sem("ut_high"), sem("ut_low")
        u_copy = sem("u_copy")
        act_out = [sem(f"act_out{i}") for i in range(2)]
        act_in = [sem(f"act_in{i}") for i in range(2)]
        s_mm, gelu_done, a_mul = sem("s_mm"), sem("gelu_done"), sem("a_mul")
        a_high, a_low = sem("a_high"), sem("a_low")
        v_high, v_low = sem("v_high"), sem("v_low")
        y_mm, y_add = sem("y_mm"), sem("y_add")
        hf_in = sem("hf_in")
        y_out = [sem(f"y_out{i}") for i in range(2)]
        out_done = sem("out_done")
        h2_done = sem("h2_done")
        ss_in = [sem(f"ss_in{i}") for i in range(2)]
        ss_out = [sem(f"ss_out{i}") for i in range(2)]

        nb = len(BLOCKS)
        first = {k: next(b for b in range(nb) if BLOCKS[b][0] == k) for k in ("ab", "out", "query")}
        raw_count = []
        for b in range(nb):
            raw_count.append(len(BLOCKS[b][2]) + (raw_count[b - 4] if b >= 4 else 0))

        def groups(ci):
            c = CHUNKS[ci][1]
            g = [("k", V), ("v", V), ("gb", V), ("khT", A), ("kk", V), ("kq", V), ("ldT", A),
                 ("p2", A), ("pt2", V), ("t1", V)]
            if ci != SAMPLE:
                g += [("p4", A), ("pt4", V), ("t2", V), ("p8", A), ("t3", V)]
            if c == P:
                g += [("n", A), ("nt", V), ("n2", A), ("nt2", V), ("nt4", A)]
            g += [("r0a", A), ("r0b", V)]
            if c == P:
                g += [("r1a", V), ("r1b", V), ("r2a", V), ("r2b", V), ("r3a", V), ("r3b", V)]
            g += [("wT", A)]
            if ci == SAMPLE:
                g += [("sw", V)]
            g += [("ws", V), ("qs", V), ("o1", V)]
            if ci == SAMPLE:
                g += [(f"su{h}{i}", V) for h in range(HEADS) for i in range(2)]
            else:
                g += [("su", V)]
            return g

        GROUPS = [(n, ci, e) for ci in range(len(CHUNKS)) for n, e in groups(ci)]
        WHERE = {(n, ci): i for i, (n, ci, _) in enumerate(GROUPS)}

        def gbank(n, ci):
            return bank[4 + WHERE[n, ci] % 4]

        def grant(eng, s_, n):
            eng.sem_inc(s_, n)

        class Grp:

            def __init__(self, k, turn=None, step=2):
                self.k, self.turn, self.step = k, turn, step

            def __add__(self, n):
                return Grp(self.k + n, self.turn, self.step)

            def __rmul__(self, m):
                return m * self.k if self.turn is None else self.turn * (self.step * m) + m * self.k

        def gate_slots(k, h):
            at_, halves = 2 * GE * k + h, 2 * GE * TURN2
            return range(GB // 2 * at_ // halves, GB // 2 * (at_ + 1) // halves)

        def par(g):
            return g.k % 2

        def half_of(g):
            return g.k // 2 if g.turn is None else g.turn * (g.step // 2) + g.k // 2

        def vbuf(q):
            return VR0 if q.k >= NGF and par(q) == 0 else VR1

        def unit_read(eng, u):
            b = max(b for b in range(nb) if UNIT0[b] <= u)
            (V if BLOCKS[b][0] == "out" else A).wait(eng, "unit", u)

        def rows(i, c, ci, width):
            return tok[0:c, i, ci, :].unsqueeze(2).to_broadcast([c, HEADS, width])

        def ostore(ci):
            if ci < 4:
                return qkvT[:, 2 * HEADS:3 * HEADS, CHUNKS[ci][0]:CHUNKS[ci][0] + P]
            return OS[0:CHUNKS[ci][1], ci - 4]

        GD, BETA, X2, X3, GC, EG, GL, EL, RQ, RK, BEG, EGL, OSS, EQ = range(14)

        block = ctx.enter_context(nc.Block())

        @block.sync
        def _(sp):
            def load_rows(dst, s):
                sp.dma_start(dst[0:META, 0, :], meta).then_inc(s, 16)
                sp.dma_start(dst[META:TB, 0, :], x_prompt[0, 0:TB - META, :]).then_inc(s, 16)
                sp.dma_start(dst[:, 1:NTB - 1, :],
                             x_prompt[0, TB - META:(NTB - 1) * TB - META, :].rearrange("(t p) d -> p t d", p=TB)
                             ).then_inc(s, 16)
                sp.dma_start(dst[0:TB - TS, NTB - 1, :],
                             x_prompt[0, (NTB - 1) * TB - META:SEQ, :]).then_inc(s, 16)
                sp.dma_start(dst[TB - TS:TB, NTB - 1, :],
                             x_sample.rearrange("b s d -> (b s) d")).then_inc(s, 16)

            def load_row(w, s):
                sp.dma_start(wrow[:], w.to_broadcast([TB, D])).then_inc(s, 16)

            load_rows(h, h_in[0])
            load_row(norm_mix_w, row_in[0])
            for b in range(nb):
                if b >= 4:
                    V.wait(sp, "low", b - 4)
                at_ = 0
                for name, c0, n in BLOCKS[b][2]:
                    sp.dma_start(RAW[:, b % 4, :, at_:at_ + n], WEIGHTS[name][:, :, c0:c0 + n]
                                 ).then_inc(raw_in[b % 4], 16)
                    at_ += n
                if b == first["out"] + 3:
                    V.wait(sp, "mixlow", "last")
                    T.wait(sp, "mixer", "last")
                    A.wait(sp, "mixer", "last")
                    V.wait(sp, "mixer", "last")
                    G.wait(sp, "mixer", "last")
                    load_rows(h, h_in[1])
                    sp.dma_start(keysrow[:], sub_keys[0].rearrange("h p k d -> k (h p) d")).then_inc(h_in[1], 16)
                    load_row(norm_ffn_w, row_in[1])
                if b == first["query"] + 5:
                    V.wait(sp, "h2", "last")
                    sp.dma_start(h2_dram.rearrange("(t p) d -> p t d", p=TB), h[:]).then_inc(h2_done, 16)
            V.wait(sp, "xn", 2, NTB - 1)
            load_row(final_norm_w.rearrange("(a d) -> a d", a=1), row_in[2])

            U = expert_u[0].rearrange("(p k) d -> p k d", p=NK)
            Vw = expert_v[0].rearrange("(p k) d -> p k d", p=NK)

            def load(dst, src, g, s_):
                k0 = GE * g
                sp.dma_start(dst, src(bass.ds(k0, GE))).then_inc(s_, 16)

            def load_u(g):
                load(Uraw[:, par(g)], lambda k: U[:, k, :], g, u_in[par(g)])

            def next_u(g):
                sp.wait_ge(ut_mm, 2 * GE * (g + -1))
                load_u(g)

            def store_act(g):
                for j in range(GE):
                    e = GE * g + j
                    sp.wait_ge(gelu_done, 2 * e + 4)
                    sp.dma_start(act_dram[bass.ds(e, 1)].rearrange("a p n -> (a p) n"), actA[:, j, :]
                                 ).then_inc(act_out[j], 16)

            for g in range(2):
                V.wait(sp, "low", nb - 4 + (g - nb) % 4)
                load_u(Grp(g))
            with sp.Fori(0, NG1 // 2, 1) as i:
                for k in range(2):
                    next_u(Grp(k + 2, i))
                    store_act(Grp(k, i))
            with sp.Fori(0, NGB // 2, 1) as i:
                for blk in range(2):
                    for k in range(TURN2 // 2 * blk, TURN2 // 2 * (blk + 1)):
                        next_u(Grp(NG1 + k + 2, i, TURN2))
                        store_act(Grp(NG1 + k, i, TURN2))
                    sp.wait_ge(gate_bank, i * (GB // 2) + ((blk + 1) * (GB // 4) + 4))
                    sp.dma_start(gate_dram[bass.ds(i * 2 + blk, 1)].rearrange("a p k n -> (a p) k n"),
                                 gblk[:, blk]).then_inc(gblk_out[blk], 16)

            def load_v(q, g):
                load(Vraw[:, par(q)], lambda k: Vw[:, k, :], g, v_in[par(q)])

            def load_g(q, g):
                load(Gt[:, par(q)].rearrange("p b (k n) -> p b k n", n=GB),
                     lambda k: gate_dram[:, :, k, :].rearrange("b p k n -> p b k n"), g, g_in[par(q)])

            sp.wait_ge(ut_low, 2 * GE * NGA + 4)
            for q in range(2):
                load_v(Grp(q), Grp(NGA + q))
            for blk in range(2):
                sp.wait_ge(gblk_out[blk], 16 * (NGB // 2 + 1))
            for q in range(2):
                load_g(Grp(q), Grp(NGA + q))
            sp.dma_start(hf[:], h2_dram.rearrange("(t p) d -> p t d", p=TB)).then_inc(hf_in, 16)
            with sp.Fori(0, NGF // 2 - 1, 1) as i:
                for k in range(2):
                    q = Grp(k + 2, i)
                    next_u(q + NGA)
                    sp.wait_ge(a_mul, GE * (q + -1) + 2)
                    load_g(q, q + NGA)
                    sp.wait_ge(v_low, 1 * (q + -1))
                    load_v(q, q + NGA)
            for j in range(GE):
                sp.wait_ge(act_out[j], 16 * (NGA + 1))
            sp.wait_ge(ut_mm, 4 * NGRP)
            with sp.Fori(0, NGA // 2, 1) as i:
                for k in range(2):
                    g = Grp(k, i)
                    q = g + NGF
                    sp.wait_ge(a_mul, GE * (q + -1) + 2)
                    load(actC[:, k], lambda k_: act_dram[k_].rearrange("k p n -> p k n"), g, act_in[k])
                    load_g(q, g)
                    sp.wait_ge(v_low, 1 * (q + -1))
                    load_v(q, g)

            for t in range(NTB):
                V.wait(sp, "yo", t)
                r0 = t * TB - META
                if t == 0:
                    sp.dma_start(y_prompt[0, 0:TB - META, :], yo[META:TB, 0, :]).then_inc(y_out[t % 2], 16)
                elif t < NTB - 1:
                    sp.dma_start(y_prompt[0, r0:r0 + TB, :], yo[:, t % 2, :]).then_inc(y_out[t % 2], 16)
                else:
                    sp.dma_start(y_prompt[0, r0:SEQ, :], yo[0:TB - TS, t % 2, :]).then_inc(y_out[t % 2], 16)
                    sp.dma_start(y_sample.rearrange("b s d -> (b s) d"), yo[TB - TS:TB, t % 2, :]
                                 ).then_inc(y_out[t % 2], 16)
            sp.wait_ge(y_out[0], 16 * 4)
            sp.wait_ge(y_out[1], 16 * 2)

        @block.gpsimd
        def _(pool):
            n = 0
            for dst, src in (
                    (crow[0:48, :], conv_qkv_w[0].rearrange("t (c p) -> (t c) p", p=P)),
                    (crow[48:52, :], conf_dw_b[0].rearrange("(c p) -> c p", p=P)),
                    (crow[52:56, :], conf_ln_w[0].rearrange("(c p) -> c p", p=P)),
                    (crow[56:60, :], conf_ln_b[0].rearrange("(c p) -> c p", p=P)),
                    (crow[60:61, :], gdn_norm_w),
                    (dwrow[:], conf_dw_w[0].rearrange("t (c p) -> (t c) p", p=P)),
                    (sconf[:], state_conf[0].rearrange("(r b) t c -> (b t) r c", r=2)),
                    (sqkv[:], state_qkv[0].rearrange("b t c -> (b t) c")),
                    (dtb[:, 0:HEADS], dt_bias.to_broadcast([P, HEADS])),
                    (dtb[:, HEADS:], a_log.to_broadcast([P, HEADS]))):
                pool.dma_start(dst, src).then_inc(small_in, 16)
                n += 1
            assert n == 10

            def op(ins, *name):
                G.op(ins, *name)
                G.now(pool)

            def keep(m, compare, fill, base_, pattern, cm):
                op(pool.affine_select(out=m, in_=m, compare_op=compare, fill=fill, base=base_,
                                      pattern=pattern, channel_multiplier=cm))

            op(pool.memset(ident[:], 0.0))
            keep(ident[:], ALU.not_equal, 1.0, 0, [[-1, P]], 1)
            op(pool.memset(ones[:], 1.0), "ident")
            op(pool.memset(tri[:], 1.0))
            keep(tri[:], ALU.is_ge, 0.0, 0, [[1, P]], -1)
            op(pool.memset(neg[:], 0.0))
            keep(neg[:], ALU.is_ge, -BIG, 0, [[1, P]], -1)
            op(pool.memset(pos[:], 0.0))
            keep(pos[:], ALU.is_gt, BIG, 0, [[-1, P]], 1)

            def within(m, width, fill, inner):
                n_ = m.shape[1] // (width if inner else 1)
                v = m.rearrange("p (b w) -> p b w", w=width) if inner else m
                tail = [[0, width]] if inner else []
                keep(v, ALU.is_ge, fill, 0, [[-width, n_]] + tail, 1)
                keep(v, ALU.is_ge, fill, width - 1, [[width, n_]] + tail, -1)

            op(pool.memset(diag16[:], 1.0))
            within(diag16[:], 16, 0.0, True)
            op(pool.memset(same_s[:], 1.0))
            within(same_s[:], STEPS, 0.0, True)
            op(pool.memset(seq_of[:], 1.0))
            within(seq_of[:], STEPS, 0.0, False)
            op(pool.tensor_copy(tri_s[:], tri[0:TS, 0:TS]))
            within(tri_s[:], STEPS, 0.0, True)
            op(pool.tensor_copy(neg_s[:], neg[0:TS, 0:TS]))
            within(neg_s[:], STEPS, -BIG, True)
            op(pool.tensor_copy(pos_s[:], pos[0:TS, 0:TS]))
            within(pos_s[:], STEPS, BIG, True)
            op(pool.iota(iota[:], pattern=[[1, P]], base=0, channel_multiplier=0,
                         allow_small_or_imprecise_dtypes=True), "masks")

            T.wait(pool, "xT", 1, NTB - 1, 1)
            V.wait(pool, "xn", 1, NTB - 1)
            op(pool.memset(qext[:, :, 0:QC - 1], 0.0))
            op(pool.memset(gext[:, 0:CC - 1], 0.0))
            op(pool.memset(tok[:], 1.0))
            op(pool.memset(state[:], 0.0), "zeros")

            outs_ = 0
            pool.dma_start(conf_sample[0][:, 0:CC - 1 - STEPS, :], state_conf[0][:, STEPS:CC - 1, :]
                           ).then_inc(out_done, 16)
            A.wait(pool, "tails")
            V.wait(pool, "tails")
            pool.dma_start(qkv_prompt[0, 0], RA2[0:QC - 1, 0:QKV]).then_inc(out_done, 16)
            for s in range(1, STEPS):
                pool.dma_start(qkv_sample[0][:, s - 1, :],
                               RA2[QC - 1 + s:QC - 1 + s + STEPS * (NSEQ - 1) + 1:STEPS, 0:QKV]
                               ).then_inc(out_done, 16)
            pool.dma_start(conf_prompt[0, 0], RA3[0:CC - 1, :]).then_inc(out_done, 16)
            pool.dma_start(conf_sample[0][:, CC - 1 - STEPS:, :], RA3[CC - 1:, :]).then_inc(out_done, 16)
            outs_ += 7
            pool.wait_ge(out_done, 16 * outs_)
            op(pool.memset(spare[0:1, 0:1], 0.0), "tails_out")
            def load_state(n):
                pool.dma_start(SS[n % 2][:], state_gdn[0].rearrange("b h k v -> h k b v")[n % HEADS]
                               ).then_inc(ss_in[n % 2], 16)

            def store_state(hh):
                V.wait(pool, "ss", hh)
                pool.dma_start(gdn_sample[0].rearrange("b h k v -> h k b v")[hh], SS[hh % 2][:]
                               ).then_inc(ss_out[hh % 2], 16)

            A.wait(pool, "wT", SAMPLE)
            V.wait(pool, "r0b", SAMPLE)
            T.wait(pool, "wT", SAMPLE)
            load_state(0)
            load_state(1)
            for n in range(2, HEADS + 2):
                T.wait(pool, "swh", n - 2)
                load_state(n)
            for hh in range(HEADS):
                store_state(hh)
                if hh < 2:
                    pool.wait_ge(ss_out[hh], 16)
                    load_state(HEADS + 2 + hh)
            V.wait(pool, "su", SAMPLE - 1)
            pool.dma_start(gdn_prompt[0, 0].rearrange("h k v -> k h v"), state[:]).then_inc(out_done, 16)
            pool.wait_ge(ss_out[0], 32)
            pool.wait_ge(ss_out[1], 32)
            pool.wait_ge(out_done, 16 * (outs_ + 1))
            op(pool.memset(spare[0:1, 0:1], 0.0), "mixer", "last")

            def low_u(g, j):
                e = GE * g + j
                pool.wait_ge(ut_high, 2 * e + 2)
                pool.wait_ge(u_copy, 2 * e + 4)
                pool.tensor_tensor(UT[:, j, 1].rearrange("p k n -> p (k n)"), Ucopy[:, j, :],
                                   UT[:, j, 0].rearrange("p k n -> p (k n)").bitcast(F32), ALU.subtract
                                   ).then_inc(ut_low, 2)

            grant(pool, ut_low, 2)
            with pool.Fori(0, NGA // 2, 1) as i:
                for k in range(2):
                    for j in range(GE):
                        low_u(Grp(k, i), j)
            low_u(Grp(NGA), 0)

            def low_v(q):
                VR = vbuf(q)
                pool.wait_ge(v_high, 1 * q + 1)
                pool.tensor_tensor(VR[:, 1], Vraw[:, par(q)], VR[:, 0].bitcast(F32), ALU.subtract
                                   ).then_inc(v_low, 1)

            for first_q, n in ((0, NGF), (NGF, NGA)):
                with pool.Fori(0, n // 2, 1) as i:
                    for k in range(2):
                        low_v(Grp(first_q + k, i))

        @block.tensor
        def _(pe):
            mm = pe.matmul

            G.wait(pe, "ident")
            pe.wait_ge(small_in, 160)
            pe.transpose(bank[4][:, 0:61], crow[:], ident[0:61, 0:61])
            T.op(pe.transpose(bank[4][:, 128:128 + CC * NG], dwrow[:], ident[0:CC * NG, 0:CC * NG]), "cols")
            for c in range(NQ):
                last = pe.transpose(bank[5][:, 24 * c:24 * c + 24], sqkv[:, P * c:P * c + P], ident[0:24, 0:24])
            T.op(last, "sqT")
            for c in range(NG):
                for r in range(2):
                    last = pe.transpose(bank[6 + c // 2][:, 240 * (c % 2) + 120 * r:240 * (c % 2) + 120 * r + 120],
                                        sconf[:, r, P * c:P * c + P], ident[0:120, 0:120])
            T.op(last, "scT")

            def norm(k):
                for t in range(NTB):
                    V.wait(pe, "xn", k, t)
                    for i in range(2):
                        if t >= 2:
                            V.wait(pe, "xlow", k, t - 2, i)
                        for j in range(4):
                            last = pe.transpose(bank[2 * (t % 2) + i][:, j * TB:(j + 1) * TB],
                                                xn[:, t % 2, (4 * i + j) * P:(4 * i + j + 1) * P],
                                                ident[0:TB, 0:TB])
                        T.op(last, "xT", k, t, i)

            def linear(b):
                kind, _, parts = BLOCKS[b]
                V.wait(pe, "low", b)
                W = WR[:, b % 2]
                for u in range(UNIT0[b], UNIT0[b + 1]):
                    if u >= 4:
                        unit_read(pe, u - 4)
                    n = u - UNIT0[b]
                    for kt in range(KT):
                        for i, (pw, px) in enumerate(((0, 0), (0, 1), (1, 0))):
                            go = dict(start=(kt == 0 and i == 0), stop=(kt == KT - 1 and i == 2))
                            if kind == "out":
                                last = mm(bank[u % 4][0:TB, 0:WB], xT[:, px, kt, n * TB:(n + 1) * TB],
                                          W[:, pw, kt, :], **go)
                            else:
                                m, half = n // 2, n % 2
                                last = mm(bank[u % 4][:, 0:HALF], W[:, pw, kt, m * P:(m + 1) * P],
                                          xT[:, px, kt, half * HALF:(half + 1) * HALF], **go)
                    T.op(last, "unit", u)

            norm(1)
            V.wait(pe, "xlow", 1, NTB - 1, 1)
            for b in range(first["out"]):
                linear(b)

            unit_read(pe, UNIT0[first["ab"] + 1] - 1)
            V.wait(pe, "scT")
            for ci, (c0, c) in enumerate(CHUNKS):
                last = pe.transpose(bank[4][0:c, 8 * ci:8 * ci + 8], abT[:, c0:c0 + c], ident[0:8, 0:8])
            T.op(last, "ab")
            V.wait(pe, "g")
            V.wait(pe, "gm")
            for ci, (c0, c) in enumerate(CHUNKS):
                s_ = ci == SAMPLE
                mm(bank[5][0:c, 8 * ci:8 * ci + 4], (tri_s if s_ else tri)[0:c, 0:c], tok[0:c, GD, ci, :])
                rows_ = c if s_ else P
                mm(bank[5][0:rows_, 8 * ci + 4:8 * ci + 8], (same_s if s_ else ones)[0:c, 0:rows_],
                   tok[0:c, GD, ci, :])
            T.op(mm(bank[6][:, 0:TS], ones[0:TS, :], gm[:].rearrange("p b h -> p (b h)")), "cum")
            for c_ in range(2 * HEADS):
                A.wait(pe, "qk2", c_)
                for ci, (c0, c) in enumerate(CHUNKS):
                    last = mm(bank[7][0:c, 8 * ci + c_:8 * ci + c_ + 1], sqb[c_ % 2][:, c0:c0 + c], ones[:, 0:1])
                T.op(last, "qk2", c_)
            A.wait(pe, "qtail")
            V.wait(pe, "ctail")
            V.wait(pe, "cum")
            V.wait(pe, "ab")
            V.wait(pe, "qk2")
            for c in range(NQ):
                last = pe.transpose(bank[4 + c // 4][0:QC - 1 + TS, P * (c % 4):P * (c % 4) + P], qtail[:, c, :],
                                    ident[:])
            for c in range(NG):
                last = pe.transpose(bank[7][0:CC - 1 + TS, P * c:P * c + P], ctail[:, c, :], ident[:])
            T.op(last, "tails")

            for ci, (c0, c) in enumerate(CHUNKS):
                s_ = ci == SAMPLE

                def group(n, *needs):
                    i = WHERE[n, ci]
                    if i >= 4:
                        m, cj, e = GROUPS[i - 4]
                        e.wait(pe, m, cj)
                    elif i == 0:
                        A.wait(pe, "tails")
                        V.wait(pe, "tails")
                    for e, m in needs:
                        e.wait(pe, m, ci)
                    return gbank(n, ci)

                def each(n, f, width, *needs, only=range(HEADS)):
                    b_ = group(n, *needs)
                    for i, hh in enumerate(only):
                        last = f(b_, i, hh)
                    T.op(last, n, ci)

                def prod4(n, L, R, *needs):
                    each(n, lambda b_, i, hh: mm(b_[0:c, i * c:(i + 1) * c], L[0:c, hh, 0:c], R[0:c, hh, 0:c]),
                         c, *needs)

                each("k", lambda b_, i, hh: pe.transpose(b_[0:c, i * P:(i + 1) * P],
                                                         qkvT[:, HEADS + hh, c0:c0 + c], ident[:]), P)
                each("v", lambda b_, i, hh: pe.transpose(b_[0:c, i * P:(i + 1) * P],
                                                         qkvT[:, 2 * HEADS + hh, c0:c0 + c], ident[:]), P)
                each("gb", lambda b_, i, hh: mm(b_[0:c, i * c:(i + 1) * c],
                                                tok[0:c, GD, ci, hh:hh + 1].to_broadcast([c, c]),
                                                (tri_s if s_ else tri)[0:c, 0:c]), c)
                each("khT", lambda b_, i, hh: pe.transpose(b_[:, i * c:(i + 1) * c], KH[0:c, hh, :],
                                                           ident[0:c, 0:c]), c, (V, "k"))
                each("kk", lambda b_, i, hh: mm(b_[0:c, i * c:(i + 1) * c], KHT[:, hh, 0:c], KHT[:, hh, 0:c]),
                     c, (A, "khT"))
                each("kq", lambda b_, i, hh: mm(b_[0:c, i * c:(i + 1) * c], KHT[:, hh, 0:c],
                                                qkvT[:, hh, c0:c0 + c]), c)
                each("ldT", lambda b_, i, hh: pe.transpose(b_[0:c, i * c:(i + 1) * c], M[0][0:c, hh, 0:c],
                                                           ident[0:c, 0:c]), c, (V, "Ld"))
                prod4("p2", M[1], M[0], (A, "ldT"))
                prod4("pt2", M[0], M[1])
                prod4("t1", M[2], M[4], (A, "p2"), (V, "t0"))
                if not s_:
                    prod4("p4", M[3], M[2], (V, "pt2"))
                    prod4("pt4", M[2], M[3])
                    prod4("t2", M[5], M[4], (A, "p4"), (V, "t1"))
                    prod4("p8", M[6], M[5], (V, "pt4"))
                    prod4("t3", M[2], M[4], (A, "p8"), (V, "t2"))
                solved = "t1" if s_ else "t3"
                if c == P:
                    prod4("n", M[4], M[7], (V, "t3"), (V, "Lo"))
                    prod4("nt", M[7], M[4])
                    prod4("n2", M[1], M[0], (V, "nt"), (A, "n"))
                    prod4("nt2", M[0], M[1])
                    prod4("nt4", M[3], M[5], (A, "n2"), (V, "nt2"))

                def solve(n, L, R, *needs):
                    for x, only in (("a", (0, 1)), ("b", (2, 3))):
                        each(n + x, lambda b_, i, hh: mm(b_[0:c, i * 256:(i + 1) * 256], L[0:c, hh, 0:c],
                                                         R[0:c, hh].rearrange("p x d -> p (x d)")),
                             0, *needs, only=only)

                solve("r0", M[4], RA, (V, solved), (V, "RA"))
                R = RB
                if c == P:
                    solve("r1", M[6], RB, (A, "nt4"), (A, "r0a"), (V, "r0b"))
                    solve("r2", M[5], RA, (V, "r1b"))
                    solve("r3", M[1], RB, (V, "r2b"))
                    R = RA
                each("wT", lambda b_, i, hh: pe.transpose(b_[:, i * c:(i + 1) * c], R[0:c, hh, 1, :],
                                                          ident[0:c, 0:c]), c,
                     *([(V, "r3b")] if c == P else [(A, "r0a"), (V, "r0b")]))
                if s_:
                    b_ = group("sw", (A, "wT"))
                    for hh in range(HEADS):
                        pe.wait_ge(ss_in[hh % 2], 16 * (hh // 2 + 1))
                        for q in range(NSEQ):
                            last = mm(b_[:, 64 * hh + 8 * q:64 * hh + 8 * q + 8], SS[hh % 2][:, q, :],
                                      WQ[:, hh, q, :])
                        T.op(last, "swh", hh)
                    each("ws", lambda b2, i, hh: pe.transpose(b2[0:c, i * P:(i + 1) * P],
                                                              M[2][:, 0, hh * TS:(hh + 1) * TS], ident[:]),
                         P, (V, "sw"))
                    each("qs", lambda b2, i, hh: pe.transpose(b2[0:c, i * P:(i + 1) * P],
                                                              M[2][:, 1, hh * TS:(hh + 1) * TS], ident[:]), P)
                else:
                    if ci:
                        V.wait(pe, "su", ci - 1)
                    each("ws", lambda b2, i, hh: mm(b2[0:c, i * P:(i + 1) * P], M[2][:, hh, 0:c], state[:, hh, :]),
                         P, (A, "wT"))
                    each("qs", lambda b2, i, hh: mm(b2[0:c, i * P:(i + 1) * P], qkvT[:, hh, c0:c0 + c],
                                                    state[:, hh, :]), P)
                each("o1", lambda b2, i, hh: mm(b2[0:c, i * P:(i + 1) * P], AT[0:c, hh, 0:c], VN[0:c, hh, :]),
                     P, (V, "ws"), (V, "kq"))
                if s_:
                    for hh in range(HEADS):
                        for i in range(2):
                            b_ = group(f"su{hh}{i}", (V, f"ktm{hh}"))
                            for q in range(4):
                                last = mm(b_[:, P * q:P * q + P], KTM[0:c, P * (4 * i + q):P * (4 * i + q) + P],
                                          VN[0:c, hh, :])
                            T.op(last, f"su{hh}{i}", ci)
                else:
                    each("su", lambda b2, i, hh: mm(b2[:, i * P:(i + 1) * P], KE[0:c, hh, :], VN[0:c, hh, :]),
                         P, (V, "KE"))

            for ci, (c0, c) in enumerate(CHUNKS):
                V.wait(pe, "on", ci)
                if ci >= 2:
                    V.wait(pe, "mix", ci - 2)
                for hh in range(HEADS):
                    last = pe.transpose(bank[4 + ci % 2][:, hh * c:(hh + 1) * c], ONB[ci % 2][0:c, hh, :],
                                        ident[0:c, 0:c])
                T.op(last, "on", ci)
            for t in range(NTB):
                V.wait(pe, "cconv", NG - 1)
                if t >= 2:
                    A.wait(pe, "cn", t - 2)
                for c in range(NG):
                    last = pe.transpose(bank[6 + t % 2][0:TB, c * P:(c + 1) * P], cT[:, c, t * TB:(t + 1) * TB],
                                        ident[:])
                T.op(last, "cn", t)
            for t in range(NTB):
                V.wait(pe, "ln", t)
                if t == 0:
                    V.wait(pe, "mix", len(CHUNKS) - 1)
                if t >= 2:
                    A.wait(pe, "csilu", t - 2)
                for c in range(NG):
                    last = pe.transpose(bank[4 + t % 2][:, c * TB:(c + 1) * TB], CN[:, t, c * P:(c + 1) * P],
                                        ident[0:TB, 0:TB])
                T.op(last, "ln", t)
            T.counts["mixer", "last"] = T.n

            V.wait(pe, "mixlow", "last")
            for b in range(first["out"], first["query"]):
                linear(b)
            unit_read(pe, UNIT0[first["query"]] - 1)
            pe.wait_ge(h_in[1], 96)
            for i in range(4):
                for j in range(4):
                    last = pe.transpose(bank[4 + i][:, j * P:(j + 1) * P], keysrow[:, 4 * i + j, :], ident[:])
            T.op(last, "keys")
            norm(2)
            V.wait(pe, "xlow", 2, NTB - 1, 1)

            def score(ct):
                unit_read(pe, UNIT0[first["query"]] + 2 * ct + 1)
                if ct >= 2:
                    A.wait(pe, "score", ct - 2)
                else:
                    A.wait(pe, "keys")
                for t in range(NTB):
                    last = mm(bank[4 + 2 * (ct % 2) + t // 4][0:TB, (t % 4) * P:(t % 4) * P + P],
                              qT[:, ct % 2, t * TB:(t + 1) * TB], keysT[:, ct, :])
                T.op(last, "score", ct)

            for b in range(first["query"], nb):
                linear(b)
                i = b - first["query"]
                score(2 * i)
                score(2 * i + 1)

            def turn_u(g, j, free):
                e = GE * g + j
                for k in range(2):
                    pe.wait_ge(free, 2 * e + (k + 1))
                    for i in range(4):
                        last = pe.transpose(bank[k][:, i * P:(i + 1) * P],
                                            Uraw[:, par(g), j, (4 * k + i) * P:(4 * k + i + 1) * P], ident[:])
                    last.then_inc(ut_mm, 1)

            def scores_of(g, j, half):
                e = GE * g + j
                pe.wait_ge(ut_low, 2 * e + 4)
                pe.wait_ge(gelu_done, 2 * e + (half + 1))
                for kt in range(KT):
                    for i, (pw, px) in enumerate(((0, 0), (0, 1), (1, 0))):
                        last = mm(bank[2 + half][:, 0:HALF], UT[:, j, pw, kt, :],
                                  xT[:, px, kt, half * HALF:(half + 1) * HALF],
                                  start=(kt == 0 and i == 0), stop=(kt == KT - 1 and i == 2))
                last.then_inc(s_mm, 1)

            def first_part(g, free, final=False, between=lambda n: None):
                for j in range(GE):
                    nxt = (g, j + 1) if j + 1 < GE else (g + 1, 0)
                    if not (final and j + 1 == GE):
                        if nxt[1] == 0:
                            pe.wait_ge(u_in[par(nxt[0])], 16 * (half_of(nxt[0]) + 1))
                        turn_u(*nxt, free)
                    for half in range(2):
                        scores_of(g, j, half)
                        between(2 * j + half)

            grant(pe, s_mm, 2)
            pe.wait_ge(u_in[0], 16)
            unit_read(pe, UNIT0[nb] - 1)
            turn_u(Grp(0), 0, u_copy)
            with pe.Fori(0, NG1 // 2, 1) as i:
                for k in range(2):
                    first_part(Grp(k, i), u_copy)

            A.wait(pe, "score", 2 * PH - 1)
            for t in range(NTB):
                V.wait(pe, "gates")
                if t >= 2:
                    V.wait(pe, "pairT", t - 2)
                for i in range(3):
                    last = pe.transpose(bank[4 + t % 2][:, i * TB:(i + 1) * TB], pick[:, t, i, :], ident[0:TB, 0:TB])
                T.op(last, "pairT", t)

            def gates_of(i, n):
                group_ = i * (GB // 2) + (n + 1)
                pe.wait_ge(is_ready, group_)
                pe.wait_ge(gate_bank, group_)
                for k in range(4):
                    s_ = (n % ISG) * 4 + k
                    o_ = bank[4 + n % 4][:, k * NK:(k + 1) * NK]
                    mm(o_, is1[:, s_, :], is2[:, s_, 0, :], start=True, stop=False)
                    last = mm(o_, is1[:, s_, :], is2[:, s_, 1, :], start=False, stop=True)
                last.then_inc(gate_mm, 1)

            with pe.Fori(0, NGB // 2, 1) as i:
                for k in range(TURN2):
                    first_part(Grp(NG1 + k, i, TURN2), u_copy,
                               between=lambda h: [gates_of(i, n) for n in gate_slots(k, h)])

            def second_part(q):
                VR = vbuf(q)
                pe.wait_ge(a_low, GE * q + GE)
                pe.wait_ge(v_low, 1 * q + 1)
                for u in range(2 * KT):
                    dt, half = u // 2, u % 2
                    if q.k < NGF:
                        bk = bank[4 + u % 4]
                        pe.wait_ge(y_add, 2 * KT * q + (u + 1))
                    else:
                        bk = bank[u % 8]
                        pe.wait_ge(y_add, 2 * KT * q + (u - 3))
                    for j in range(GE):
                        for i, (pw, pa) in enumerate(((0, 0), (0, 1), (1, 0))):
                            last = mm(bk[:, 0:HALF], VR[:, pw, j, dt * P:(dt + 1) * P],
                                      AR[:, par(q), pa, j, half * HALF:(half + 1) * HALF],
                                      start=(j == 0 and i == 0), stop=(j == GE - 1 and i == 2))
                    last.then_inc(y_mm, 1)

            grant(pe, y_mm, 2 * KT)
            first_part(Grp(NGA), ut_low)
            with pe.Fori(0, NGF // 2 - 1, 1) as i:
                for k in range(2):
                    first_part(Grp(k + 1 + NGA, i), ut_low)
                    second_part(Grp(k, i))
            first_part(Grp(NGRP - 1), ut_low, True)
            second_part(Grp(NGF - 2))
            second_part(Grp(NGF - 1))
            pe.wait_ge(gelu_done, 2 * NK + 2)
            with pe.Fori(0, NGA // 2, 1) as i:
                for k in range(2):
                    second_part(Grp(NGF + k, i))

            V.wait(pe, "y_all")
            for t in range(NTB):
                for i in range(2):
                    if t >= 2:
                        V.wait(pe, "hf", t - 2, i)
                    for j in range(4):
                        last = pe.transpose(bank[2 * (t % 2) + i][0:TB, j * P:(j + 1) * P],
                                            yT[:, 4 * i + j, t * TB:(t + 1) * TB], ident[:])
                    T.op(last, "y", t, i)

        @block.scalar
        def _(act):
            def fn(out, in_, f, *name, **kw):
                return A.op(act.activation(out, in_, f, **kw), *name)

            def high(b):
                n = sum(x[2] for x in BLOCKS[b][2])
                act.wait_ge(raw_in[b % 4], 16 * raw_count[b])
                if b >= 2:
                    T.wait(act, "unit", UNIT0[b - 1] - 1)
                fn(WR[:, b % 2, 0, :, 0:n], RAW[:, b % 4, :, 0:n], ACT.Copy, "high", b)

            def norm(k):
                act.wait_ge(h_in[k - 1], 80 if k == 1 else 96)
                for t in range(NTB):
                    if k == 2:
                        V.wait(act, "h2", t)
                    fn(sq[:], h[:, t, :], ACT.Square, "ss", k, t, accum_out=ss[:, t:t + 1])
                    A.now(act)
                V.wait(act, "ms", k)
                fn(ss[:, 16:16 + NTB], ss[:, 8:8 + NTB], ACT.Sqrt, "rt", k)
                for t in range(NTB):
                    for i in range(2):
                        T.wait(act, "xT", k, t, i)
                        fn(xT[:, 0, 4 * i:4 * i + 4, t * TB:(t + 1) * TB],
                           bank[2 * (t % 2) + i][:, 0:4 * TB].rearrange("p (k n) -> p k n", k=4), ACT.Copy,
                           "xhigh", k, t, i)

            def seqs(ap):
                return ap.rearrange("p (q s) -> p q s", q=NSEQ)

            def evacuate(b):
                kind, i, _ = BLOCKS[b]
                for u in range(UNIT0[b], UNIT0[b + 1]):
                    n = u - UNIT0[b]
                    m, half = n // 2, n % 2
                    bk = bank[u % 4]
                    src = bk[:, 0:HALF]
                    cols_ = slice(half * HALF, (half + 1) * HALF)
                    T.wait(act, "unit", u)
                    if kind == "ab":
                        fn(abT[:, cols_], bk[0:2 * HEADS, 0:HALF], ACT.Copy, "unit", u)
                    elif kind == "z":
                        fn(zT[:, 2 * i + m, cols_], src, ACT.Silu, "unit", u)
                    elif kind == "query":
                        ct = 2 * i + m
                        if ct >= 2:
                            T.wait(act, "score", ct - 2)
                        fn(qT[:, ct % 2, cols_], src, ACT.Copy, "unit", u)
                    elif kind == "qkv":
                        c = 2 * i + m
                        e = c % 2
                        if half == 0:
                            if c >= 2:
                                V.wait(act, "qconv", c - 2)
                            fn(qext[:, e, QC - 1:QC - 1 + HALF], src, ACT.Copy, "unit", u)
                        else:
                            k = TP - HALF
                            x = seqs(qext[:, e, QEXT:])
                            fn(qext[:, e, QC - 1 + HALF:QEXT], bk[:, 0:k], ACT.Copy)
                            fn(x[:, :, QC - 1:], seqs(bk[:, k:HALF]), ACT.Copy)
                            if c == 0:
                                V.wait(act, "sqT")
                            fn(x[:, :, 0:QC - 1], seqs(sqT[:, c, :]), ACT.Copy)
                            fn(qtail[:, c, :], bk[:, k - (QC - 1):HALF], ACT.Copy, "unit", u)
                    elif kind == "glu":
                        if n == 0 and i:
                            V.wait(act, "cconv", i - 1)
                        k = TP - HALF
                        if n == 0:
                            fn(gext[:, CC - 1:CC - 1 + HALF], src, ACT.Copy, "unit", u)
                        elif n == 1:
                            x = seqs(gext[:, CEXT:])
                            fn(gext[:, CC - 1 + HALF:CEXT], bk[:, 0:k], ACT.Copy)
                            fn(x[:, :, CC - 1:], seqs(bk[:, k:HALF]), ACT.Copy, "unit", u)
                            if i == 0:
                                V.wait(act, "scT")
                            fn(x[:, :, 0:CC - 1], seqs(scT[:, i, :]), ACT.Copy)
                        else:
                            fn(gate[:, cols_], src, ACT.Sigmoid, "unit", u)

            def silu(c):
                V.wait(act, "qconv", c)
                fn(qkvT[:, c, :], qkvT[:, c, :], ACT.Silu, "silu", c)

            high(0)
            high(1)
            norm(1)
            G.wait(act, "zeros")
            done = 0
            for b in range(first["out"]):
                evacuate(b)
                while done < 2 * BLOCKS[b][1] and BLOCKS[b][0] == "qkv":
                    silu(done)
                    done += 1
                if b + 2 < nb:
                    high(b + 2)
            A.counts["qtail",] = A.n
            while done < NQ:
                silu(done)
                done += 1

            V.wait(act, "ab")
            fn(tok[:, X2], tok[:, BETA], ACT.Exp, scale=-1.0)
            fn(tok[:, X3], tok[:, GD], ACT.Abs)
            A.now(act)
            fn(tok[:, X3], tok[:, X3], ACT.Exp, scale=-1.0)
            fn(dtb[:, HEADS:], dtb[:, HEADS:], ACT.Exp, "exps")
            V.wait(act, "exps")
            fn(tok[:, X3], tok[:, X3], ACT.Ln, "ln")
            V.wait(act, "cum")
            fn(tok[:, EG], tok[:, GC], ACT.Exp)
            fn(tok[:, EL], tok[:, EL], ACT.Exp)
            fn(tok[:, EGL], tok[:, GL], ACT.Exp)
            fn(gls[:], gls[:], ACT.Exp, "cum")
            for c in range(2 * HEADS):
                if c >= 2:
                    T.wait(act, "qk2", c - 2)
                A.now(act)
                fn(sqb[c % 2][:], qkvT[:, c, :], ACT.Square, "qk2", c)
            V.wait(act, "qk2")
            fn(tok[:, RQ], tok[:, RQ], ACT.Sqrt)
            fn(tok[:, RK], tok[:, RK], ACT.Sqrt, "rqk")
            T.wait(act, "tails")
            for i in range(3):
                fn(RA2[0:QC - 1 + TS, 512 * i:512 * i + 512], bank[4 + i][0:QC - 1 + TS, :], ACT.Copy, "tails")

            for ci, (c0, c) in enumerate(CHUNKS):
                s_ = ci == SAMPLE

                def take(n, dst, rows_=c, width=c, only=HEADS):
                    T.wait(act, n, ci)
                    fn(dst, gbank(n, ci)[0:rows_, 0:only * width].rearrange("p (h n) -> p h n", h=only), ACT.Copy,
                       n, ci)

                V.wait(act, "arg", ci)
                fn(M[6][0:c, :, 0:c], M[6][0:c, :, 0:c], ACT.Exp, scale=-1.0)
                fn(M[5][0:c, :, 0:c], M[5][0:c, :, 0:c], ACT.Exp, "exp", ci)
                take("khT", KHT[:, :, 0:c], P)
                take("ldT", M[1][0:c, :, 0:c])
                take("p2", M[2][0:c, :, 0:c])
                if not s_:
                    take("p4", M[5][0:c, :, 0:c])
                    take("p8", M[2][0:c, :, 0:c])
                if c == P:
                    take("n", M[0][:])
                    take("n2", M[3][:])
                    take("nt4", M[6][:])
                T.wait(act, "r0a", ci)
                if ci == 0:
                    G.wait(act, "tails_out")
                fn(RB[0:c, 0:2].rearrange("p h x d -> p h (x d)"),
                   gbank("r0a", ci)[0:c, :].rearrange("p (h n) -> p h n", h=2), ACT.Copy, "r0a", ci)
                if s_:
                    T.wait(act, "wT", ci)
                    for hh in range(HEADS):
                        fn(WQ[:, hh, :, 0:STEPS], seqs(gbank("wT", ci)[:, hh * TS:(hh + 1) * TS]), ACT.Copy)
                        fn(WQ[:, hh, :, STEPS:], seqs(qkvT[:, hh, TP:]), ACT.Copy, "wT", ci)
                else:
                    take("wT", M[2][:, :, 0:c], P)
            V.wait(act, "oss")
            fn(tok[:, OSS], tok[:, OSS], ACT.Sqrt, "oss")

            def mixed(n, src, dst, *wait):
                V.wait(act, *wait) if wait else A.now(act)
                fn(dst, src, ACT.Copy, *n)

            for ci, (c0, c) in enumerate(CHUNKS):
                mixed(("mixhigh", ci), mixf[ci % 2][:, :, 0:c], xT[:, 0, 0:HEADS, c0:c0 + c], "mix", ci)
            G.wait(act, "mixer", "last")
            for t in range(NTB):
                T.wait(act, "cn", t)
                fn(CN[:, t, :], bank[6 + t % 2][0:TB, :], ACT.Copy, "cn", t)
            V.wait(act, "cvar")
            fn(lnst[:, :, 8:9], lnst[:, :, 8:9], ACT.Sqrt, "cvar")
            for t in range(NTB):
                T.wait(act, "ln", t)
                V.wait(act, "mixlow", len(CHUNKS) - 1) if t < 2 else V.wait(act, "clow", t - 2)
                for c in range(NG):
                    fn(mixf[t % 2][:, c, 0:TB], bank[4 + t % 2][:, c * TB:(c + 1) * TB], ACT.Silu, "csilu", t,
                       bias=cols[:, 56 + c:57 + c], scale=cols[:, 52 + c:53 + c])
                mixed(("chigh", t), mixf[t % 2][:, :, 0:TB], xT[:, 0, HEADS:KT, t * TB:(t + 1) * TB])
            A.counts["mixer", "last"] = A.n

            for b in range(first["out"], first["query"]):
                high(b + 2)
            norm(2)
            act.wait_ge(h2_done, 16)
            for i in range(4):
                T.wait(act, "keys") if i == 0 else None
                fn(keysT[:, 4 * i:4 * i + 4, :], bank[4 + i][:, :].rearrange("p (k n) -> p k n", k=4), ACT.Copy,
                   "keys")
            for b in range(first["query"], nb):
                evacuate(b)
                if b + 2 < nb:
                    high(b + 2)
                for ct in (2 * (b - first["query"]), 2 * (b - first["query"]) + 1):
                    T.wait(act, "score", ct)
                    fn(scores[:, 0:4, ct, :], bank[4 + 2 * (ct % 2)][0:TB, :].rearrange("p (t n) -> p t n", t=4),
                       ACT.Copy)
                    fn(scores[:, 4, ct, :], bank[5 + 2 * (ct % 2)][0:TB, 0:P], ACT.Copy, "score", ct)
            grant(act, gate_bank, 4)
            grant(act, gblk_out[0], 16)
            grant(act, gblk_out[1], 16)
            grant(act, u_copy, 2)
            grant(act, gelu_done, 2)
            grant(act, act_out[0], 16)
            grant(act, act_out[1], 16)

            def split_u(g, j, copy=False):
                e = GE * g + j
                for k in range(2):
                    act.wait_ge(ut_mm, 2 * e + (k + 1))
                    if k == 0:
                        act.wait_ge(s_mm, 2 * e)
                        if copy:
                            act.wait_ge(ut_low, 2 * e)
                    act.activation(UT[:, j, 0, 4 * k:4 * k + 4, :],
                                   bank[k][:, :].rearrange("p (k n) -> p k n", k=4), ACT.Copy
                                   ).then_inc(ut_high, 1)
                    if copy:
                        act.activation(Ucopy[:, j, 4 * k * P:4 * (k + 1) * P], bank[k][:, :], ACT.Copy
                                       ).then_inc(u_copy, 1)

            def first_part(g, final=False, copy=False, between=lambda n: None):
                for j in range(GE):
                    e = GE * g + j
                    nxt = (g, j + 1) if j + 1 < GE else (g + 1, 0)
                    if not (final and j + 1 == GE):
                        split_u(*nxt, copy)
                    if copy:
                        act.wait_ge(act_out[j], 16 * g + 16)
                    else:
                        act.wait_ge(a_mul, e + (1 - GE * NGA))
                    for half in range(2):
                        act.wait_ge(s_mm, 2 * e + (half + 3))
                        act.activation((actA if copy else actv)[:, j, half * HALF:(half + 1) * HALF],
                                       bank[2 + half][:, 0:HALF], ACT.Gelu).then_inc(gelu_done, 1)
                        between(2 * j + half)
                    if not copy:
                        high_a(g + -NGA, j)

            def high_a(q, j):
                act.wait_ge(a_mul, GE * q + (j + 3))
                if j == 0:
                    act.wait_ge(y_mm, 2 * KT * q)
                act.activation(AR[:, par(q), 0, j, :], prod[:, j, :], ACT.Copy).then_inc(a_high, 1)

            def split_v(q):
                act.wait_ge(v_in[par(q)], 16 * (half_of(q) + 1))
                act.wait_ge(y_mm, 2 * KT * q + (0 if q.k >= NGF else 2 * KT))
                act.activation(vbuf(q)[:, 0], Vraw[:, par(q)], ACT.Copy).then_inc(v_high, 1)

            split_u(Grp(0), 0, True)
            with act.Fori(0, NG1 // 2, 1) as i:
                for k in range(2):
                    first_part(Grp(k, i), copy=True)
            V.wait(act, "top", NTB - 1)
            fn(pick[:, :, 2, :], pick[:, :, 2, :], ACT.Exp, "gexp")

            def gates_of(i, n):
                blk, q = n // (GB // 4), n % (GB // 4)
                act.wait_ge(gate_mm, i * (GB // 2) + (n + 1 + ISG))
                if q == 0:
                    act.wait_ge(gblk_out[blk], i * 16 + 16)
                act.activation(gblk[:, blk, :, 4 * q:4 * q + 4],
                               bank[4 + n % 4][:, :].rearrange("p (k n) -> p n k", k=4), ACT.Copy
                               ).then_inc(gate_bank, 1)

            with act.Fori(0, NGB // 2, 1) as i:
                for k in range(TURN2):
                    first_part(Grp(NG1 + k, i, TURN2), copy=True,
                               between=lambda h: [gates_of(i, n) for n in gate_slots(k, h)])
            for i in range(2):
                act.wait_ge(gblk_out[i], 16 * (NGB // 2 + 1))
                act.wait_ge(act_out[i], 16 * (NGA + 1))
            first_part(Grp(NGA))
            with act.Fori(0, NGF // 2 - 1, 1) as i:
                for k in range(2):
                    split_v(Grp(k, i))
                    first_part(Grp(k + 1 + NGA, i))
            split_v(Grp(NGF - 2))
            first_part(Grp(NGRP - 1), True)
            split_v(Grp(NGF - 1))
            with act.Fori(0, NGA // 2, 1) as i:
                for k in range(2):
                    q = Grp(NGF + k, i)
                    for j in range(GE):
                        high_a(q, j)
                    split_v(q)

            for t in range(NTB):
                V.wait(act, "hf", t, 1)
                A.now(act)
                fn(yo[:, 0, :], hf[:, t, :], ACT.Square, "ss", 3, t, accum_out=fs[:, t:t + 1])
            V.wait(act, "ms", 3)
            fn(fs[:, 16:16 + NTB], fs[:, 8:8 + NTB], ACT.Sqrt, "rt", 3)

        @block.vector
        def _(dve):
            def op(ins, *name):
                return V.op(ins, *name)

            def chain(ins, *name):
                V.op(ins, *name)
                V.now(dve)

            tt = dve.tensor_tensor

            def low(b):
                n = sum(x[2] for x in BLOCKS[b][2])
                A.wait(dve, "high", b)
                op(tt(WR[:, b % 2, 1, :, 0:n], RAW[:, b % 4, :, 0:n], WR[:, b % 2, 0, :, 0:n].bitcast(F32),
                      ALU.subtract), "low", b)

            def rsqrt_in(src, dst, scale):
                chain(dve.tensor_scalar(dst, src, scale, EPS, ALU.mult, ALU.add))

            def norm(k):
                A.wait(dve, "ss", k, NTB - 1)
                op(dve.tensor_scalar(ss[:, 8:8 + NTB], ss[:, 0:NTB], 1.0 / D, EPS, ALU.mult, ALU.add), "ms", k)
                A.wait(dve, "rt", k)
                chain(dve.reciprocal(ss[:, 8:8 + NTB], ss[:, 16:16 + NTB]))
                dve.wait_ge(row_in[k - 1], 16)

                def lows(t):
                    for i in range(2):
                        A.wait(dve, "xhigh", k, t, i)
                        o_ = (slice(None), slice(4 * i, 4 * i + 4), slice(t * TB, (t + 1) * TB))
                        op(tt(xT[:, 1][o_], bank[2 * (t % 2) + i][:, 0:4 * TB].rearrange("p (k n) -> p k n", k=4),
                              xT[:, 0][o_].bitcast(F32), ALU.subtract), "xlow", k, t, i)

                for t in range(NTB):
                    if t >= 2:
                        T.wait(dve, "xT", k, t - 2, 1)
                    op(dve.scalar_tensor_tensor(xn[:, t % 2, :], h[:, t, :], ss[:, 8 + t:9 + t], wrow[:],
                                                ALU.mult, ALU.mult), "xn", k, t)
                    if t:
                        lows(t - 1)
                lows(NTB - 1)

            def conv(dst, dstq, src, srcq, w, taps, width, bias=None):
                d3 = dstq.rearrange("p (q s) -> p q s", q=NSEQ)
                s3 = srcq.rearrange("p (q s) -> p q s", q=NSEQ)
                for j in range(taps):
                    a, b = src[:, j:j + TP], s3[:, :, j:j + STEPS]
                    if j == 0:
                        if bias is None:
                            op(dve.tensor_scalar(dst, a, w(j), None, ALU.mult))
                            op(dve.tensor_scalar(d3, b, w(j), None, ALU.mult))
                        else:
                            op(dve.tensor_scalar(dst, a, w(j), bias, ALU.mult, ALU.add))
                            op(dve.tensor_scalar(d3, b, w(j), bias, ALU.mult, ALU.add))
                    else:
                        V.now(dve)
                        op(dve.scalar_tensor_tensor(dst, a, w(j), dst, ALU.mult, ALU.add))
                        op(dve.scalar_tensor_tensor(d3, b, w(j), d3, ALU.mult, ALU.add))

            T.wait(dve, "cols")
            op(dve.tensor_copy(cols[:], bank[4][:, 0:61]))
            op(dve.tensor_copy(dwcols[:], bank[4][:, 128:128 + CC * NG]))
            T.wait(dve, "sqT")
            op(dve.tensor_copy(sqT[:].rearrange("p c n -> p (c n)"), bank[5][:, 0:24 * NQ]), "sqT")
            T.wait(dve, "scT")
            for i in range(2):
                chain(dve.tensor_copy(scT[:, 2 * i:2 * i + 2, :].rearrange("p c n -> p (c n)"),
                                      bank[6 + i][:, 0:480]), "scT")
            low(0)
            low(1)
            norm(1)
            for b in range(first["out"]):
                kind, i, _ = BLOCKS[b]
                if kind == "qkv":
                    for c in (2 * i, 2 * i + 1):
                        e = c % 2
                        A.wait(dve, "unit", UNIT0[b] + 2 * (c % 2) + 1)
                        G.wait(dve, "zeros")
                        conv(qkvT[:, c, 0:TP], qkvT[:, c, TP:], qext[:, e, 0:QEXT], qext[:, e, QEXT:],
                             lambda j: cols[:, NQ * j + c:NQ * j + c + 1], QC, QEXT)
                        V.counts["qconv", c] = V.n
                elif kind == "glu":
                    c = i
                    x = gext[:, CC - 1:CEXT]
                    xs = gext[:, CEXT:].rearrange("p (q s) -> p q s", q=NSEQ)
                    A.wait(dve, "unit", UNIT0[b] + 3)
                    op(tt(x, x, gate[:, 0:TP], ALU.mult))
                    chain(tt(xs[:, :, CC - 1:], xs[:, :, CC - 1:],
                             gate[:, TP:].rearrange("p (q s) -> p q s", q=NSEQ), ALU.mult))
                    op(dve.tensor_copy(ctail[:, c, 0:CC - 1], x[:, TP - (CC - 1):]))
                    op(dve.tensor_copy(ctail[:, c, CC - 1:].rearrange("p (q s) -> p q s", q=NSEQ),
                                       xs[:, :, CC - 1:]), "ctail")
                    conv(cT[:, c, 0:TP], cT[:, c, TP:], gext[:, 0:CEXT], gext[:, CEXT:],
                         lambda j: dwcols[:, NG * j + c:NG * j + c + 1], CC, CEXT, cols[:, 48 + c:49 + c])
                    V.counts["cconv", c] = V.n
                if b + 2 < nb:
                    low(b + 2)

            G.wait(dve, "masks")
            T.wait(dve, "ab")
            for ci, (c0, c) in enumerate(CHUNKS):
                op(tt(tok[0:c, GD, ci, :], bank[4][0:c, 8 * ci:8 * ci + 4], dtb[0:c, 0:HEADS], ALU.add))
                op(dve.tensor_copy(tok[0:c, BETA, ci, :], bank[4][0:c, 8 * ci + 4:8 * ci + 8]), "ab")
            A.wait(dve, "exps")
            op(dve.tensor_scalar(tok[:, X2], tok[:, X2], 1.0, None, ALU.add))
            chain(dve.tensor_scalar(tok[:, X3], tok[:, X3], 1.0, None, ALU.add), "exps")
            op(dve.reciprocal(tok[:, BETA], tok[:, X2]))
            A.wait(dve, "ln")
            chain(dve.scalar_tensor_tensor(tok[:, GD], tok[:, GD], 0.0, tok[:, X3], ALU.max, ALU.add))
            chain(dve.scalar_tensor_tensor(tok[:, GD], tok[:, GD], -1.0,
                                           dtb[:, HEADS:].unsqueeze(1).to_broadcast([P, len(CHUNKS), HEADS]),
                                           ALU.mult, ALU.mult), "g")
            op(tt(gm[:], tok[0:TS, GD, SAMPLE, :].unsqueeze(1).to_broadcast([TS, NSEQ, HEADS]),
                  seq_of[:].unsqueeze(2).to_broadcast([TS, NSEQ, HEADS]), ALU.mult), "gm")
            T.wait(dve, "cum")
            op(dve.tensor_copy(gls[:].rearrange("p b h -> p (b h)"), bank[6][:, 0:TS]))
            for ci, (c0, c) in enumerate(CHUNKS):
                n = c if ci == SAMPLE else P
                op(dve.tensor_copy(tok[0:c, GC, ci, :], bank[5][0:c, 8 * ci:8 * ci + 4]))
                op(dve.tensor_copy(tok[0:n, GL, ci, :], bank[5][0:n, 8 * ci + 4:8 * ci + 8]))
            V.now(dve)
            op(tt(tok[:, EL], tok[:, GL], tok[:, GC], ALU.subtract), "cum")
            T.wait(dve, "qk2", 2 * HEADS - 1)
            for ci, (c0, c) in enumerate(CHUNKS):
                op(dve.tensor_scalar(tok[0:c, RQ, ci, :], bank[7][0:c, 8 * ci:8 * ci + 4], EPS, None, ALU.add))
                op(dve.tensor_scalar(tok[0:c, RK, ci, :], bank[7][0:c, 8 * ci + 4:8 * ci + 8], EPS, None, ALU.add),
                   "qk2")
            A.wait(dve, "rqk")
            op(dve.reciprocal(tok[:, RQ], tok[:, RQ]))
            chain(dve.reciprocal(tok[:, RK], tok[:, RK]))
            chain(dve.tensor_scalar(tok[:, RQ], tok[:, RQ], float(DH) ** -0.5, None, ALU.mult))
            A.wait(dve, "cum")
            op(tt(tok[:, EQ], tok[:, EG], tok[:, RQ], ALU.mult))
            chain(tt(tok[:, BEG], tok[:, EG], tok[:, BETA], ALU.mult))
            T.wait(dve, "tails")
            chain(dve.tensor_copy(RA3[:], bank[7][0:CC - 1 + TS, :]), "tails")

            for ci, (c0, c) in enumerate(CHUNKS):
                s_ = ci == SAMPLE

                def src(n, width=c, heads=HEADS, rows_=c):
                    T.wait(dve, n, ci)
                    return gbank(n, ci)[0:rows_, 0:heads * width].rearrange("p (h n) -> p h n", h=heads)

                def mask(m):
                    return m[0:c, 0:c].unsqueeze(1).to_broadcast([c, HEADS, c])

                def sq_(m):
                    return m[0:c, :, 0:c]

                chain(tt(KH[0:c], src("k", P), rows(RK, c, ci, P), ALU.mult), "k", ci)
                op(tt(KE[0:c], KH[0:c], rows(EL, c, ci, P), ALU.mult), "KE", ci)
                op(tt(RA[0:c, :, 1, :], KH[0:c], rows(BEG, c, ci, P), ALU.mult))
                op(tt(RA[0:c, :, 0, :], src("v", P), rows(BETA, c, ci, P), ALU.mult), "v", ci)
                V.counts["RA", ci] = V.n
                chain(tt(sq_(M[7]), src("gb"), rows(GC, c, ci, c), ALU.subtract), "gb", ci)
                op(tt(sq_(M[6]), sq_(M[7]), mask(pos_s if s_ else pos), ALU.add))
                op(tt(sq_(M[5]), sq_(M[7]), mask(neg_s if s_ else neg), ALU.add), "arg", ci)
                A.wait(dve, "exp", ci)
                if ci == 0:
                    G.wait(dve, "tails_out")
                L = M[3] if c == P else M[0]
                chain(tt(sq_(L), src("kk"), sq_(M[6]), ALU.mult), "kk", ci)
                chain(tt(sq_(L), sq_(L), rows(BETA, c, ci, c), ALU.mult), "Ld", ci)
                if c == P:
                    chain(tt(sq_(M[0]), sq_(L), mask(diag16), ALU.mult), "Ld", ci)
                    op(tt(sq_(M[7]), sq_(L), sq_(M[0]), ALU.subtract), "Lo", ci)
                op(tt(AT[0:c, :, 0:c], src("kq"), sq_(M[5]), ALU.mult), "kq", ci)
                A.wait(dve, "ldT", ci)
                chain(tt(sq_(M[4]), mask(ident), sq_(M[1]), ALU.subtract), "t0", ci)
                op(dve.tensor_copy(sq_(M[3]), src("pt2")), "pt2", ci)

                def add(n, dst, a, *sl):
                    chain(tt(dst, a, sl[0], ALU.add), n, ci)

                chain(tt(sq_(M[4]), sq_(M[4]), src("t1"), ALU.add), "t1", ci)
                if not s_:
                    op(dve.tensor_copy(sq_(M[6]), src("pt4")), "pt4", ci)
                    chain(tt(sq_(M[4]), sq_(M[4]), src("t2"), ALU.add), "t2", ci)
                    chain(tt(sq_(M[4]), sq_(M[4]), src("t3"), ALU.add), "t3", ci)
                if c == P:
                    op(dve.tensor_copy(sq_(M[1]), src("nt")), "nt", ci)
                    op(dve.tensor_copy(sq_(M[5]), src("nt2")), "nt2", ci)

                def two(t, i):
                    return t[0:c, 2 * i:2 * i + 2].rearrange("p h x d -> p h (x d)")

                op(dve.tensor_copy(two(RB, 1), src("r0b", 256, 2)), "r0b", ci)
                R = RB
                if c == P:
                    A.wait(dve, "r0a", ci)
                    for n, x, y, f in (("r1", RB, RA, ALU.add), ("r2", RA, RB, ALU.add), ("r3", RB, RA, ALU.subtract)):
                        V.now(dve)
                        for i, ab in enumerate("ab"):
                            op(tt(two(y, i), two(x, i), src(n + ab, 256, 2), f), n + ab, ci)
                    R = RA
                if s_:
                    T.wait(dve, "swh", HEADS - 1)
                    sv = gbank("sw", ci)[:, 0:256].rearrange("p (g x) -> p g x", x=2 * STEPS)
                    for i in range(2):
                        op(dve.tensor_copy(M[2][:, i, :].rearrange("p (g x) -> p g x", x=STEPS),
                                           sv[:, :, STEPS * i:STEPS * (i + 1)]), "sw", ci)
                V.now(dve)
                if c != P:
                    A.wait(dve, "r0a", ci)
                chain(tt(VN[0:c], R[0:c, :, 0, :], src("ws", P), ALU.subtract), "ws", ci)
                O = ostore(ci)
                op(tt(O, src("qs", P), rows(EQ, c, ci, P), ALU.mult), "qs", ci)
                chain(tt(M[3][0:c], src("o1", P), rows(RQ, c, ci, P), ALU.mult), "o1", ci)
                chain(tt(O, O, M[3][0:c], ALU.add))
                chain(tt(M[3][0:c], O, O, ALU.mult))
                op(dve.tensor_reduce(tok[0:c, OSS, ci, :], M[3][0:c], AX.X, ALU.add), "oss", ci)
                if not s_:
                    chain(tt(state[:], state[:], rows(EGL, P, ci, P), ALU.mult))
                    chain(tt(state[:], state[:], src("su", P, HEADS, P), ALU.add), "su", ci)
                else:
                    for hh in range(HEADS):
                        if hh:
                            T.wait(dve, f"su{hh - 1}1", ci)
                        op(tt(KTM[:].rearrange("p (b d) -> p b d", b=NSEQ),
                              KE[0:c, hh, :].unsqueeze(1).to_broadcast([c, NSEQ, DH]),
                              seq_of[:].unsqueeze(2).to_broadcast([c, NSEQ, DH]), ALU.mult), f"ktm{hh}", ci)
                        dve.wait_ge(ss_in[hh % 2], 16 * (hh // 2 + 3))
                        S_ = SS[hh % 2]
                        chain(tt(S_[:], S_[:], gls[:, :, hh:hh + 1].to_broadcast([P, NSEQ, DH]), ALU.mult))
                        for i in range(2):
                            op(tt(S_[:, 4 * i:4 * i + 4], S_[:, 4 * i:4 * i + 4], src(f"su{hh}{i}", P, 4, P), ALU.add),
                               f"su{hh}{i}", ci)
                        V.counts["ss", hh] = V.n

            V.now(dve)
            op(dve.tensor_scalar(tok[:, OSS], tok[:, OSS], 1.0 / DH, EPS, ALU.mult, ALU.add), "oss")
            A.wait(dve, "oss")
            chain(dve.reciprocal(tok[:, OSS], tok[:, OSS]))

            def mixlow(ci):
                c0, c = CHUNKS[ci]
                A.wait(dve, "mixhigh", ci)
                op(tt(xT[:, 1, 0:HEADS, c0:c0 + c], mixf[ci % 2][:, :, 0:c],
                      xT[:, 0, 0:HEADS, c0:c0 + c].bitcast(F32), ALU.subtract), "mixlow", ci)

            for ci, (c0, c) in enumerate(CHUNKS):
                if ci >= 2:
                    T.wait(dve, "on", ci - 2)
                op(tt(ONB[ci % 2][0:c], ostore(ci), rows(OSS, c, ci, P), ALU.mult), "on", ci)
                T.wait(dve, "on", ci)
                op(dve.scalar_tensor_tensor(mixf[ci % 2][:, :, 0:c],
                                            bank[4 + ci % 2][:, 0:HEADS * c].rearrange("p (h n) -> p h n", h=HEADS),
                                            cols[:, 60:61], zT[:, :, c0:c0 + c], ALU.mult, ALU.mult), "mix", ci)
                if ci:
                    mixlow(ci - 1)
            mixlow(len(CHUNKS) - 1)
            for t in range(NTB):
                A.wait(dve, "cn", t)
                chain(dve.bn_stats(lnst[:, t, 0:6], CN[:, t, :]))
                chain(dve.bn_aggr(lnst[:, t, 6:8], lnst[:, t, 0:6]))
            op(dve.tensor_scalar(lnst[:, :, 8:9], lnst[:, :, 7:8], EPS, None, ALU.add), "cvar")
            A.wait(dve, "cvar")
            chain(dve.reciprocal(lnst[:, :, 9:10], lnst[:, :, 8:9]))
            for t in range(NTB):
                op(dve.tensor_scalar(CN[:, t, :], CN[:, t, :], lnst[:, t, 6:7], lnst[:, t, 9:10], ALU.subtract,
                                     ALU.mult), "ln", t)
            for t in range(NTB):
                A.wait(dve, "chigh", t)
                o_ = (slice(None), slice(HEADS, KT), slice(t * TB, (t + 1) * TB))
                op(tt(xT[:, 1][o_], mixf[t % 2][:, :, 0:TB], xT[:, 0][o_].bitcast(F32), ALU.subtract), "clow", t)
            V.counts["mixlow", "last"] = V.n
            V.counts["mixer", "last"] = V.n

            for b in range(first["out"], first["query"]):
                i = BLOCKS[b][1]
                if i == 0:
                    dve.wait_ge(h_in[1], 96)
                for t in range(NTB):
                    T.wait(dve, "unit", UNIT0[b] + t)
                    x = h[:, t, i * WB:(i + 1) * WB]
                    op(tt(x, x, bank[(UNIT0[b] + t) % 4][0:TB, 0:WB], ALU.add), "unit", UNIT0[b] + t)
                    V.counts["h2", t] = V.n
                low(b + 2)
            V.counts["h2", "last"] = V.n
            norm(2)
            for b in range(first["query"], nb - 2):
                low(b + 2)

            for t in range(NTB):
                A.wait(dve, "score", 2 * PH - 1)
                S_ = scores[:, t]

                def top(best_, besti_, v, n):
                    for c in range(n):
                        op(dve.max(best_(c)[:, 0:8], v(c)))
                    V.now(dve)
                    for c in range(n):
                        op(dve.max_index(besti_(c)[:, 0:8], best_(c)[:, 0:8], v(c)))
                    V.now(dve)
                    for c in range(n):
                        op(dve.match_replace(v(c), best_(c)[:, 0:8], v(c), LOWEST))
                    V.now(dve)
                    for c in range(n):
                        op(dve.max(best_(c)[:, 8:16], v(c)))
                    V.now(dve)
                    for c in range(n):
                        op(dve.max_index(besti_(c)[:, 8:16], best_(c)[:, 8:16], v(c)))
                    V.now(dve)

                top(lambda c: best[:, c], lambda c: besti[:, c], lambda c: S_[:, c, :], 2 * PH)
                op(dve.tensor_copy(bestf[:], besti[:]))
                bv = best[:].rearrange("p (h x) a -> p h x a", x=2)
                fv = bestf[:].rearrange("p (h x) a -> p h x a", x=2)
                sh = [TB, PH, TOPK, TOPK]
                chain(tt(cand[:], bv[:, :, 0, :].unsqueeze(3).to_broadcast(sh),
                         bv[:, :, 1, :].unsqueeze(2).to_broadcast(sh), ALU.add))
                top16 = pick[:, t, 2, :]
                top(lambda c: top16[:, 16 * c:16 * c + 16], lambda c: topi[:, 16 * c:16 * c + 16],
                    lambda c: cand[:, c].rearrange("p a b -> p (a b)"), PH)
                hr = top16.rearrange("p (h r) -> p h r", h=PH)
                chain(dve.tensor_copy(gmax[:], hr[:, :, 0]))
                op(tt(hr, hr, gmax[:].unsqueeze(2).to_broadcast([TB, PH, TOPK]), ALU.subtract), "top", t)
                op(dve.tensor_scalar(topa[:, 0], topi[:], 4, None, ALU.logical_shift_right))
                chain(dve.tensor_scalar(topa[:, 1], topi[:], 15, None, ALU.bitwise_and))
                chain(dve.tensor_copy(topf[:], topa[:]))
                for x in range(2):
                    chain(tt(eqa[:], iota[0:TB, 0:TOPK].unsqueeze(1).to_broadcast([TB, PAIRS, TOPK]),
                             topf[:, x, :].unsqueeze(2).to_broadcast([TB, PAIRS, TOPK]), ALU.is_equal))
                    chain(tt(sel[:].rearrange("p (h r) a -> p h r a", h=PH),
                             eqa[:].rearrange("p (h r) a -> p h r a", h=PH),
                             fv[:, :, x, :].unsqueeze(2).to_broadcast(sh), ALU.mult))
                    chain(dve.tensor_reduce(pick[:, t, x, :], sel[:], AX.X, ALU.add))
            A.wait(dve, "gexp")
            gv = pick[:, :, 2, :].rearrange("p t (h r) -> p t h r", h=PH)
            chain(dve.tensor_reduce(gsum[:], gv, AX.X, ALU.add))
            chain(dve.reciprocal(gsum[:], gsum[:]))
            op(tt(gv, gv, gsum[:].unsqueeze(3).to_broadcast([TB, NTB, PH, TOPK]), ALU.mult), "gates")
            for t in range(NTB):
                T.wait(dve, "pairT", t)
                chain(dve.tensor_copy(pairT[:, 0:3, t * TB:(t + 1) * TB],
                                      bank[4 + t % 2][:, 0:3 * TB].rearrange("p (x n) -> p x n", x=3)), "pairT", t)
            chain(dve.tensor_copy(ghi[:], pairT[:, 2, :]))
            chain(tt(pairT[:, 3, :], pairT[:, 2, :], ghi[:].bitcast(F32), ALU.subtract))

            grant(dve, gate_mm, ISG)
            with dve.Fori(0, NGB // 2, 1) as i:
                for n in range(GB // 2):
                    dve.wait_ge(gate_mm, i * (GB // 2) + (n + 1))
                    for k in range(4):
                        s1 = (n % ISG) * 4 + k
                        col = i * (2 * GB) + (4 * n + k)
                        dve.tensor_scalar(is1[:, s1, :], iota[:], pairT[:, 0, bass.ds(col, 1)], None, ALU.is_equal)
                        for x, part in enumerate((ghi[:].bitcast(F32), pairT[:, 3, :])):
                            last = dve.tensor_scalar(is2[:, s1, x, :], iota[:], pairT[:, 1, bass.ds(col, 1)],
                                                     part[:, bass.ds(col, 1)], ALU.is_equal, ALU.mult)
                    last.then_inc(is_ready, 1)

            def split_u(g, j):
                e = GE * g + j
                for k in range(2):
                    dve.wait_ge(ut_high, 2 * e + (k + 1))
                    tt(UT[:, j, 1, 4 * k:4 * k + 4, :], bank[k][:, :].rearrange("p (k n) -> p k n", k=4),
                       UT[:, j, 0, 4 * k:4 * k + 4, :].bitcast(F32), ALU.subtract).then_inc(ut_low, 1)

            def gated(q, j, src):
                if j == 0:
                    dve.wait_ge(g_in[par(q)], 16 * (half_of(q) + 1))
                tt(prod[:, j, :].rearrange("p (b n) -> p b n", b=NGB), src.rearrange("p (b n) -> p b n", b=NGB),
                   Gt[:, par(q), :, j * GB:(j + 1) * GB], ALU.mult).then_inc(a_mul, 1)

            def low_a(q, j):
                dve.wait_ge(a_high, GE * q + (j + 1))
                tt(AR[:, par(q), 1, j, :], prod[:, j, :], AR[:, par(q), 0, j, :].bitcast(F32),
                   ALU.subtract).then_inc(a_low, 1)

            def first_part(q, final=False):
                g = q + NGA
                for j in range(GE):
                    nxt = (g, j + 1) if j + 1 < GE else (g + 1, 0)
                    if not (final and j + 1 == GE):
                        split_u(*nxt)
                    dve.wait_ge(gelu_done, 2 * (GE * g + j) + 4)
                    gated(q, j, actv[:, j, :])
                    low_a(q, j)

            def stored_part(q):
                dve.wait_ge(act_in[par(q)], 16 * (half_of(q) + (1 - NGF // 2)))
                for j in range(GE):
                    gated(q, j, actC[:, par(q), j, :])
                for j in range(GE):
                    low_a(q, j)

            def sums(q):
                for u in range(2 * KT):
                    dt, half = u // 2, u % 2
                    y = yT[:, dt, half * HALF:(half + 1) * HALF]
                    dve.wait_ge(y_mm, 2 * KT * q + (2 * KT + u + 1))
                    tt(y, y, bank[4 + u % 4 if q.k < NGF else u % 8][:, 0:HALF], ALU.add).then_inc(y_add, 1)

            grant(dve, a_mul, 2)
            grant(dve, y_add, 4)
            dve.wait_ge(gblk_out[0], 16 * (NGB // 2 + 1))
            dve.wait_ge(gblk_out[1], 16 * (NGB // 2 + 1))
            chain(dve.memset(yT[:], 0.0))
            first_part(Grp(0))
            with dve.Fori(0, NGF // 2 - 1, 1) as i:
                for k in range(2):
                    first_part(Grp(k + 1, i))
                    sums(Grp(k, i))
            first_part(Grp(NGF - 1), True)
            sums(Grp(NGF - 2))
            stored_part(Grp(NGF))
            sums(Grp(NGF - 1))
            with dve.Fori(0, NGA // 2 - 1, 1) as i:
                for k in range(2):
                    stored_part(Grp(NGF + 1 + k, i))
                    sums(Grp(NGF + k, i))
            stored_part(Grp(NGRP - 1))
            sums(Grp(NGRP - 2))
            sums(Grp(NGRP - 1))

            dve.wait_ge(y_add, 2 * KT * NGRP + 4)
            chain(dve.memset(fs[:, 23:24], 0.0), "y_all")

            dve.wait_ge(hf_in, 16)
            for t in range(NTB):
                for i in range(2):
                    T.wait(dve, "y", t, i)
                    x = hf[:, t, 512 * i:512 * i + 512]
                    op(tt(x, x, bank[2 * (t % 2) + i][0:TB, :], ALU.add), "hf", t, i)
            A.wait(dve, "ss", 3, NTB - 1)
            op(dve.tensor_scalar(fs[:, 8:8 + NTB], fs[:, 0:NTB], 1.0 / D, EPS, ALU.mult, ALU.add), "ms", 3)
            A.wait(dve, "rt", 3)
            chain(dve.reciprocal(fs[:, 8:8 + NTB], fs[:, 16:16 + NTB]))
            dve.wait_ge(row_in[2], 16)
            for t in range(NTB):
                if t >= 2:
                    dve.wait_ge(y_out[t % 2], 16 * (t // 2))
                op(dve.scalar_tensor_tensor(yo[:, t % 2, :], hf[:, t, :], fs[:, 8 + t:9 + t], wrow[:],
                                            ALU.mult, ALU.mult), "yo", t)


INPUTS = ["x_prompt", "x_sample", "state_gdn", "state_qkv_conv", "state_conf_conv", "meta_tokens", "norm_mix_w",
          "w_in", "conv_qkv_w", "a_log", "dt_bias", "gdn_norm_w", "conf_dw_w", "conf_dw_b", "conf_ln_w",
          "conf_ln_b", "w_out", "norm_ffn_w", "w_query", "sub_keys", "expert_u", "expert_v", "final_norm_w"]
OUTPUTS = [(1, SEQ, D), (NSEQ, STEPS, D), (1, 1, HEADS, DH, DH), (1, 1, QC - 1, QKV), (1, 1, CC - 1, CW),
           (1, NSEQ, HEADS, DH, DH), (1, NSEQ, QC - 1, QKV), (1, NSEQ, CC - 1, CW)]


def kernel(**inputs):
    from concourse import bacc
    from concourse.bass_utils import run_bass_kernel_spmd

    counts = {}
    for _ in range(2):
        nc = bacc.Bacc("TRN2", target_bir_lowering=False, num_devices=1)
        arrays, ins = {}, []
        for name in INPUTS:
            a = np.ascontiguousarray(inputs[name])
            arrays[f"in_{name}"] = a
            ins.append(nc.dram_tensor(f"in_{name}", a.shape, F32, kind="ExternalInput").ap())
        outs = [nc.dram_tensor(f"out_{i}", shape, F32, kind="ExternalOutput").ap()
                for i, shape in enumerate(OUTPUTS)]
        build(nc, ins, outs, counts)
    r = run_bass_kernel_spmd(nc, [arrays], core_ids=[0])
    return tuple(r.results[0][f"out_{i}"] for i in range(len(OUTPUTS)))
```

```python
from contextlib import ExitStack

import numpy as np

import concourse.bass as bass
from concourse import mybir

F32 = mybir.dt.float32
F32R = mybir.dt.float32r
U32 = mybir.dt.uint32
BF16 = mybir.dt.bfloat16
ALU = mybir.AluOpType
ACT = mybir.ActivationFunctionType
AX = mybir.AxisListType

P = 128
D = 1024
KT = D // P
META, SEQ, NSEQ, STEPS = 16, 512, 8, 4
TP = META + SEQ
TS = NSEQ * STEPS
NT = TP + TS
TB = 112
NTB = NT // TB
HALF = NT // 2
HEADS, DH = 4, 128
QC, CC = 4, 31
QKV, GW, CW = 1536, 512, 512
NQ, NG = QKV // P, CW // P
INW = QKV + GW + 2 * HEADS + 2 * CW
QEXT = (QC - 1) + TP
QSEG = (QC - 1) + STEPS
CEXT = (CC - 1) + TP
CSEG = (CC - 1) + STEPS
PH, KD, NK, TOPK = 8, 128, 128, 16
NE = NK * NK
PAIRS = PH * TOPK
EPS = 1e-6
BIG = 1e30
LOWEST = -3.0e38
CHUNKS = [(0, 128), (128, 128), (256, 128), (384, 128), (512, 16), (TP, TS)]
SAMPLE = len(CHUNKS) - 1
WB = 256
GE = 2
NGRP = NK // GE
GB = 56
NGB = NT // GB
NG1, TURN2 = 20, 8
NGA = NG1 + TURN2 * (NGB // 2)
ISG = 4
NGF = NGRP - NGA
assert NT == NTB * TB and NT == NGB * GB and NG1 % 2 == 0 and TURN2 % 2 == 0 and NGF % 2 == 0


class Steps:

    def __init__(self, sem, counts):
        self.sem, self.counts, self.n = sem, counts, 0

    def op(self, ins, *name):
        ins.then_inc(self.sem, 1)
        self.n += 1
        if name:
            self.counts[name] = self.n
        return ins

    def now(self, eng):
        if self.n:
            eng.wait_ge(self.sem, self.n)

    def wait(self, eng, *name):
        eng.wait_ge(self.sem, self.counts.get(name, 1))


def linear_blocks():
    z0, ab0 = QKV, QKV + GW
    v0 = ab0 + 2 * HEADS
    blocks = [("ab", 0, [("in", ab0, P)])]
    blocks += [("qkv", i, [("in", WB * i, WB)]) for i in range(QKV // WB)]
    glu = [("glu", c, [("in", v0 + P * c, P), ("in", v0 + CW + P * c, P)]) for c in range(NG)]
    z = [("z", i, [("in", z0 + WB * i, WB)]) for i in range(GW // WB)]
    blocks[1:1] = [glu[0]]
    blocks += [glu[1], z[0], z[1], glu[3], glu[2]]
    blocks += [("out", i, [("out", WB * i, WB)]) for i in range(D // WB)]
    blocks += [("query", i, [("query", WB * i, WB)]) for i in range(2 * PH * KD // WB)]
    return blocks


BLOCKS = linear_blocks()
GLUS = [b for b, x in enumerate(BLOCKS) if x[0] == "glu"]
UNIT0 = [0]
for _kind, _, _parts in BLOCKS:
    UNIT0.append(UNIT0[-1] + (NTB if _kind == "out" else 2 * sum(n for _, _, n in _parts) // P))


def build(nc, ins, outs, counts):
    (x_prompt, x_sample, state_gdn, state_qkv, state_conf, meta, norm_mix_w, w_in, conv_qkv_w, a_log,
     dt_bias, gdn_norm_w, conf_dw_w, conf_dw_b, conf_ln_w, conf_ln_b, w_out, norm_ffn_w, w_query,
     sub_keys, expert_uT, expert_v, final_norm_w) = ins
    (y_prompt, y_sample, gdn_prompt, qkv_prompt, conf_prompt, gdn_sample, qkv_sample, conf_sample) = outs
    WEIGHTS = {"in": w_in[0].rearrange("(k p) n -> p k n", p=P),
               "out": w_out[0].rearrange("(k p) n -> p k n", p=P),
               "query": w_query[0].rearrange("(k p) n -> p k n", p=P)}

    h2_dram = nc.dram_tensor("h2_dram", (NT, D), F32, kind="Internal").ap()
    gate_dram = nc.dram_tensor("gate_dram", (NGB, NK, NK, GB), F32, kind="Internal").ap()
    act_dram = nc.dram_tensor("act_dram", (GE * NGA, P, NT), F32, kind="Internal").ap()

    ctx = ExitStack()
    with ctx:
        def at(name, shape, dt, word):
            return nc.alloc_sbuf_tensor_at(name, shape, dt, offset=base + 4 * word)

        base = -(-nc.sbuf_base // 64) * 64
        room = (nc.sbuf_top - base) // 4
        used = {"all": 0}

        def place(name, shape, dt=F32, region="all"):
            words = int(np.prod(shape[1:])) * mybir.dt.size(dt) // 4
            words = -(-words // 8) * 8
            t = at(name, shape, dt, used[region])
            used[region] += words
            assert used[region] <= room
            return t

        ident = place("ident", [P, P])
        tri = place("tri", [P, P])
        neg = place("neg", [P, P])
        pos = place("pos", [P, P])
        diag16 = place("diag16", [P, P])
        tri_s = place("tri_s", [TS, TS])
        neg_s = place("neg_s", [TS, TS])
        pos_s = place("pos_s", [TS, TS])
        same_s = place("same_s", [TS, TS])
        seq_of = place("seq_of", [TS, NSEQ])
        ones = place("ones", [P, P])
        iota = place("iota", [P, P])
        cols = place("cols", [P, 61])
        dwcols = place("dwcols", [P, CC * NG])
        w_wrow = used["all"]
        wrow = place("wrow", [TB, D])
        w_xT = used["all"]
        xT = place("xT", [P, 2, KT, NT], F32R)
        WR = place("WR", [P, 2, 2, KT, WB], F32R)
        RAW = place("RAW", [P, 4, KT, WB])
        late = used["all"]
        raws = late - 4 * KT * WB
        used["x"] = used["m"] = used["t"] = used["g"] = used["e"] = used["n"] = late

        h = place("h", [TB, NTB, D], region="n")
        xn = place("xn", [TB, 2, D], region="n")
        sq = place("sq", [TB, D], region="n")
        ss = place("ss", [TB, 3 * 8], region="n")
        qext = place("qext", [P, 2, QEXT + NSEQ * QSEG], region="m")
        w_g = used["m"]
        used["m"] += -(-(CEXT + NSEQ * CSEG) // 8) * 8
        gext = [at(f"gext{i}", [P, CEXT + NSEQ * CSEG], F32, w)
                for i, w in enumerate((w_g, w_wrow, raws + 3 * KT * WB, raws + 3 * KT * WB + D))]
        gate = place("gate", [P, NT], region="m")
        qkvT = place("qkvT", [P, NQ, NT], region="m")
        cT = place("cT", [P, NG, NT], region="m")
        abT = at("abT", [2 * HEADS, NT], F32, used["m"] - NT)
        zT = place("zT", [P, HEADS, NT], region="m")
        sqT = place("sqT", [P, NQ, NSEQ * (QC - 1)], region="m")
        qtail = place("qtail", [P, NQ, (QC - 1) + TS], region="m")
        ctail = place("ctail", [P, NG, (CC - 1) + TS], region="m")
        ctmp = place("ctmp", [P, NT], region="m")
        tok = place("tok", [P, 14, len(CHUNKS), HEADS], region="m")
        state = place("state", [P, HEADS, DH], region="m")
        dtb = place("dtb", [P, 2 * HEADS], region="m")
        WQ = place("WQ", [P, HEADS, NSEQ, 2 * STEPS], region="m")
        gls = place("gls", [P, NSEQ, HEADS], region="m")
        gm = place("gm", [TS, NSEQ, HEADS], region="m")
        gdn0 = used["m"]
        used["c"] = gdn0
        crow = place("crow", [61, P], region="c")
        dwrow = place("dwrow", [CC * NG, P], region="c")
        sconf = place("sconf", [120, 2, CW], region="c")
        sqkv = place("sqkv", [NSEQ * (QC - 1), QKV], region="c")
        scT = place("scT", [P, NG, NSEQ * (CC - 1)], region="c")
        used["d"] = gdn0
        used["d1"] = w_xT

        def delta_set(i, region):
            B = {}
            for name, shape in (("KH", [P, HEADS, DH]), ("KHT", [P, HEADS, P]), ("KE", [P, HEADS, DH]),
                                ("RA", [P, HEADS, 2, DH]), ("RB", [P, HEADS, 2, DH])):
                B[name] = place(f"{name}_{i}", shape, region=region)
            B["M"] = [place(f"M{m}_{i}", [P, HEADS, P], region=region) for m in range(8)]
            B["AT"] = place(f"AT_{i}", [P, HEADS, P], region=region)
            B["VN"] = place(f"VN_{i}", [P, HEADS, DH], region=region)
            return B

        SETS = [delta_set(0, "d"), delta_set(1, "d1")]
        assert used["d1"] <= w_xT + 2 * KT * NT
        m0 = gdn0 + 512 * 7
        OS = at("OS", [P, 2, HEADS, DH], F32, late)
        pairT = place("pairT", [P, 5, NT], region="t")
        ghi = place("ghi", [P, NT], BF16, region="t")
        iotab = place("iotab", [P, NK], BF16, region="t")
        used["g"] = used["t"]
        used["k"] = used["t"]
        eqa = place("eqa", [TB, PAIRS, TOPK], region="k")
        qT = place("qT", [P, 2, NT], region="t")
        keysT = place("keysT", [P, 2 * PH, NK], region="t")
        scores = place("scores", [TB, NTB, 2 * PH, NK], region="t")
        best = place("best", [TB, 2 * PH, TOPK], region="t")
        besti = place("besti", [TB, 2 * PH, TOPK], U32, region="t")
        bestf = place("bestf", [TB, 2 * PH, TOPK], region="t")
        cand = place("cand", [TB, PH, TOPK, TOPK], region="t")
        sel = place("sel", [TB, PAIRS, TOPK], region="t")
        topi = place("topi", [TB, PAIRS], U32, region="t")
        topa = place("topa", [TB, 2, PAIRS], U32, region="t")
        topf = place("topf", [TB, 2, PAIRS], region="t")
        pick = place("pick", [TB, NTB, 3, PAIRS], region="t")
        gsum = place("gsum", [TB, NTB, PH], region="t")
        gmax = place("gmax", [TB, PH], region="t")
        assert used["t"] <= room - 2 * NT
        is1 = place("is1", [P, 4 * ISG, NK], BF16, region="g")
        is2 = place("is2", [P, 4 * ISG, 3, NK], BF16, region="g")
        assert used["g"] <= room - 2 * NT - 2 * GB * NK
        gblk = place("gblk", [P, 2, NK, GB], region="g")
        SS = [at(f"SS{i}", [P, NSEQ, DH], F32, raws + KT * WB + 1024 * i) for i in range(HEADS)]
        CN = at("CN", [TB, 2, CW], F32, raws + 3 * KT * WB)
        lnst = at("lnst", [TB, NTB, 6 + 2 + 2], F32, late + 1088)
        sqb = [at(f"sqb{i}", [P, NT], F32, m0 + 512 + 1024 * i) for i in range(2)]
        RA2 = at("RA2", [P, 3 * CW], F32, raws)
        KTM = at("KTM", [TS, NSEQ * DH], F32, gdn0 + 512 * 3)
        ONB = [at(f"ONB{i}", [P, HEADS, DH], F32, raws + 3 * KT * WB + D + 512 * i) for i in range(2)]
        RA3 = at("RA3", [CC - 1 + TS, CW], F32, late + 1176 + 832)
        keysrow = at("keysrow", [P, 2 * PH, KD], F32, used["n"])
        Uraw = at("Uraw", [P, 2, GE, D], F32, raws)
        Vraw = at("Vraw", [P, 2, GE, D], F32, raws + 2 * GE * D)
        wrs = raws - 4 * KT * WB
        actA = at("actA", [P, 2, NT], F32, room - 2 * NT)
        actC = at("actC", [P, 2, GE, NT], F32, raws)
        UT = at("UT", [P, 2, 2, KT, P], F32R, wrs)
        VR1 = at("VR1", [P, 2, GE, D], F32R, wrs + 4 * KT * P)
        VR0 = at("VR0", [P, 2, GE, D], F32R, wrs)
        AR = place("AR", [P, 2, 2, GE, NT], F32R, region="e")
        Gt = place("Gt", [P, 2, NGB, GE * GB], region="e")
        actv = place("actv", [P, 2, NT], region="e")
        prod = place("prod", [P, 2, NT], region="e")
        yT = place("yT", [P, KT, NT], region="e")
        hf = place("hf", [TB, NTB, D], region="e")
        yo = place("yo", [TB, 2, D], region="e")
        fs = place("fs", [TB, 24], region="e")

        bank = [ctx.enter_context(nc.psum_tensor(f"bank{i}", [P, 512], F32)) for i in range(8)]

        def sem(name):
            return ctx.enter_context(nc.semaphore(name))

        V = Steps(sem("vector_done"), counts.setdefault("V", {}))
        A = Steps(sem("scalar_done"), counts.setdefault("A", {}))
        T = Steps(sem("tensor_done"), counts.setdefault("T", {}))
        G = Steps(sem("gpsimd_done"), counts.setdefault("G", {}))
        h_in = [sem(f"h_in{i}") for i in range(2)]
        row_in = [sem(f"row_in{i}") for i in range(3)]
        small_in = sem("small_in")
        raw_in = [sem(f"raw_in{i}") for i in range(4)]
        gate_mm = sem("gate_mm")
        gate_bank = sem("gate_bank")
        is_ready = sem("is_ready")
        gblk_out = [sem(f"gblk_out{i}") for i in range(2)]
        u_in = [sem(f"u_in{i}") for i in range(2)]
        v_in = [sem(f"v_in{i}") for i in range(2)]
        g_in = [sem(f"g_in{i}") for i in range(2)]
        ut_high, ut_low = sem("ut_high"), sem("ut_low")
        act_out = [sem(f"act_out{i}") for i in range(2)]
        act_in = [sem(f"act_in{i}") for i in range(2)]
        s_mm, gelu_done, a_mul = sem("s_mm"), sem("gelu_done"), sem("a_mul")
        a_high, a_low = sem("a_high"), sem("a_low")
        v_high, v_low = sem("v_high"), sem("v_low")
        y_mm, y_add = sem("y_mm"), sem("y_add")
        hf_in = sem("hf_in")
        y_out = [sem(f"y_out{i}") for i in range(2)]
        out_done = sem("out_done")
        h2_done = sem("h2_done")
        ss_out = sem("ss_out")
        ss_in = [sem(f"ss_in{i}") for i in range(HEADS)]

        nb = len(BLOCKS)
        first = {k: next(b for b in range(nb) if BLOCKS[b][0] == k) for k in ("ab", "out", "query")}
        raw_count = []
        for b in range(nb):
            raw_count.append(len(BLOCKS[b][2]) + (raw_count[b - 4] if b >= 4 else 0))

        def groups(ci):
            c = CHUNKS[ci][1]
            g = [("k", V), ("v", V), ("gb", V), ("khT", A), ("kk", V), ("kq", V), ("ldT", A),
                 ("p2", A), ("pt2", V), ("t1", V)]
            if ci != SAMPLE:
                g += [("p4", A), ("pt4", V), ("t2", V), ("p8", A), ("t3", V)]
            if c == P:
                g += [("n", A), ("nt", V), ("n2", A), ("nt2", V), ("nt4", A)]
            g += [("r0a", A), ("r0b", V)]
            if c == P:
                g += [("r1a", V), ("r1b", V), ("r2a", V), ("r2b", V), ("r3a", V), ("r3b", V)]
            g += [("wT", A)]
            if ci == SAMPLE:
                g += [("sw", V)]
            g += [("ws", V), ("qs", V), ("o1", V)]
            if ci == SAMPLE:
                g += [("on", V)]
            else:
                g += [("su", V), ("on", V)]
            return g

        STEP = {}
        for n, _ in groups(0) + groups(SAMPLE):
            STEP.setdefault(n, len(STEP))
        STEP["sw"] = STEP["wT"] + 0.5
        ON_FIRST, ON_STEP = {0: 96, 1: 100, 2: 104, 3: 108, SAMPLE: 119, 4: 124}, {"oss": 0, "onb": 1, "on": 1.9}
        for hh in range(HEADS):
            STEP["sw", hh] = STEP["wT"] + 0.5 + hh
        FIRST = {0: 0, 1: 18, 2: 36, 3: 54, SAMPLE: 72, 4: 90}
        SET = {ci: i % 2 for i, ci in enumerate(FIRST)}
        LN = len(CHUNKS)
        ROOTS = LN + NTB
        LN_AT = {"cs": (78, 2), "roots": (93 - 5 * NTB, 5), "cn": (95, 5), "ln": (98, 5)}

        def turn(n, ci):
            if ci >= LN:
                return LN_AT[n][0] + LN_AT[n][1] * (ci - LN), ci
            if n in ON_STEP:
                return ON_FIRST[ci] + ON_STEP[n], ci
            late_ = HEADS - 1 if ci == SAMPLE and not isinstance(n, tuple) and STEP[n] > STEP["sw"] else 0
            return FIRST[ci] + STEP[n] + late_, ci

        def side_by_side(tile, ln_tile, filler=iter(())):
            n = 0
            tiles = {ci: (tile if ci < LN else ln_tile)(ci) for ci in range(ROOTS + 1)}
            step = {ci: next(t, None) for ci, t in tiles.items()}
            step = {ci: n_ for ci, n_ in step.items() if n_}
            while step:
                ci = min(step, key=lambda c: turn(step[c], c))
                step[ci] = next(tiles[ci], None)
                n += 1
                if n % 3 == 0:
                    next(filler, None)
                if step[ci] is None:
                    del step[ci]
            for _ in filler:
                pass

        GROUPS = sorted([(n, ci, e) for ci in range(LN) for n, e in groups(ci) if n != "sw"]
                        + [(n, LN + t, e) for t in range(NTB) for n, e in (("cs", V), ("cn", V), ("ln", A))],
                        key=lambda x: turn(x[0], x[1]))
        RING = [4, 5, 6, 7, 0, 1, 2]
        WHERE = {(n, ci): i for i, (n, ci, _) in enumerate(GROUPS)}

        def gbank(n, ci):
            if n[:2] == "su" and n != "su":
                return bank[4 + 2 * (int(n[2]) % 2) + int(n[3])]
            return bank[3 if n == "sw" else RING[WHERE[n, ci] % len(RING)]]

        def grant(eng, s_, n):
            eng.sem_inc(s_, n)

        class Grp:

            def __init__(self, k, turn=None, step=2):
                self.k, self.turn, self.step = k, turn, step

            def __add__(self, n):
                return Grp(self.k + n, self.turn, self.step)

            def __rmul__(self, m):
                return m * self.k if self.turn is None else self.turn * (self.step * m) + m * self.k

        def gate_slots(k, h):
            at_, halves = 2 * GE * k + h, 2 * GE * TURN2
            return range(GB // 2 * at_ // halves, GB // 2 * (at_ + 1) // halves)

        def par(g):
            return g.k % 2

        def half_of(g):
            return g.k // 2 if g.turn is None else g.turn * (g.step // 2) + g.k // 2

        def vbuf(q):
            return VR0 if q.k >= NGF and par(q) == 0 else VR1

        def unit_read(eng, u):
            b = max(b for b in range(nb) if UNIT0[b] <= u)
            (V if BLOCKS[b][0] == "out" else A).wait(eng, "unit", u)

        def rows(i, c, ci, width):
            return tok[0:c, i, ci, :].unsqueeze(2).to_broadcast([c, HEADS, width])

        def ostore(ci):
            if ci < 4:
                return qkvT[:, 2 * HEADS:3 * HEADS, CHUNKS[ci][0]:CHUNKS[ci][0] + P]
            return OS[0:CHUNKS[ci][1], ci - 4]

        SC_AB, SC_CUM, SC_QK = 2, 5, first["out"] - HEADS

        assert SET[SAMPLE] == 0
        for i in range(2):
            of_set = [ci for ci in FIRST if SET[ci] == i]
            for a, b in zip(of_set, of_set[1:]):
                assert turn("o1" if a == SAMPLE else "su", a)[0] < FIRST[b]

        def mixer_out(k):
            return qkvT[:, k, :] if k < HEADS else cT[:, k - HEADS, :]

        GD, BETA, X2, X3, GC, EG, GL, EL, RQ, RK, BEG, EGL, OSS, EQ = range(14)

        def conv_parts(dst, dstq, src, srcq, j):
            d3 = dstq.rearrange("p (q s) -> p q s", q=NSEQ)
            s3 = srcq.rearrange("p (q s) -> p q s", q=NSEQ)
            return (dst, src[:, j:j + TP]), (d3, s3[:, :, j:j + STEPS])

        block = ctx.enter_context(nc.Block())

        @block.sync
        def _(sp):
            def load_rows(dst, s):
                sp.dma_start(dst[0:META, 0, :], meta).then_inc(s, 16)
                sp.dma_start(dst[META:TB, 0, :], x_prompt[0, 0:TB - META, :]).then_inc(s, 16)
                sp.dma_start(dst[:, 1:NTB - 1, :],
                             x_prompt[0, TB - META:(NTB - 1) * TB - META, :].rearrange("(t p) d -> p t d", p=TB)
                             ).then_inc(s, 16)
                sp.dma_start(dst[0:TB - TS, NTB - 1, :],
                             x_prompt[0, (NTB - 1) * TB - META:SEQ, :]).then_inc(s, 16)
                sp.dma_start(dst[TB - TS:TB, NTB - 1, :],
                             x_sample.rearrange("b s d -> (b s) d")).then_inc(s, 16)

            def load_row(w, s):
                sp.dma_start(wrow[:], w.to_broadcast([TB, D])).then_inc(s, 16)

            load_rows(h, h_in[0])
            load_row(norm_mix_w, row_in[0])

            def mixer_io():
                sp.dma_start(conf_sample[0][:, 0:CC - 1 - STEPS, :], state_conf[0][:, STEPS:CC - 1, :]
                             ).then_inc(out_done, 16)
                for hh in range(HEADS):
                    V.wait(sp, "low", first["out"] + hh // 2)
                    sp.dma_start(SS[hh][:], state_gdn[0].rearrange("b h k v -> h k b v")[hh]).then_inc(ss_in[hh], 16)
                A.wait(sp, "tails")
                V.wait(sp, "tails")
                sp.dma_start(qkv_prompt[0, 0], RA2[0:QC - 1, 0:QKV]).then_inc(out_done, 16)
                for s in range(1, STEPS):
                    sp.dma_start(qkv_sample[0][:, s - 1, :],
                                 RA2[QC - 1 + s:QC - 1 + s + STEPS * (NSEQ - 1) + 1:STEPS, 0:QKV]
                                 ).then_inc(out_done, 16)
                sp.dma_start(conf_prompt[0, 0], RA3[0:CC - 1, :]).then_inc(out_done, 16)
                sp.dma_start(conf_sample[0][:, CC - 1 - STEPS:, :], RA3[CC - 1:, :]).then_inc(out_done, 16)
                V.wait(sp, "su", SAMPLE - 1)
                sp.dma_start(gdn_prompt[0, 0].rearrange("h k v -> k h v"), state[:]).then_inc(out_done, 16)
                sp.wait_ge(out_done, 16 * 8)

            for b in range(nb):
                if b == first["out"] + 2:
                    mixer_io()
                    G.wait(sp, "cconv", 2)
                    V.wait(sp, "mixlow", "last")
                    T.wait(sp, "mixer", "last")
                    A.wait(sp, "mixer", "last")
                    load_rows(h, h_in[1])
                    sp.dma_start(keysrow[:], sub_keys[0].rearrange("h p k d -> k (h p) d")).then_inc(h_in[1], 16)
                    load_row(norm_ffn_w, row_in[1])
                if b in (first["out"] + 4, first["out"] + 5):
                    for hh in (2 * (b - first["out"] - 4), 2 * (b - first["out"] - 4) + 1):
                        V.wait(sp, "ss", hh)
                        sp.dma_start(gdn_sample[0].rearrange("b h k v -> h k b v")[hh], SS[hh][:]
                                     ).then_inc(ss_out, 16)
                    sp.wait_ge(ss_out, 32 * (b - first["out"] - 3))
                if b >= 4:
                    V.wait(sp, "low", b - 4)
                at_ = 0
                for name, c0, n in BLOCKS[b][2]:
                    sp.dma_start(RAW[:, b % 4, :, at_:at_ + n], WEIGHTS[name][:, :, c0:c0 + n]
                                 ).then_inc(raw_in[b % 4], 16)
                    at_ += n
                if b == first["query"] + 5:
                    V.wait(sp, "h2", "last")
                    sp.dma_start(h2_dram.rearrange("(t p) d -> p t d", p=TB), h[:]).then_inc(h2_done, 16)
            V.wait(sp, "xn", 2, NTB - 1)
            load_row(final_norm_w.rearrange("(a d) -> a d", a=1), row_in[2])

            Vw = expert_v[0].rearrange("(p k) d -> p k d", p=NK)

            def load(dst, src, g, s_):
                k0 = GE * g
                sp.dma_start(dst, src(bass.ds(k0, GE))).then_inc(s_, 16)

            def load_u(g):
                load(Uraw[:, par(g)], lambda k: expert_uT[k].rearrange("k p t e -> p k (t e)"), g, u_in[par(g)])

            def next_u(g):
                sp.wait_ge(ut_low, GE * (g + -1))
                load_u(g)

            def store_act(g):
                for j in range(GE):
                    e = GE * g + j
                    sp.wait_ge(gelu_done, 2 * e + 6)
                    sp.dma_start(act_dram[bass.ds(e, 1)].rearrange("a p n -> (a p) n"), actA[:, j, :]
                                 ).then_inc(act_out[j], 16)

            for g in range(2):
                V.wait(sp, "low", nb - 4 + (g - nb) % 4)
                load_u(Grp(g))
            with sp.Fori(0, NG1 // 2, 1) as i:
                for k in range(2):
                    next_u(Grp(k + 2, i))
                    store_act(Grp(k, i))
            with sp.Fori(0, NGB // 2, 1) as i:
                for blk in range(2):
                    for k in range(TURN2 // 2 * blk, TURN2 // 2 * (blk + 1)):
                        next_u(Grp(NG1 + k + 2, i, TURN2))
                        store_act(Grp(NG1 + k, i, TURN2))
                    sp.wait_ge(gate_bank, i * (GB // 2) + ((blk + 1) * (GB // 4) + 4))
                    sp.dma_start(gate_dram[bass.ds(i * 2 + blk, 1)].rearrange("a p k n -> (a p) k n"),
                                 gblk[:, blk]).then_inc(gblk_out[blk], 16)

            def load_v(q, g):
                load(Vraw[:, par(q)], lambda k: Vw[:, k, :], g, v_in[par(q)])

            def load_g(q, g):
                load(Gt[:, par(q)].rearrange("p b (k n) -> p b k n", n=GB),
                     lambda k: gate_dram[:, :, k, :].rearrange("b p k n -> p b k n"), g, g_in[par(q)])

            V.wait(sp, "low", nb - 1)
            for q in range(2):
                load_v(Grp(q), Grp(NGA + q))
            for blk in range(2):
                sp.wait_ge(gblk_out[blk], 16 * (NGB // 2 + 1))
            for q in range(2):
                load_g(Grp(q), Grp(NGA + q))
            sp.dma_start(hf[:], h2_dram.rearrange("(t p) d -> p t d", p=TB)).then_inc(hf_in, 16)
            with sp.Fori(0, NGF // 2 - 1, 1) as i:
                for k in range(2):
                    q = Grp(k + 2, i)
                    next_u(q + NGA)
                    sp.wait_ge(a_mul, GE * (q + -1) + 2)
                    load_g(q, q + NGA)
                    sp.wait_ge(v_low, 1 * (q + -1))
                    load_v(q, q + NGA)
            for j in range(GE):
                sp.wait_ge(act_out[j], 16 * (NGA + 1))
            sp.wait_ge(ut_low, NK)
            with sp.Fori(0, NGA // 2, 1) as i:
                for k in range(2):
                    g = Grp(k, i)
                    q = g + NGF
                    sp.wait_ge(a_mul, GE * (q + -1) + 2)
                    load(actC[:, k], lambda k_: act_dram[k_].rearrange("k p n -> p k n"), g, act_in[k])
                    load_g(q, g)
                    sp.wait_ge(v_low, 1 * (q + -1))
                    load_v(q, g)

            for t in range(NTB):
                V.wait(sp, "yo", t)
                r0 = t * TB - META
                if t == 0:
                    sp.dma_start(y_prompt[0, 0:TB - META, :], yo[META:TB, 0, :]).then_inc(y_out[t % 2], 16)
                elif t < NTB - 1:
                    sp.dma_start(y_prompt[0, r0:r0 + TB, :], yo[:, t % 2, :]).then_inc(y_out[t % 2], 16)
                else:
                    sp.dma_start(y_prompt[0, r0:SEQ, :], yo[0:TB - TS, t % 2, :]).then_inc(y_out[t % 2], 16)
                    sp.dma_start(y_sample.rearrange("b s d -> (b s) d"), yo[TB - TS:TB, t % 2, :]
                                 ).then_inc(y_out[t % 2], 16)
            sp.wait_ge(y_out[0], 16 * 4)
            sp.wait_ge(y_out[1], 16 * 2)

        @block.gpsimd
        def _(pool):
            n = 0
            for dst, src in (
                    (crow[0:48, :], conv_qkv_w[0].rearrange("t (c p) -> (t c) p", p=P)),
                    (crow[48:52, :], conf_dw_b[0].rearrange("(c p) -> c p", p=P)),
                    (crow[52:56, :], conf_ln_w[0].rearrange("(c p) -> c p", p=P)),
                    (crow[56:60, :], conf_ln_b[0].rearrange("(c p) -> c p", p=P)),
                    (crow[60:61, :], gdn_norm_w),
                    (dwrow[:], conf_dw_w[0].rearrange("t (c p) -> (t c) p", p=P)),
                    (sconf[:], state_conf[0].rearrange("(r b) t c -> (b t) r c", r=2)),
                    (sqkv[:], state_qkv[0].rearrange("b t c -> (b t) c")),
                    (dtb[:, 0:HEADS], dt_bias.to_broadcast([P, HEADS])),
                    (dtb[:, HEADS:], a_log.to_broadcast([P, HEADS]))):
                pool.dma_start(dst, src).then_inc(small_in, 16)
                n += 1
            assert n == 10

            def op(ins, *name):
                G.op(ins, *name)
                G.now(pool)

            def keep(m, compare, fill, base_, pattern, cm):
                op(pool.affine_select(out=m, in_=m, compare_op=compare, fill=fill, base=base_,
                                      pattern=pattern, channel_multiplier=cm))

            op(pool.memset(ident[:], 0.0))
            keep(ident[:], ALU.not_equal, 1.0, 0, [[-1, P]], 1)
            op(pool.memset(ones[:], 1.0), "ident")
            op(pool.memset(tri[:], 1.0))
            keep(tri[:], ALU.is_ge, 0.0, 0, [[1, P]], -1)
            op(pool.memset(neg[:], 0.0))
            keep(neg[:], ALU.is_ge, -BIG, 0, [[1, P]], -1)
            op(pool.memset(pos[:], 0.0))
            keep(pos[:], ALU.is_gt, BIG, 0, [[-1, P]], 1)

            def within(m, width, fill, inner):
                n_ = m.shape[1] // (width if inner else 1)
                v = m.rearrange("p (b w) -> p b w", w=width) if inner else m
                tail = [[0, width]] if inner else []
                keep(v, ALU.is_ge, fill, 0, [[-width, n_]] + tail, 1)
                keep(v, ALU.is_ge, fill, width - 1, [[width, n_]] + tail, -1)

            op(pool.memset(diag16[:], 1.0))
            within(diag16[:], 16, 0.0, True)
            op(pool.memset(same_s[:], 1.0))
            within(same_s[:], STEPS, 0.0, True)
            op(pool.memset(seq_of[:], 1.0))
            within(seq_of[:], STEPS, 0.0, False)
            op(pool.tensor_copy(tri_s[:], tri[0:TS, 0:TS]))
            within(tri_s[:], STEPS, 0.0, True)
            op(pool.tensor_copy(neg_s[:], neg[0:TS, 0:TS]))
            within(neg_s[:], STEPS, -BIG, True)
            op(pool.tensor_copy(pos_s[:], pos[0:TS, 0:TS]))
            within(pos_s[:], STEPS, BIG, True)
            op(pool.iota(iota[:], pattern=[[1, P]], base=0, channel_multiplier=0,
                         allow_small_or_imprecise_dtypes=True), "masks")

            T.wait(pool, "xT", 1, NTB - 1, 1)
            V.wait(pool, "xn", 1, NTB - 1)
            op(pool.memset(qext[:, :, 0:QC - 1], 0.0))
            op(pool.memset(gext[0][:, 0:CC - 1], 0.0))
            op(pool.memset(gext[1][:, 0:CC - 1], 0.0))
            op(pool.memset(tok[:], 1.0))
            op(pool.memset(state[:], 0.0), "zeros")

            for c in (0, 2):
                if c == 2:
                    V.wait(pool, "low", first["out"] - 2)
                    op(pool.memset(gext[2][:, 0:CC - 1], 0.0))
                V.wait(pool, "glu", c)
                for j in range(CC):
                    w = dwcols[:, NG * j + c:NG * j + c + 1]
                    parts = conv_parts(cT[:, c, 0:TP], cT[:, c, TP:], gext[c][:, 0:CEXT], gext[c][:, CEXT:], j)
                    tmp = ctmp[:, 0:TP], ctmp[:, TP:].rearrange("p (q s) -> p q s", q=NSEQ)
                    for (d, x), t_ in zip(parts, tmp):
                        if j == 0:
                            G.op(pool.tensor_scalar(d, x, w, cols[:, 48 + c:49 + c], ALU.mult, ALU.add))
                        else:
                            G.op(pool.tensor_scalar(t_, x, w, None, ALU.mult))
                    G.now(pool)
                    if j:
                        for (d, x), t_ in zip(parts, tmp):
                            G.op(pool.tensor_tensor(d, d, t_, ALU.add))
                        G.now(pool)
                G.counts["cconv", c] = G.n

            def low_u(g):
                for j in range(GE):
                    pool.wait_ge(ut_high, GE * g + (j + 1))
                    pool.tensor_tensor(UT[:, j, 1].rearrange("p k n -> p (k n)"), Uraw[:, par(g), j, :],
                                       UT[:, j, 0].rearrange("p k n -> p (k n)").bitcast(F32), ALU.subtract
                                       ).then_inc(ut_low, 1)

            low_u(Grp(0))
            with pool.Fori(0, NGA // 2, 1) as i:
                for k in range(2):
                    low_u(Grp(k + 1, i))
            low_u(Grp(NGA + 1))

            def low_v(q):
                VR = vbuf(q)
                pool.wait_ge(v_high, 1 * q + 1)
                pool.tensor_tensor(VR[:, 1], Vraw[:, par(q)], VR[:, 0].bitcast(F32), ALU.subtract
                                   ).then_inc(v_low, 1)

            with pool.Fori(0, NGF // 2 - 1, 1) as i:
                for k in range(2):
                    low_v(Grp(k, i))
                    low_u(Grp(k + 2 + NGA, i))
            low_v(Grp(NGF - 2))
            low_v(Grp(NGF - 1))
            with pool.Fori(0, NGA // 2, 1) as i:
                for k in range(2):
                    low_v(Grp(NGF + k, i))

        @block.tensor
        def _(pe):
            mm = pe.matmul

            G.wait(pe, "ident")
            pe.wait_ge(small_in, 160)
            pe.transpose(bank[4][:, 0:61], crow[:], ident[0:61, 0:61])
            T.op(pe.transpose(bank[4][:, 128:128 + CC * NG], dwrow[:], ident[0:CC * NG, 0:CC * NG]), "cols")
            for c in range(NQ):
                last = pe.transpose(bank[5][:, 24 * c:24 * c + 24], sqkv[:, P * c:P * c + P], ident[0:24, 0:24])
            T.op(last, "sqT")
            for c in range(NG):
                for r in range(2):
                    last = pe.transpose(bank[6 + c // 2][:, 240 * (c % 2) + 120 * r:240 * (c % 2) + 120 * r + 120],
                                        sconf[:, r, P * c:P * c + P], ident[0:120, 0:120])
            T.op(last, "scT")

            def norm(k):
                for t in range(NTB):
                    V.wait(pe, "xn", k, t)
                    for i in range(2):
                        if t >= 2:
                            V.wait(pe, "xlow", k, t - 2, i)
                        for j in range(4):
                            last = pe.transpose(bank[2 * (t % 2) + i][:, j * TB:(j + 1) * TB],
                                                xn[:, t % 2, (4 * i + j) * P:(4 * i + j + 1) * P],
                                                ident[0:TB, 0:TB])
                        T.op(last, "xT", k, t, i)

            def linear(b):
                kind, _, parts = BLOCKS[b]
                V.wait(pe, "low", b)
                W = WR[:, b % 2]
                for u in range(UNIT0[b], UNIT0[b + 1]):
                    if u >= 4:
                        unit_read(pe, u - 4)
                    n = u - UNIT0[b]
                    for kt in range(KT):
                        for i, (pw, px) in enumerate(((0, 0), (0, 1), (1, 0))):
                            go = dict(start=(kt == 0 and i == 0), stop=(kt == KT - 1 and i == 2))
                            if kind == "out":
                                last = mm(bank[u % 4][0:TB, 0:WB], xT[:, px, kt, n * TB:(n + 1) * TB],
                                          W[:, pw, kt, :], **go)
                            else:
                                m, half = n // 2, n % 2
                                last = mm(bank[u % 4][:, 0:HALF], W[:, pw, kt, m * P:(m + 1) * P],
                                          xT[:, px, kt, half * HALF:(half + 1) * HALF], **go)
                    T.op(last, "unit", u)

            def scalars(b):
                if b == SC_AB:
                    unit_read(pe, UNIT0[first["ab"] + 1] - 1)
                    V.wait(pe, "scT")
                    for ci, (c0, c) in enumerate(CHUNKS):
                        last = pe.transpose(bank[4][0:c, 8 * ci:8 * ci + 8], abT[:, c0:c0 + c], ident[0:8, 0:8])
                    T.op(last, "ab")
                elif b == SC_CUM:
                    V.wait(pe, "g")
                    V.wait(pe, "gm")
                    for ci, (c0, c) in enumerate(CHUNKS):
                        s_ = ci == SAMPLE
                        mm(bank[5][0:c, 8 * ci:8 * ci + 4], (tri_s if s_ else tri)[0:c, 0:c], tok[0:c, GD, ci, :])
                        rows_ = c if s_ else P
                        mm(bank[5][0:rows_, 8 * ci + 4:8 * ci + 8], (same_s if s_ else ones)[0:c, 0:rows_],
                           tok[0:c, GD, ci, :])
                    T.op(mm(bank[6][:, 0:TS], ones[0:TS, :], gm[:].rearrange("p b h -> p (b h)")), "cum")
                elif b >= SC_QK:
                    for c_ in (2 * (b - SC_QK), 2 * (b - SC_QK) + 1):
                        A.wait(pe, "qk2", c_)
                        for ci, (c0, c) in enumerate(CHUNKS):
                            last = mm(bank[7][0:c, 8 * ci + c_:8 * ci + c_ + 1], sqb[c_ % 2][:, c0:c0 + c],
                                      ones[:, 0:1])
                        T.op(last, "qk2", c_)

            norm(1)
            V.wait(pe, "xlow", 1, NTB - 1, 1)
            for b in range(first["out"]):
                linear(b)
                scalars(b)

            A.wait(pe, "qtail")
            V.wait(pe, "ctail")
            V.wait(pe, "cum")
            V.wait(pe, "ab")
            V.wait(pe, "qk2")
            for c in range(NQ):
                last = pe.transpose(bank[4 + c // 4][0:QC - 1 + TS, P * (c % 4):P * (c % 4) + P], qtail[:, c, :],
                                    ident[:])
            for c in range(NG):
                last = pe.transpose(bank[7][0:CC - 1 + TS, P * c:P * c + P], ctail[:, c, :], ident[:])
            T.op(last, "tails")

            def free_bank(n, ci):
                i = WHERE.get((n, ci), len(RING))
                if n == "sw":
                    pass
                elif i >= len(RING):
                    m, cj, e = GROUPS[i - len(RING)]
                    e.wait(pe, m, cj)
                elif i == 0:
                    A.wait(pe, "tails")
                    V.wait(pe, "tails")
                    unit_read(pe, UNIT0[first["out"]] - 1)

            def tile(ci):
                c0, c = CHUNKS[ci]
                s_ = ci == SAMPLE
                B = SETS[SET[ci]]
                KH, KHT, KE, RA, RB, M, AT, VN = (B[n_] for n_ in ("KH", "KHT", "KE", "RA", "RB", "M", "AT", "VN"))

                def group(n, *needs):
                    free_bank(n, ci)
                    for e, m in needs:
                        e.wait(pe, m, ci)
                    return gbank(n, ci)

                def each(n, f, width, *needs, only=range(HEADS)):
                    b_ = group(n, *needs)
                    for i, hh in enumerate(only):
                        last = f(b_, i, hh)
                    T.op(last, n, ci)

                def prod4(n, L, R, *needs):
                    each(n, lambda b_, i, hh: mm(b_[0:c, i * c:(i + 1) * c], L[0:c, hh, 0:c], R[0:c, hh, 0:c]),
                         c, *needs)

                yield "k"
                each("k", lambda b_, i, hh: pe.transpose(b_[0:c, i * P:(i + 1) * P],
                                                         qkvT[:, HEADS + hh, c0:c0 + c], ident[:]), P)
                yield "v"
                each("v", lambda b_, i, hh: pe.transpose(b_[0:c, i * P:(i + 1) * P],
                                                         qkvT[:, 2 * HEADS + hh, c0:c0 + c], ident[:]), P)
                yield "gb"
                each("gb", lambda b_, i, hh: mm(b_[0:c, i * c:(i + 1) * c],
                                                tok[0:c, GD, ci, hh:hh + 1].to_broadcast([c, c]),
                                                (tri_s if s_ else tri)[0:c, 0:c]), c)
                yield "khT"
                each("khT", lambda b_, i, hh: pe.transpose(b_[:, i * c:(i + 1) * c], KH[0:c, hh, :],
                                                           ident[0:c, 0:c]), c, (V, "k"))
                yield "kk"
                each("kk", lambda b_, i, hh: mm(b_[0:c, i * c:(i + 1) * c], KHT[:, hh, 0:c], KHT[:, hh, 0:c]),
                     c, (A, "khT"))
                yield "kq"
                each("kq", lambda b_, i, hh: mm(b_[0:c, i * c:(i + 1) * c], KHT[:, hh, 0:c],
                                                qkvT[:, hh, c0:c0 + c]), c)
                yield "ldT"
                each("ldT", lambda b_, i, hh: pe.transpose(b_[0:c, i * c:(i + 1) * c], M[0][0:c, hh, 0:c],
                                                           ident[0:c, 0:c]), c, (V, "Ld"))
                yield "p2"
                prod4("p2", M[1], M[0], (A, "ldT"))
                yield "pt2"
                prod4("pt2", M[0], M[1])
                yield "t1"
                prod4("t1", M[2], M[4], (A, "p2"), (V, "t0"))
                if not s_:
                    yield "p4"
                    prod4("p4", M[3], M[2], (V, "pt2"))
                    yield "pt4"
                    prod4("pt4", M[2], M[3])
                    yield "t2"
                    prod4("t2", M[5], M[4], (A, "p4"), (V, "t1"))
                    yield "p8"
                    prod4("p8", M[6], M[5], (V, "pt4"))
                    yield "t3"
                    prod4("t3", M[2], M[4], (A, "p8"), (V, "t2"))
                solved = "t1" if s_ else "t3"
                if c == P:
                    yield "n"
                    prod4("n", M[4], M[7], (V, "t3"), (V, "Lo"))
                    yield "nt"
                    prod4("nt", M[7], M[4])
                    yield "n2"
                    prod4("n2", M[1], M[0], (V, "nt"), (A, "n"))
                    yield "nt2"
                    prod4("nt2", M[0], M[1])
                    yield "nt4"
                    prod4("nt4", M[3], M[5], (A, "n2"), (V, "nt2"))

                def solve(n, L, R, *needs):
                    for x, only in (("a", (0, 1)), ("b", (2, 3))):
                        yield n + x
                        each(n + x, lambda b_, i, hh: mm(b_[0:c, i * 256:(i + 1) * 256], L[0:c, hh, 0:c],
                                                         R[0:c, hh].rearrange("p x d -> p (x d)")),
                             0, *needs, only=only)

                yield from solve("r0", M[4], RA, (V, solved), (V, "RA"))
                R = RB
                if c == P:
                    yield from solve("r1", M[6], RB, (A, "nt4"), (A, "r0a"), (V, "r0b"))
                    yield from solve("r2", M[5], RA, (V, "r1b"))
                    yield from solve("r3", M[1], RB, (V, "r2b"))
                    R = RA
                yield "wT"
                each("wT", lambda b_, i, hh: pe.transpose(b_[:, i * c:(i + 1) * c], R[0:c, hh, 1, :],
                                                          ident[0:c, 0:c]), c,
                     *([(V, "r3b")] if c == P else [(A, "r0a"), (V, "r0b")]))
                if s_:
                    for hh in range(HEADS):
                        yield "sw", hh
                        if hh == 0:
                            b_ = group("sw", (A, "wT"))
                        pe.wait_ge(ss_in[hh], 16)
                        for q in range(NSEQ):
                            last = mm(b_[:, 64 * hh + 8 * q:64 * hh + 8 * q + 8], SS[hh][:, q, :],
                                      WQ[:, hh, q, :])
                        T.op(last, "swh", hh)
                    yield "ws"
                    each("ws", lambda b2, i, hh: pe.transpose(b2[0:c, i * P:(i + 1) * P],
                                                              M[2][:, 0, hh * TS:(hh + 1) * TS], ident[:]),
                         P, (V, "sw"))
                    yield "qs"
                    each("qs", lambda b2, i, hh: pe.transpose(b2[0:c, i * P:(i + 1) * P],
                                                              M[2][:, 1, hh * TS:(hh + 1) * TS], ident[:]), P)
                else:
                    if ci:
                        V.wait(pe, "su", ci - 1)
                    yield "ws"
                    each("ws", lambda b2, i, hh: mm(b2[0:c, i * P:(i + 1) * P], M[2][:, hh, 0:c], state[:, hh, :]),
                         P, (A, "wT"))
                    yield "qs"
                    each("qs", lambda b2, i, hh: mm(b2[0:c, i * P:(i + 1) * P], qkvT[:, hh, c0:c0 + c],
                                                    state[:, hh, :]), P)
                yield "o1"
                each("o1", lambda b2, i, hh: mm(b2[0:c, i * P:(i + 1) * P], AT[0:c, hh, 0:c], VN[0:c, hh, :]),
                     P, (V, "ws"), (V, "kq"))
                if not s_:
                    yield "su"
                    each("su", lambda b2, i, hh: mm(b2[:, i * P:(i + 1) * P], KE[0:c, hh, :], VN[0:c, hh, :]),
                         P, (V, "KE"))

                yield "on"
                each("on", lambda b2, i, hh: pe.transpose(b2[:, i * c:(i + 1) * c], ONB[ci % 2][0:c, hh, :],
                                                          ident[0:c, 0:c]), c, (V, "onb"))

            def ln_tile(ci):
                t = ci - LN
                if ci == ROOTS:
                    return
                for n in ("cs", "cn"):
                    yield n
                    G.wait(pe, "cconv", 2)
                    V.wait(pe, "cconv", 1)
                    V.wait(pe, "cconv", 3)
                    free_bank(n, ci)
                    for c in range(NG):
                        last = pe.transpose(gbank(n, ci)[0:TB, c * P:(c + 1) * P], cT[:, c, t * TB:(t + 1) * TB],
                                            ident[:])
                    T.op(last, n, ci)
                yield "ln"
                V.wait(pe, "cn", ci)
                free_bank("ln", ci)
                for c in range(NG):
                    last = pe.transpose(gbank("ln", ci)[:, c * TB:(c + 1) * TB], CN[:, t % 2, c * P:(c + 1) * P],
                                        ident[0:TB, 0:TB])
                T.op(last, "ln", ci)

            side_by_side(tile, ln_tile)
            T.counts["mixer", "last"] = T.n

            def sample_state(hh):
                V.wait(pe, f"ktm{hh}", SAMPLE)
                for i in range(2):
                    if hh >= 2:
                        V.wait(pe, f"su{hh - 2}{i}", SAMPLE)
                    b_ = gbank(f"su{hh}{i}", SAMPLE)
                    for q in range(4):
                        last = mm(b_[:, P * q:P * q + P], KTM[0:TS, P * (4 * i + q):P * (4 * i + q) + P],
                                  SETS[0]["VN"][0:TS, hh, :])
                    T.op(last, f"su{hh}{i}", SAMPLE)

            V.wait(pe, "on", SAMPLE - 1)
            A.wait(pe, "ln", LN + NTB - 1)
            sample_state(0)
            V.wait(pe, "mixlow", "last")
            for b in range(first["out"], first["query"]):
                linear(b)
                if b - first["out"] < HEADS - 1:
                    sample_state(b - first["out"] + 1)
            unit_read(pe, UNIT0[first["query"]] - 1)
            V.wait(pe, f"su{HEADS - 1}1", SAMPLE)
            pe.wait_ge(h_in[1], 96)
            for i in range(4):
                for j in range(4):
                    last = pe.transpose(bank[4 + i][:, j * P:(j + 1) * P], keysrow[:, 4 * i + j, :], ident[:])
            T.op(last, "keys")
            norm(2)
            V.wait(pe, "xlow", 2, NTB - 1, 1)

            def score(ct):
                unit_read(pe, UNIT0[first["query"]] + 2 * ct + 1)
                if ct >= 2:
                    A.wait(pe, "score", ct - 2)
                else:
                    A.wait(pe, "keys")
                for t in range(NTB):
                    last = mm(bank[4 + 2 * (ct % 2) + t // 4][0:TB, (t % 4) * P:(t % 4) * P + P],
                              qT[:, ct % 2, t * TB:(t + 1) * TB], keysT[:, ct, :])
                T.op(last, "score", ct)

            for b in range(first["query"], nb):
                linear(b)
                i = b - first["query"]
                score(2 * i)
                score(2 * i + 1)

            def scores_of(g, j, half):
                e = GE * g + j
                if half == 0:
                    pe.wait_ge(ut_low, e + 1)
                pe.wait_ge(gelu_done, 2 * e + (half + 1))
                for kt in range(KT):
                    for i, (pw, px) in enumerate(((0, 0), (0, 1), (1, 0))):
                        last = mm(bank[2 * j + half][:, 0:HALF], UT[:, j, pw, kt, :],
                                  xT[:, px, kt, half * HALF:(half + 1) * HALF],
                                  start=(kt == 0 and i == 0), stop=(kt == KT - 1 and i == 2))
                last.then_inc(s_mm, 1)

            def first_part(g, between=lambda n: None):
                for j in range(GE):
                    for half in range(2):
                        scores_of(g, j, half)
                        between(2 * j + half)

            grant(pe, s_mm, 2)
            unit_read(pe, UNIT0[nb] - 1)
            with pe.Fori(0, NG1 // 2, 1) as i:
                for k in range(2):
                    first_part(Grp(k, i))

            A.wait(pe, "score", 2 * PH - 1)
            for t in range(NTB):
                V.wait(pe, "gates")
                if t >= 2:
                    V.wait(pe, "pairT", t - 2)
                for i in range(3):
                    last = pe.transpose(bank[4 + t % 2][:, i * TB:(i + 1) * TB], pick[:, t, i, :], ident[0:TB, 0:TB])
                T.op(last, "pairT", t)

            def gates_of(i, n):
                group_ = i * (GB // 2) + (n + 1)
                pe.wait_ge(is_ready, group_)
                pe.wait_ge(gate_bank, group_)
                for k in range(4):
                    s_ = (n % ISG) * 4 + k
                    o_ = bank[4 + n % 4][:, k * NK:(k + 1) * NK]
                    for x in range(3):
                        last = mm(o_, is1[:, s_, :], is2[:, s_, x, :], start=(x == 0), stop=(x == 2))
                last.then_inc(gate_mm, 1)

            with pe.Fori(0, NGB // 2, 1) as i:
                for k in range(TURN2):
                    first_part(Grp(NG1 + k, i, TURN2),
                               between=lambda h: [gates_of(i, n) for n in gate_slots(k, h)])

            def second_part(q):
                VR = vbuf(q)
                pe.wait_ge(a_low, GE * q + GE)
                pe.wait_ge(v_low, 1 * q + 1)
                for u in range(2 * KT):
                    dt, half = u // 2, u % 2
                    if q.k < NGF:
                        bk = bank[4 + u % 4]
                        pe.wait_ge(y_add, 2 * KT * q + (u + 1))
                    else:
                        bk = bank[u % 8]
                        pe.wait_ge(y_add, 2 * KT * q + (u - 3))
                    for j in range(GE):
                        for i, (pw, pa) in enumerate(((0, 0), (0, 1), (1, 0))):
                            last = mm(bk[:, 0:HALF], VR[:, pw, j, dt * P:(dt + 1) * P],
                                      AR[:, par(q), pa, j, half * HALF:(half + 1) * HALF],
                                      start=(j == 0 and i == 0), stop=(j == GE - 1 and i == 2))
                    last.then_inc(y_mm, 1)

            grant(pe, y_mm, 2 * KT)
            first_part(Grp(NGA))
            with pe.Fori(0, NGF // 2 - 1, 1) as i:
                for k in range(2):
                    first_part(Grp(k + 1 + NGA, i))
                    second_part(Grp(k, i))
            first_part(Grp(NGRP - 1))
            second_part(Grp(NGF - 2))
            second_part(Grp(NGF - 1))
            pe.wait_ge(gelu_done, 2 * NK + 4)
            with pe.Fori(0, NGA // 2, 1) as i:
                for k in range(2):
                    second_part(Grp(NGF + k, i))

            V.wait(pe, "y_all")
            for t in range(NTB):
                for i in range(2):
                    if t >= 2:
                        V.wait(pe, "hf", t - 2, i)
                    for j in range(4):
                        last = pe.transpose(bank[2 * (t % 2) + i][0:TB, j * P:(j + 1) * P],
                                            yT[:, 4 * i + j, t * TB:(t + 1) * TB], ident[:])
                    T.op(last, "y", t, i)

        @block.scalar
        def _(act):
            def fn(out, in_, f, *name, **kw):
                return A.op(act.activation(out, in_, f, **kw), *name)

            def high(b):
                n = sum(x[2] for x in BLOCKS[b][2])
                act.wait_ge(raw_in[b % 4], 16 * raw_count[b])
                if b >= 2:
                    T.wait(act, "unit", UNIT0[b - 1] - 1)
                fn(WR[:, b % 2, 0, :, 0:n], RAW[:, b % 4, :, 0:n], ACT.Copy, "high", b)

            def norm(k):
                act.wait_ge(h_in[k - 1], 80 if k == 1 else 96)
                for t in range(NTB):
                    if k == 2:
                        V.wait(act, "h2", t)
                    fn(sq[:], h[:, t, :], ACT.Square, "ss", k, t, accum_out=ss[:, t:t + 1])
                    A.now(act)
                V.wait(act, "ms", k)
                fn(ss[:, 16:16 + NTB], ss[:, 8:8 + NTB], ACT.Sqrt, "rt", k)
                for t in range(NTB):
                    for i in range(2):
                        T.wait(act, "xT", k, t, i)
                        fn(xT[:, 0, 4 * i:4 * i + 4, t * TB:(t + 1) * TB],
                           bank[2 * (t % 2) + i][:, 0:4 * TB].rearrange("p (k n) -> p k n", k=4), ACT.Copy,
                           "xhigh", k, t, i)

            def seqs(ap):
                return ap.rearrange("p (q s) -> p q s", q=NSEQ)

            def evacuate(b):
                kind, i, _ = BLOCKS[b]
                for u in range(UNIT0[b], UNIT0[b + 1]):
                    n = u - UNIT0[b]
                    m, half = n // 2, n % 2
                    bk = bank[u % 4]
                    src = bk[:, 0:HALF]
                    cols_ = slice(half * HALF, (half + 1) * HALF)
                    T.wait(act, "unit", u)
                    if kind == "ab":
                        fn(abT[:, cols_], bk[0:2 * HEADS, 0:HALF], ACT.Copy, "unit", u)
                    elif kind == "z":
                        fn(zT[:, 2 * i + m, cols_], src, ACT.Silu, "unit", u)
                    elif kind == "query":
                        ct = 2 * i + m
                        if ct >= 2:
                            T.wait(act, "score", ct - 2)
                        fn(qT[:, ct % 2, cols_], src, ACT.Copy, "unit", u)
                    elif kind == "qkv":
                        c = 2 * i + m
                        e = c % 2
                        if half == 0:
                            if c >= 2:
                                V.wait(act, "qconv", c - 2)
                            fn(qext[:, e, QC - 1:QC - 1 + HALF], src, ACT.Copy, "unit", u)
                        else:
                            k = TP - HALF
                            x = seqs(qext[:, e, QEXT:])
                            fn(qext[:, e, QC - 1 + HALF:QEXT], bk[:, 0:k], ACT.Copy)
                            fn(x[:, :, QC - 1:], seqs(bk[:, k:HALF]), ACT.Copy)
                            if c == 0:
                                V.wait(act, "sqT")
                            fn(x[:, :, 0:QC - 1], seqs(sqT[:, c, :]), ACT.Copy)
                            fn(qtail[:, c, :], bk[:, k - (QC - 1):HALF], ACT.Copy, "unit", u)
                    elif kind == "glu":
                        if n == 0 and i == 1:
                            V.wait(act, "xn", 1, NTB - 1)
                        if n == 0 and i >= 2:
                            V.wait(act, "low", first["out"] - 2)
                        k = TP - HALF
                        if n == 0:
                            fn(gext[i][:, CC - 1:CC - 1 + HALF], src, ACT.Copy, "unit", u)
                        elif n == 1:
                            x = seqs(gext[i][:, CEXT:])
                            fn(gext[i][:, CC - 1 + HALF:CEXT], bk[:, 0:k], ACT.Copy)
                            fn(x[:, :, CC - 1:], seqs(bk[:, k:HALF]), ACT.Copy, "unit", u)
                            if i == 0:
                                V.wait(act, "scT")
                            fn(x[:, :, 0:CC - 1], seqs(scT[:, i, :]), ACT.Copy)
                        else:
                            if n == 2 and b > GLUS[0]:
                                V.wait(act, "glu", BLOCKS[max(g for g in GLUS if g < b)][1])
                            fn(gate[:, cols_], src, ACT.Sigmoid, "unit", u)

            def silu(c):
                V.wait(act, "qconv", c)
                fn(qkvT[:, c, :], qkvT[:, c, :], ACT.Silu, "silu", c)

            high(0)
            high(1)
            norm(1)
            G.wait(act, "zeros")
            def scalars(b):
                if b == SC_AB:
                    V.wait(act, "ab")
                    fn(tok[:, X2], tok[:, BETA], ACT.Exp, scale=-1.0)
                    fn(tok[:, X3], tok[:, GD], ACT.Abs)
                    A.now(act)
                    fn(tok[:, X3], tok[:, X3], ACT.Exp, scale=-1.0)
                    fn(dtb[:, HEADS:], dtb[:, HEADS:], ACT.Exp, "exps")
                elif b == SC_AB + 1:
                    V.wait(act, "exps")
                    fn(tok[:, X3], tok[:, X3], ACT.Ln, "ln")
                elif b == SC_CUM + 1:
                    V.wait(act, "cum")
                    fn(tok[:, EG], tok[:, GC], ACT.Exp)
                    fn(tok[:, EL], tok[:, EL], ACT.Exp)
                    fn(tok[:, EGL], tok[:, GL], ACT.Exp)
                    fn(gls[:], gls[:], ACT.Exp, "cum")
                if b >= SC_QK - 1 and b < SC_QK - 1 + HEADS:
                    for c in (2 * (b - SC_QK + 1), 2 * (b - SC_QK + 1) + 1):
                        if c >= 2:
                            T.wait(act, "qk2", c - 2)
                        A.now(act)
                        fn(sqb[c % 2][:], qkvT[:, c, :], ACT.Square, "qk2", c)

            done = 0
            for b in range(first["out"]):
                evacuate(b)
                while done < 2 * sum(x[0] == "qkv" for x in BLOCKS[:b]):
                    silu(done)
                    done += 1
                if b + 2 < nb:
                    high(b + 2)
                scalars(b)
            A.counts["qtail",] = A.n
            V.wait(act, "qk2")
            fn(tok[:, RQ], tok[:, RQ], ACT.Sqrt)
            fn(tok[:, RK], tok[:, RK], ACT.Sqrt, "rqk")
            T.wait(act, "tails")
            V.wait(act, "low", first["out"] - 1)
            for i in range(3):
                fn(RA2[0:QC - 1 + TS, 512 * i:512 * i + 512], bank[4 + i][0:QC - 1 + TS, :], ACT.Copy, "tails")

            def tile(ci):
                c0, c = CHUNKS[ci]
                s_ = ci == SAMPLE
                B = SETS[SET[ci]]
                KH, KHT, KE, RA, RB, M, AT, VN = (B[n_] for n_ in ("KH", "KHT", "KE", "RA", "RB", "M", "AT", "VN"))

                def take(n, dst, rows_=c, width=c, only=HEADS):
                    T.wait(act, n, ci)
                    fn(dst, gbank(n, ci)[0:rows_, 0:only * width].rearrange("p (h n) -> p h n", h=only), ACT.Copy,
                       n, ci)

                yield "gb"
                V.wait(act, "arg", ci)
                fn(M[6][0:c, :, 0:c], M[6][0:c, :, 0:c], ACT.Exp, scale=-1.0)
                fn(M[5][0:c, :, 0:c], M[5][0:c, :, 0:c], ACT.Exp, "exp", ci)
                yield "khT"
                take("khT", KHT[:, :, 0:c], P)
                yield "ldT"
                take("ldT", M[1][0:c, :, 0:c])
                yield "p2"
                take("p2", M[2][0:c, :, 0:c])
                if not s_:
                    yield "p4"
                    take("p4", M[5][0:c, :, 0:c])
                    yield "p8"
                    take("p8", M[2][0:c, :, 0:c])
                if c == P:
                    yield "n"
                    take("n", M[0][:])
                    yield "n2"
                    take("n2", M[3][:])
                    yield "nt4"
                    take("nt4", M[6][:])
                yield "r0a"
                T.wait(act, "r0a", ci)
                fn(RB[0:c, 0:2].rearrange("p h x d -> p h (x d)"),
                   gbank("r0a", ci)[0:c, :].rearrange("p (h n) -> p h n", h=2), ACT.Copy, "r0a", ci)
                if s_:
                    yield "wT"
                    T.wait(act, "wT", ci)
                    for hh in range(HEADS):
                        fn(WQ[:, hh, :, 0:STEPS], seqs(gbank("wT", ci)[:, hh * TS:(hh + 1) * TS]), ACT.Copy)
                        fn(WQ[:, hh, :, STEPS:], seqs(qkvT[:, hh, TP:]), ACT.Copy, "wT", ci)
                else:
                    yield "wT"
                    take("wT", M[2][:, :, 0:c], P)

                if ci >= 4:
                    yield "oss"
                    V.wait(act, "oss", ci)
                    fn(tok[0:c, OSS, ci, :], tok[0:c, OSS, ci, :], ACT.Sqrt, "oss", ci)

            def ln_tile(ci):
                t = ci - LN
                if ci == ROOTS:
                    yield "roots"
                    V.wait(act, "cvar", ROOTS - 1)
                    fn(lnst[:, :, 8:9], lnst[:, :, 8:9], ACT.Sqrt)
                    V.wait(act, "oss", 3)
                    fn(tok[:, OSS, 0:4, :], tok[:, OSS, 0:4, :], ACT.Sqrt, "roots")
                    return
                yield "ln"
                T.wait(act, "ln", ci)
                for c in range(NG):
                    fn(cT[:, c, t * TB:(t + 1) * TB], gbank("ln", ci)[:, c * TB:(c + 1) * TB], ACT.Silu, "ln", ci,
                       bias=cols[:, 56 + c:57 + c], scale=cols[:, 52 + c:53 + c])

            side_by_side(tile, ln_tile)
            V.wait(act, "delta")
            A.now(act)
            for k in range(KT):
                fn(xT[:, 0, k, :], mixer_out(k), ACT.Copy, "mixhigh", k)
            A.counts["mixer", "last"] = A.n

            for b in range(first["out"], first["query"]):
                high(b + 2)
            norm(2)
            act.wait_ge(h2_done, 16)
            for i in range(4):
                if i == 0:
                    T.wait(act, "keys")
                fn(keysT[:, 4 * i:4 * i + 4, :], bank[4 + i][:, :].rearrange("p (k n) -> p k n", k=4), ACT.Copy,
                   "keys")
            for b in range(first["query"], nb):
                evacuate(b)
                if b + 2 < nb:
                    high(b + 2)
                for ct in (2 * (b - first["query"]), 2 * (b - first["query"]) + 1):
                    T.wait(act, "score", ct)
                    fn(scores[:, 0:4, ct, :], bank[4 + 2 * (ct % 2)][0:TB, :].rearrange("p (t n) -> p t n", t=4),
                       ACT.Copy)
                    fn(scores[:, 4, ct, :], bank[5 + 2 * (ct % 2)][0:TB, 0:P], ACT.Copy, "score", ct)
            grant(act, gate_bank, 4)
            grant(act, gblk_out[0], 16)
            grant(act, gblk_out[1], 16)
            grant(act, gelu_done, 4)
            grant(act, act_out[0], 16)
            grant(act, act_out[1], 16)

            def split_u(g, j):
                if j == 0:
                    act.wait_ge(u_in[par(g)], 16 * (half_of(g) + 1))
                act.activation(UT[:, j, 0].rearrange("p k n -> p (k n)"), Uraw[:, par(g), j, :], ACT.Copy
                               ).then_inc(ut_high, 1)

            def first_part(g, final=False, store=False, between=lambda n: None):
                for j in range(GE):
                    e = GE * g + j
                    if store:
                        act.wait_ge(act_out[j], 16 * g + 16)
                    else:
                        act.wait_ge(a_mul, e + (1 - GE * NGA))
                    for half in range(2):
                        act.wait_ge(s_mm, 2 * e + (half + 3))
                        act.activation((actA if store else actv)[:, j, half * HALF:(half + 1) * HALF],
                                       bank[2 * j + half][:, 0:HALF], ACT.Gelu).then_inc(gelu_done, 1)
                        if half and not final:
                            split_u(g + 1, j)
                        between(2 * j + half)
                    if not store:
                        high_a(g + -NGA, j)

            def high_a(q, j):
                act.wait_ge(a_mul, GE * q + (j + 3))
                if j == 0:
                    act.wait_ge(y_mm, 2 * KT * q)
                act.activation(AR[:, par(q), 0, j, :], prod[:, j, :], ACT.Copy).then_inc(a_high, 1)

            def split_v(q):
                act.wait_ge(v_in[par(q)], 16 * (half_of(q) + 1))
                act.wait_ge(y_mm, 2 * KT * q + (0 if q.k >= NGF else 2 * KT))
                act.activation(vbuf(q)[:, 0], Vraw[:, par(q)], ACT.Copy).then_inc(v_high, 1)

            T.wait(act, "unit", UNIT0[nb] - 1)
            for j in range(GE):
                split_u(Grp(0), j)
            with act.Fori(0, NG1 // 2, 1) as i:
                for k in range(2):
                    first_part(Grp(k, i), store=True)
            V.wait(act, "top", NTB - 1)
            fn(pick[:, :, 2, :], pick[:, :, 2, :], ACT.Exp, "gexp")

            def gates_of(i, n):
                blk, q = n // (GB // 4), n % (GB // 4)
                act.wait_ge(gate_mm, i * (GB // 2) + (n + 1 + ISG))
                if q == 0:
                    act.wait_ge(gblk_out[blk], i * 16 + 16)
                act.activation(gblk[:, blk, :, 4 * q:4 * q + 4],
                               bank[4 + n % 4][:, :].rearrange("p (k n) -> p n k", k=4), ACT.Copy
                               ).then_inc(gate_bank, 1)

            with act.Fori(0, NGB // 2, 1) as i:
                for k in range(TURN2):
                    first_part(Grp(NG1 + k, i, TURN2), store=True,
                               between=lambda h: [gates_of(i, n) for n in gate_slots(k, h)])
            for i in range(2):
                act.wait_ge(gblk_out[i], 16 * (NGB // 2 + 1))
                act.wait_ge(act_out[i], 16 * (NGA + 1))
            first_part(Grp(NGA))
            with act.Fori(0, NGF // 2 - 1, 1) as i:
                for k in range(2):
                    split_v(Grp(k, i))
                    first_part(Grp(k + 1 + NGA, i))
            split_v(Grp(NGF - 2))
            first_part(Grp(NGRP - 1), True)
            split_v(Grp(NGF - 1))
            with act.Fori(0, NGA // 2, 1) as i:
                for k in range(2):
                    q = Grp(NGF + k, i)
                    for j in range(GE):
                        high_a(q, j)
                    split_v(q)

            for t in range(NTB):
                V.wait(act, "hf", t, 1)
                A.now(act)
                fn(yo[:, 0, :], hf[:, t, :], ACT.Square, "ss", 3, t, accum_out=fs[:, t:t + 1])
            V.wait(act, "ms", 3)
            fn(fs[:, 16:16 + NTB], fs[:, 8:8 + NTB], ACT.Sqrt, "rt", 3)

        @block.vector
        def _(dve):
            def op(ins, *name):
                return V.op(ins, *name)

            def chain(ins, *name):
                V.op(ins, *name)
                V.now(dve)

            tt = dve.tensor_tensor

            def low(b):
                n = sum(x[2] for x in BLOCKS[b][2])
                A.wait(dve, "high", b)
                op(tt(WR[:, b % 2, 1, :, 0:n], RAW[:, b % 4, :, 0:n], WR[:, b % 2, 0, :, 0:n].bitcast(F32),
                      ALU.subtract), "low", b)

            def rsqrt_in(src, dst, scale):
                chain(dve.tensor_scalar(dst, src, scale, EPS, ALU.mult, ALU.add))

            def norm(k):
                A.wait(dve, "ss", k, NTB - 1)
                op(dve.tensor_scalar(ss[:, 8:8 + NTB], ss[:, 0:NTB], 1.0 / D, EPS, ALU.mult, ALU.add), "ms", k)
                A.wait(dve, "rt", k)
                chain(dve.reciprocal(ss[:, 8:8 + NTB], ss[:, 16:16 + NTB]))
                dve.wait_ge(row_in[k - 1], 16)

                def lows(t):
                    for i in range(2):
                        A.wait(dve, "xhigh", k, t, i)
                        o_ = (slice(None), slice(4 * i, 4 * i + 4), slice(t * TB, (t + 1) * TB))
                        op(tt(xT[:, 1][o_], bank[2 * (t % 2) + i][:, 0:4 * TB].rearrange("p (k n) -> p k n", k=4),
                              xT[:, 0][o_].bitcast(F32), ALU.subtract), "xlow", k, t, i)

                for t in range(NTB):
                    if t >= 2:
                        T.wait(dve, "xT", k, t - 2, 1)
                    op(dve.scalar_tensor_tensor(xn[:, t % 2, :], h[:, t, :], ss[:, 8 + t:9 + t], wrow[:],
                                                ALU.mult, ALU.mult), "xn", k, t)
                    if t:
                        lows(t - 1)
                lows(NTB - 1)

            def scalars(b):
                if b == SC_AB:
                    G.wait(dve, "masks")
                    T.wait(dve, "ab")
                    for ci, (c0, c) in enumerate(CHUNKS):
                        op(tt(tok[0:c, GD, ci, :], bank[4][0:c, 8 * ci:8 * ci + 4], dtb[0:c, 0:HEADS], ALU.add))
                        op(dve.tensor_copy(tok[0:c, BETA, ci, :], bank[4][0:c, 8 * ci + 4:8 * ci + 8]), "ab")
                elif b == SC_AB + 1:
                    A.wait(dve, "exps")
                    op(dve.tensor_scalar(tok[:, X2], tok[:, X2], 1.0, None, ALU.add))
                    chain(dve.tensor_scalar(tok[:, X3], tok[:, X3], 1.0, None, ALU.add), "exps")
                    op(dve.reciprocal(tok[:, BETA], tok[:, X2]))
                elif b == SC_AB + 2:
                    A.wait(dve, "ln")
                    chain(dve.scalar_tensor_tensor(tok[:, GD], tok[:, GD], 0.0, tok[:, X3], ALU.max, ALU.add))
                    chain(dve.scalar_tensor_tensor(tok[:, GD], tok[:, GD], -1.0,
                                                   dtb[:, HEADS:].unsqueeze(1).to_broadcast([P, len(CHUNKS), HEADS]),
                                                   ALU.mult, ALU.mult), "g")
                    op(tt(gm[:], tok[0:TS, GD, SAMPLE, :].unsqueeze(1).to_broadcast([TS, NSEQ, HEADS]),
                          seq_of[:].unsqueeze(2).to_broadcast([TS, NSEQ, HEADS]), ALU.mult), "gm")
                elif b == SC_CUM:
                    T.wait(dve, "cum")
                    op(dve.tensor_copy(gls[:].rearrange("p b h -> p (b h)"), bank[6][:, 0:TS]))
                    for ci, (c0, c) in enumerate(CHUNKS):
                        n = c if ci == SAMPLE else P
                        op(dve.tensor_copy(tok[0:c, GC, ci, :], bank[5][0:c, 8 * ci:8 * ci + 4]))
                        op(dve.tensor_copy(tok[0:n, GL, ci, :], bank[5][0:n, 8 * ci + 4:8 * ci + 8]))
                    V.now(dve)
                    op(tt(tok[:, EL], tok[:, GL], tok[:, GC], ALU.subtract), "cum")

            def conformer_conv(c):
                if c == NG - 1:
                    T.wait(dve, "ab")
                for j in range(CC):
                    w = dwcols[:, NG * j + c:NG * j + c + 1]
                    V.now(dve)
                    for d, x in conv_parts(cT[:, c, 0:TP], cT[:, c, TP:], gext[c][:, 0:CEXT], gext[c][:, CEXT:], j):
                        if j == 0:
                            op(dve.tensor_scalar(d, x, w, cols[:, 48 + c:49 + c], ALU.mult, ALU.add))
                        else:
                            op(dve.scalar_tensor_tensor(d, x, w, d, ALU.mult, ALU.add))
                    V.counts["cconv", c] = V.n
                    yield

            T.wait(dve, "cols")
            op(dve.tensor_copy(cols[:], bank[4][:, 0:61]))
            op(dve.tensor_copy(dwcols[:], bank[4][:, 128:128 + CC * NG]))
            T.wait(dve, "sqT")
            op(dve.tensor_copy(sqT[:].rearrange("p c n -> p (c n)"), bank[5][:, 0:24 * NQ]), "sqT")
            T.wait(dve, "scT")
            for i in range(2):
                chain(dve.tensor_copy(scT[:, 2 * i:2 * i + 2, :].rearrange("p c n -> p (c n)"),
                                      bank[6 + i][:, 0:480]), "scT")
            low(0)
            low(1)
            norm(1)
            conv1 = conformer_conv(1)
            for b in range(first["out"]):
                kind, i, _ = BLOCKS[b]
                if kind == "qkv":
                    for c in (2 * i, 2 * i + 1):
                        e = c % 2
                        A.wait(dve, "unit", UNIT0[b] + 2 * (c % 2) + 1)
                        G.wait(dve, "zeros")
                        for j in range(QC):
                            w = cols[:, NQ * j + c:NQ * j + c + 1]
                            if j:
                                V.now(dve)
                            for d, x in conv_parts(qkvT[:, c, 0:TP], qkvT[:, c, TP:], qext[:, e, 0:QEXT],
                                                   qext[:, e, QEXT:], j):
                                if j == 0:
                                    op(dve.tensor_scalar(d, x, w, None, ALU.mult))
                                else:
                                    op(dve.scalar_tensor_tensor(d, x, w, d, ALU.mult, ALU.add))
                        V.counts["qconv", c] = V.n
                elif kind == "glu":
                    c = i
                    x = gext[c][:, CC - 1:CEXT]
                    xs = gext[c][:, CEXT:].rearrange("p (q s) -> p q s", q=NSEQ)
                    A.wait(dve, "unit", UNIT0[b] + 3)
                    op(tt(x, x, gate[:, 0:TP], ALU.mult))
                    chain(tt(xs[:, :, CC - 1:], xs[:, :, CC - 1:],
                             gate[:, TP:].rearrange("p (q s) -> p q s", q=NSEQ), ALU.mult), "glu", c)
                    op(dve.tensor_copy(ctail[:, c, 0:CC - 1], x[:, TP - (CC - 1):]))
                    op(dve.tensor_copy(ctail[:, c, CC - 1:].rearrange("p (q s) -> p q s", q=NSEQ),
                                       xs[:, :, CC - 1:]), "ctail")
                    if c == NG - 1:
                        op(dve.memset(gext[c][:, 0:CC - 1], 0.0))
                if b + 2 < nb:
                    low(b + 2)
                scalars(b)
                if b > GLUS[1]:
                    for _ in range(-(-CC // (first["out"] - GLUS[1] - 1))):
                        next(conv1, None)

            T.wait(dve, "qk2", 2 * HEADS - 1)
            for ci, (c0, c) in enumerate(CHUNKS):
                op(dve.tensor_scalar(tok[0:c, RQ, ci, :], bank[7][0:c, 8 * ci:8 * ci + 4], EPS, None, ALU.add))
                op(dve.tensor_scalar(tok[0:c, RK, ci, :], bank[7][0:c, 8 * ci + 4:8 * ci + 8], EPS, None, ALU.add),
                   "qk2")
            A.wait(dve, "rqk")
            op(dve.reciprocal(tok[:, RQ], tok[:, RQ]))
            chain(dve.reciprocal(tok[:, RK], tok[:, RK]))
            chain(dve.tensor_scalar(tok[:, RQ], tok[:, RQ], float(DH) ** -0.5, None, ALU.mult))
            A.wait(dve, "cum")
            op(tt(tok[:, EQ], tok[:, EG], tok[:, RQ], ALU.mult))
            chain(tt(tok[:, BEG], tok[:, EG], tok[:, BETA], ALU.mult))
            T.wait(dve, "tails")
            chain(dve.tensor_copy(RA3[:], bank[7][0:CC - 1 + TS, :]), "tails")

            def tile(ci):
                c0, c = CHUNKS[ci]
                s_ = ci == SAMPLE
                B = SETS[SET[ci]]
                KH, KHT, KE, RA, RB, M, AT, VN = (B[n_] for n_ in ("KH", "KHT", "KE", "RA", "RB", "M", "AT", "VN"))

                def src(n, width=c, heads=HEADS, rows_=c):
                    T.wait(dve, n, ci)
                    return gbank(n, ci)[0:rows_, 0:heads * width].rearrange("p (h n) -> p h n", h=heads)

                def mask(m):
                    return m[0:c, 0:c].unsqueeze(1).to_broadcast([c, HEADS, c])

                def sq_(m):
                    return m[0:c, :, 0:c]

                yield "k"
                chain(tt(KH[0:c], src("k", P), rows(RK, c, ci, P), ALU.mult), "k", ci)
                op(tt(KE[0:c], KH[0:c], rows(EL, c, ci, P), ALU.mult), "KE", ci)
                op(tt(RA[0:c, :, 1, :], KH[0:c], rows(BEG, c, ci, P), ALU.mult))
                yield "v"
                op(tt(RA[0:c, :, 0, :], src("v", P), rows(BETA, c, ci, P), ALU.mult), "v", ci)
                V.counts["RA", ci] = V.n
                yield "gb"
                chain(tt(sq_(M[7]), src("gb"), rows(GC, c, ci, c), ALU.subtract), "gb", ci)
                op(tt(sq_(M[6]), sq_(M[7]), mask(pos_s if s_ else pos), ALU.add))
                op(tt(sq_(M[5]), sq_(M[7]), mask(neg_s if s_ else neg), ALU.add), "arg", ci)
                yield "kk"
                A.wait(dve, "exp", ci)
                L = M[3] if c == P else M[0]
                chain(tt(sq_(L), src("kk"), sq_(M[6]), ALU.mult), "kk", ci)
                chain(tt(sq_(L), sq_(L), rows(BETA, c, ci, c), ALU.mult), "Ld", ci)
                if c == P:
                    chain(tt(sq_(M[0]), sq_(L), mask(diag16), ALU.mult), "Ld", ci)
                    op(tt(sq_(M[7]), sq_(L), sq_(M[0]), ALU.subtract), "Lo", ci)
                yield "kq"
                op(tt(AT[0:c, :, 0:c], src("kq"), sq_(M[5]), ALU.mult), "kq", ci)
                yield "ldT"
                A.wait(dve, "ldT", ci)
                chain(tt(sq_(M[4]), mask(ident), sq_(M[1]), ALU.subtract), "t0", ci)
                yield "pt2"
                op(dve.tensor_copy(sq_(M[3]), src("pt2")), "pt2", ci)

                yield "t1"
                chain(tt(sq_(M[4]), sq_(M[4]), src("t1"), ALU.add), "t1", ci)
                if not s_:
                    yield "pt4"
                    op(dve.tensor_copy(sq_(M[6]), src("pt4")), "pt4", ci)
                    yield "t2"
                    chain(tt(sq_(M[4]), sq_(M[4]), src("t2"), ALU.add), "t2", ci)
                    yield "t3"
                    chain(tt(sq_(M[4]), sq_(M[4]), src("t3"), ALU.add), "t3", ci)
                if c == P:
                    yield "nt"
                    op(dve.tensor_copy(sq_(M[1]), src("nt")), "nt", ci)
                    yield "nt2"
                    op(dve.tensor_copy(sq_(M[5]), src("nt2")), "nt2", ci)

                def two(t, i):
                    return t[0:c, 2 * i:2 * i + 2].rearrange("p h x d -> p h (x d)")

                yield "r0b"
                op(dve.tensor_copy(two(RB, 1), src("r0b", 256, 2)), "r0b", ci)
                R = RB
                if c == P:
                    A.wait(dve, "r0a", ci)
                    for n, x, y, f in (("r1", RB, RA, ALU.add), ("r2", RA, RB, ALU.add), ("r3", RB, RA, ALU.subtract)):
                        for i, ab in enumerate("ab"):
                            yield n + ab
                            if i == 0:
                                V.now(dve)
                            op(tt(two(y, i), two(x, i), src(n + ab, 256, 2), f), n + ab, ci)
                    R = RA
                if s_:
                    yield "sw", HEADS - 1
                    T.wait(dve, "swh", HEADS - 1)
                    sv = gbank("sw", ci)[:, 0:256].rearrange("p (g x) -> p g x", x=2 * STEPS)
                    for i in range(2):
                        op(dve.tensor_copy(M[2][:, i, :].rearrange("p (g x) -> p g x", x=STEPS),
                                           sv[:, :, STEPS * i:STEPS * (i + 1)]), "sw", ci)
                yield "ws"
                V.now(dve)
                if c != P:
                    A.wait(dve, "r0a", ci)
                chain(tt(VN[0:c], R[0:c, :, 0, :], src("ws", P), ALU.subtract), "ws", ci)
                O = ostore(ci)
                yield "qs"
                op(tt(O, src("qs", P), rows(EQ, c, ci, P), ALU.mult), "qs", ci)
                yield "o1"
                chain(tt(M[3][0:c], src("o1", P), rows(RQ, c, ci, P), ALU.mult), "o1", ci)
                chain(tt(O, O, M[3][0:c], ALU.add))
                chain(tt(M[3][0:c], O, O, ALU.mult))
                chain(dve.tensor_reduce(tok[0:c, OSS, ci, :], M[3][0:c], AX.X, ALU.add))
                op(dve.tensor_scalar(tok[0:c, OSS, ci, :], tok[0:c, OSS, ci, :], 1.0 / DH, EPS, ALU.mult, ALU.add),
                   "oss", ci)
                if not s_:
                    yield "su"
                    chain(tt(state[:], state[:], rows(EGL, P, ci, P), ALU.mult))
                    chain(tt(state[:], state[:], src("su", P, HEADS, P), ALU.add), "su", ci)
                yield "onb"
                if ci >= 2:
                    T.wait(dve, "on", ci - 2)
                if ci >= 4:
                    A.wait(dve, "oss", ci)
                    chain(dve.reciprocal(tok[0:c, OSS, ci, :], tok[0:c, OSS, ci, :]))
                op(tt(ONB[ci % 2][0:c], O, rows(OSS, c, ci, P), ALU.mult), "onb", ci)
                yield "on"
                op(dve.scalar_tensor_tensor(qkvT[:, 0:HEADS, c0:c0 + c], src("on", c, HEADS, P), cols[:, 60:61],
                                            zT[:, :, c0:c0 + c], ALU.mult, ALU.mult), "on", ci)

            def ln_tile(ci):
                t = ci - LN
                if ci == ROOTS:
                    yield "roots"
                    A.wait(dve, "roots")
                    op(dve.reciprocal(lnst[:, :, 9:10], lnst[:, :, 8:9]))
                    chain(dve.reciprocal(tok[:, OSS, 0:4, :], tok[:, OSS, 0:4, :]))
                    return
                yield "cs"
                T.wait(dve, "cs", ci)
                chain(dve.bn_stats(lnst[:, t, 0:6], gbank("cs", ci)[0:TB, :]), "cs", ci)
                chain(dve.bn_aggr(lnst[:, t, 6:8], lnst[:, t, 0:6]))
                op(dve.tensor_scalar(lnst[:, t, 8:9], lnst[:, t, 7:8], EPS, None, ALU.add), "cvar", ci)
                yield "cn"
                T.wait(dve, "cn", ci)
                if t >= 2:
                    T.wait(dve, "ln", ci - 2)
                op(dve.tensor_scalar(CN[:, t % 2, :], gbank("cn", ci)[0:TB, :], lnst[:, t, 6:7], lnst[:, t, 9:10],
                                     ALU.subtract, ALU.mult), "cn", ci)

            side_by_side(tile, ln_tile, conformer_conv(3))
            def sample_state(hh):
                if hh:
                    T.wait(dve, f"su{hh - 1}1", SAMPLE)
                op(tt(KTM[:].rearrange("p (b d) -> p b d", b=NSEQ),
                      SETS[0]["KE"][0:TS, hh, :].unsqueeze(1).to_broadcast([TS, NSEQ, DH]),
                      seq_of[:].unsqueeze(2).to_broadcast([TS, NSEQ, DH]), ALU.mult), f"ktm{hh}", SAMPLE)
                dve.wait_ge(ss_in[hh], 16)
                S_ = SS[hh]
                op(tt(S_[:], S_[:], gls[:, :, hh:hh + 1].to_broadcast([P, NSEQ, DH]), ALU.mult))
                yield
                V.now(dve)
                for i in range(2):
                    T.wait(dve, f"su{hh}{i}", SAMPLE)
                    op(tt(S_[:, 4 * i:4 * i + 4], S_[:, 4 * i:4 * i + 4],
                          gbank(f"su{hh}{i}", SAMPLE)[:, :].rearrange("p (q n) -> p q n", q=4), ALU.add),
                       f"su{hh}{i}", SAMPLE)
                V.counts["ss", hh] = V.n

            chain(dve.memset(lnst[0:1, 0, 0:1], 0.0), "delta")
            state_ = sample_state(0)
            next(state_)
            for k in range(KT):
                A.wait(dve, "mixhigh", k)
                op(tt(xT[:, 1, k, :], mixer_out(k), xT[:, 0, k, :].bitcast(F32), ALU.subtract), "mixlow", k)
            V.counts["mixlow", "last"] = V.n
            for _ in state_:
                pass
            state_ = sample_state(1)
            next(state_)
            V.counts["mixer", "last"] = V.n

            for b in range(first["out"], first["query"]):
                i = BLOCKS[b][1]
                if i == 0:
                    dve.wait_ge(h_in[1], 96)
                for t in range(NTB):
                    T.wait(dve, "unit", UNIT0[b] + t)
                    x = h[:, t, i * WB:(i + 1) * WB]
                    op(tt(x, x, bank[(UNIT0[b] + t) % 4][0:TB, 0:WB], ALU.add), "unit", UNIT0[b] + t)
                    V.counts["h2", t] = V.n
                for _ in state_:
                    pass
                if i < HEADS - 2:
                    state_ = sample_state(i + 2)
                    next(state_)
                low(b + 2)
            V.counts["h2", "last"] = V.n
            norm(2)
            for b in range(first["query"], nb - 2):
                low(b + 2)

            for t in range(NTB):
                A.wait(dve, "score", 2 * PH - 1)
                S_ = scores[:, t]

                def top(best_, besti_, v, n):
                    for c in range(n):
                        op(dve.max(best_(c)[:, 0:8], v(c)))
                    V.now(dve)
                    for c in range(n):
                        op(dve.max_index(besti_(c)[:, 0:8], best_(c)[:, 0:8], v(c)))
                    V.now(dve)
                    for c in range(n):
                        op(dve.match_replace(v(c), best_(c)[:, 0:8], v(c), LOWEST))
                    V.now(dve)
                    for c in range(n):
                        op(dve.max(best_(c)[:, 8:16], v(c)))
                    V.now(dve)
                    for c in range(n):
                        op(dve.max_index(besti_(c)[:, 8:16], best_(c)[:, 8:16], v(c)))
                    V.now(dve)

                top(lambda c: best[:, c], lambda c: besti[:, c], lambda c: S_[:, c, :], 2 * PH)
                op(dve.tensor_copy(bestf[:], besti[:]))
                bv = best[:].rearrange("p (h x) a -> p h x a", x=2)
                fv = bestf[:].rearrange("p (h x) a -> p h x a", x=2)
                sh = [TB, PH, TOPK, TOPK]
                chain(tt(cand[:], bv[:, :, 0, :].unsqueeze(3).to_broadcast(sh),
                         bv[:, :, 1, :].unsqueeze(2).to_broadcast(sh), ALU.add))
                top16 = pick[:, t, 2, :]
                top(lambda c: top16[:, 16 * c:16 * c + 16], lambda c: topi[:, 16 * c:16 * c + 16],
                    lambda c: cand[:, c].rearrange("p a b -> p (a b)"), PH)
                hr = top16.rearrange("p (h r) -> p h r", h=PH)
                chain(dve.tensor_copy(gmax[:], hr[:, :, 0]))
                op(tt(hr, hr, gmax[:].unsqueeze(2).to_broadcast([TB, PH, TOPK]), ALU.subtract), "top", t)
                op(dve.tensor_scalar(topa[:, 0], topi[:], 4, None, ALU.logical_shift_right))
                chain(dve.tensor_scalar(topa[:, 1], topi[:], 15, None, ALU.bitwise_and))
                chain(dve.tensor_copy(topf[:], topa[:]))
                for x in range(2):
                    chain(tt(eqa[:], iota[0:TB, 0:TOPK].unsqueeze(1).to_broadcast([TB, PAIRS, TOPK]),
                             topf[:, x, :].unsqueeze(2).to_broadcast([TB, PAIRS, TOPK]), ALU.is_equal))
                    chain(tt(sel[:].rearrange("p (h r) a -> p h r a", h=PH),
                             eqa[:].rearrange("p (h r) a -> p h r a", h=PH),
                             fv[:, :, x, :].unsqueeze(2).to_broadcast(sh), ALU.mult))
                    chain(dve.tensor_reduce(pick[:, t, x, :], sel[:], AX.X, ALU.add))
            A.wait(dve, "gexp")
            gv = pick[:, :, 2, :].rearrange("p t (h r) -> p t h r", h=PH)
            chain(dve.tensor_reduce(gsum[:], gv, AX.X, ALU.add))
            chain(dve.reciprocal(gsum[:], gsum[:]))
            op(tt(gv, gv, gsum[:].unsqueeze(3).to_broadcast([TB, NTB, PH, TOPK]), ALU.mult), "gates")
            for t in range(NTB):
                T.wait(dve, "pairT", t)
                chain(dve.tensor_copy(pairT[:, 0:3, t * TB:(t + 1) * TB],
                                      bank[4 + t % 2][:, 0:3 * TB].rearrange("p (x n) -> p x n", x=3)), "pairT", t)
            for x in (2, 3):
                chain(dve.tensor_copy(ghi[:], pairT[:, x, :]))
                chain(tt(pairT[:, x + 1, :], pairT[:, x, :], ghi[:], ALU.subtract))
                chain(dve.tensor_copy(pairT[:, x, :], ghi[:]))
            chain(dve.tensor_copy(iotab[:], iota[:]))

            grant(dve, gate_mm, ISG)
            with dve.Fori(0, NGB // 2, 1) as i:
                for n in range(GB // 2):
                    dve.wait_ge(gate_mm, i * (GB // 2) + (n + 1))
                    for k in range(4):
                        s1 = (n % ISG) * 4 + k
                        col = i * (2 * GB) + (4 * n + k)
                        dve.tensor_scalar(is1[:, s1, :], iotab[:], pairT[:, 0, bass.ds(col, 1)], None, ALU.is_equal)
                        for x in range(3):
                            last = dve.tensor_scalar(is2[:, s1, x, :], iotab[:], pairT[:, 1, bass.ds(col, 1)],
                                                     pairT[:, 2 + x, bass.ds(col, 1)], ALU.is_equal, ALU.mult)
                    last.then_inc(is_ready, 1)

            def gated(q, j, src):
                if j == 0:
                    dve.wait_ge(g_in[par(q)], 16 * (half_of(q) + 1))
                tt(prod[:, j, :].rearrange("p (b n) -> p b n", b=NGB), src.rearrange("p (b n) -> p b n", b=NGB),
                   Gt[:, par(q), :, j * GB:(j + 1) * GB], ALU.mult).then_inc(a_mul, 1)

            def low_a(q, j):
                dve.wait_ge(a_high, GE * q + (j + 1))
                tt(AR[:, par(q), 1, j, :], prod[:, j, :], AR[:, par(q), 0, j, :].bitcast(F32),
                   ALU.subtract).then_inc(a_low, 1)

            def first_part(q):
                for j in range(GE):
                    dve.wait_ge(gelu_done, 2 * (GE * (q + NGA) + j) + 6)
                    gated(q, j, actv[:, j, :])
                    low_a(q, j)

            def stored_part(q):
                dve.wait_ge(act_in[par(q)], 16 * (half_of(q) + (1 - NGF // 2)))
                for j in range(GE):
                    gated(q, j, actC[:, par(q), j, :])
                for j in range(GE):
                    low_a(q, j)

            def sums(q):
                for u in range(2 * KT):
                    dt, half = u // 2, u % 2
                    y = yT[:, dt, half * HALF:(half + 1) * HALF]
                    dve.wait_ge(y_mm, 2 * KT * q + (2 * KT + u + 1))
                    tt(y, y, bank[4 + u % 4 if q.k < NGF else u % 8][:, 0:HALF], ALU.add).then_inc(y_add, 1)

            grant(dve, a_mul, 2)
            grant(dve, y_add, 4)
            dve.wait_ge(gblk_out[0], 16 * (NGB // 2 + 1))
            dve.wait_ge(gblk_out[1], 16 * (NGB // 2 + 1))
            chain(dve.memset(yT[:], 0.0))
            first_part(Grp(0))
            with dve.Fori(0, NGF // 2 - 1, 1) as i:
                for k in range(2):
                    first_part(Grp(k + 1, i))
                    sums(Grp(k, i))
            first_part(Grp(NGF - 1))
            sums(Grp(NGF - 2))
            stored_part(Grp(NGF))
            sums(Grp(NGF - 1))
            with dve.Fori(0, NGA // 2 - 1, 1) as i:
                for k in range(2):
                    stored_part(Grp(NGF + 1 + k, i))
                    sums(Grp(NGF + k, i))
            stored_part(Grp(NGRP - 1))
            sums(Grp(NGRP - 2))
            sums(Grp(NGRP - 1))

            dve.wait_ge(y_add, 2 * KT * NGRP + 4)
            chain(dve.memset(fs[:, 23:24], 0.0), "y_all")

            dve.wait_ge(hf_in, 16)
            for t in range(NTB):
                for i in range(2):
                    T.wait(dve, "y", t, i)
                    x = hf[:, t, 512 * i:512 * i + 512]
                    op(tt(x, x, bank[2 * (t % 2) + i][0:TB, :], ALU.add), "hf", t, i)
            A.wait(dve, "ss", 3, NTB - 1)
            op(dve.tensor_scalar(fs[:, 8:8 + NTB], fs[:, 0:NTB], 1.0 / D, EPS, ALU.mult, ALU.add), "ms", 3)
            A.wait(dve, "rt", 3)
            chain(dve.reciprocal(fs[:, 8:8 + NTB], fs[:, 16:16 + NTB]))
            dve.wait_ge(row_in[2], 16)
            for t in range(NTB):
                if t >= 2:
                    dve.wait_ge(y_out[t % 2], 16 * (t // 2))
                op(dve.scalar_tensor_tensor(yo[:, t % 2, :], hf[:, t, :], fs[:, 8 + t:9 + t], wrow[:],
                                            ALU.mult, ALU.mult), "yo", t)


INPUTS = ["x_prompt", "x_sample", "state_gdn", "state_qkv_conv", "state_conf_conv", "meta_tokens", "norm_mix_w",
          "w_in", "conv_qkv_w", "a_log", "dt_bias", "gdn_norm_w", "conf_dw_w", "conf_dw_b", "conf_ln_w",
          "conf_ln_b", "w_out", "norm_ffn_w", "w_query", "sub_keys", "expert_u", "expert_v", "final_norm_w"]
OUTPUTS = [(1, SEQ, D), (NSEQ, STEPS, D), (1, 1, HEADS, DH, DH), (1, 1, QC - 1, QKV), (1, 1, CC - 1, CW),
           (1, NSEQ, HEADS, DH, DH), (1, NSEQ, QC - 1, QKV), (1, NSEQ, CC - 1, CW)]


def kernel(**inputs):
    from concourse import bacc
    from concourse.bass_utils import run_bass_kernel_spmd

    counts = {}
    for _ in range(2):
        nc = bacc.Bacc("TRN2", target_bir_lowering=False, num_devices=1)
        arrays, ins = {}, []
        for name in INPUTS:
            a = np.asarray(inputs[name])
            if name == "expert_u":
                a = a.reshape(NK, NK, KT, P).transpose(1, 3, 2, 0)
            a = np.ascontiguousarray(a)
            arrays[f"in_{name}"] = a
            ins.append(nc.dram_tensor(f"in_{name}", a.shape, F32, kind="ExternalInput").ap())
        outs = [nc.dram_tensor(f"out_{i}", shape, F32, kind="ExternalOutput").ap()
                for i, shape in enumerate(OUTPUTS)]
        build(nc, ins, outs, counts)
    r = run_bass_kernel_spmd(nc, [arrays], core_ids=[0])
    return tuple(r.results[0][f"out_{i}"] for i in range(len(OUTPUTS)))
```
